# Optimizing a Trainium2 kernel written in Bass

```python
import jax, jax.numpy as jnp
from jax import lax
import numpy as np

D_MODEL = 1024
BATCH = 1
SEQ = 512
DEPTH = 1

CTX_LEN = 256
GRID_W = 64
D_F = D_MODEL // 2
N_FG = 4
FG = D_F // N_FG
D_M = D_MODEL // 2
N_H = 4
DH = D_M // N_H
CHUNK = 64
CONV_K = 3
N_GATE_KINDS = 4
FORGET_BIAS_LO = 3.0
FORGET_BIAS_HI = 6.0
N_BRANCH = 2
N_EXPERTS = 16
CAP_FACTOR = 2
D_FF_E = D_MODEL
EPS = 1e-6
OFF_F = 0
OFF_QK = OFF_F + D_F
OFF_V = OFF_QK + 2 * D_M
OFF_O = OFF_V + D_M
OFF_G = OFF_O + D_M
OFF_BR = OFF_G + N_GATE_KINDS * N_H
IN_COLS = OFF_BR + N_BRANCH * D_MODEL


def rmsnorm(x, g):
    xf = x.astype(jnp.float32)
    y = xf * lax.rsqrt(jnp.mean(xf * xf, axis=-1, keepdims=True) + EPS)
    return (y * g.astype(jnp.float32)).astype(x.dtype)

def modulate(h, shift, scale):
    return h * (1 + scale) + shift

def grid_conv(u, w, rows):
    b, l, ch = u.shape
    ug = u.reshape(b, rows, l // rows, ch)
    out = lax.conv_general_dilated(ug, w[:, :, None, :].astype(u.dtype), (1, 1), 'SAME',
                                   dimension_numbers=('NHWC', 'HWIO', 'NHWC'),
                                   feature_group_count=ch)
    return out.reshape(b, l, ch)

def mlstm_inputs(p, rows, w_conv, b_gates):
    b, l, _ = p.shape
    qk = jax.nn.silu(grid_conv(p[..., OFF_QK:OFF_V], w_conv, rows))
    to_heads = lambda a: a.reshape(b, l, N_H, DH).transpose(0, 2, 1, 3).astype(jnp.float32)
    q = to_heads(qk[..., :D_M])
    k = to_heads(qk[..., D_M:]) * (DH ** -0.5)
    v = to_heads(p[..., OFF_V:OFF_O])
    g = (p[..., OFF_G:OFF_BR].astype(jnp.float32).reshape(b, l, N_GATE_KINDS, N_H).transpose(2, 0, 3, 1)
         + b_gates.astype(jnp.float32)[:, None, :, None])
    return q, k, v, g

def zero_state(b):
    return (jnp.zeros((b, N_H, DH, DH), jnp.float32), jnp.zeros((b, N_H, DH), jnp.float32),
            jnp.zeros((b, N_H), jnp.float32))

def mlstm_scan(q, k, v, ig, fl, state):
    b, h, l, dh = q.shape
    nc = l // CHUNK

    def chunks(a):
        return jnp.moveaxis(a.reshape((b, h, nc, CHUNK) + a.shape[3:]), 2, 0)

    tril = jnp.tril(jnp.ones((CHUNK, CHUNK), dtype=bool))

    def step(carry, inp):
        c0, n0, m0 = carry
        qc, kc, vc, ic, fc = inp
        cum = jnp.cumsum(fc, axis=-1)
        logw = jnp.where(tril, cum[..., :, None] - cum[..., None, :] + ic[..., None, :], -jnp.inf)
        inter = cum + m0[..., None]
        m = jnp.maximum(inter, logw.max(-1))
        s = jnp.einsum('bhjd,bhsd->bhjs', qc, kc) * jnp.exp(logw - m[..., None])
        dec = jnp.exp(inter - m)
        num = jnp.einsum('bhjs,bhsd->bhjd', s, vc) + dec[..., None] * jnp.einsum('bhjk,bhkv->bhjv', qc, c0)
        den = s.sum(-1) + dec * jnp.einsum('bhjk,bhk->bhj', qc, n0)
        hc = num / jnp.maximum(jnp.abs(den), jnp.exp(-m))[..., None]
        tot = cum[..., -1]
        a = tot[..., None] - cum + ic
        m_new = jnp.maximum(tot + m0, a.max(-1))
        wa = jnp.exp(a - m_new[..., None])
        dn = jnp.exp(tot + m0 - m_new)
        c_new = dn[..., None, None] * c0 + jnp.einsum('bhs,bhsk,bhsv->bhkv', wa, kc, vc)
        n_new = dn[..., None] * n0 + jnp.einsum('bhs,bhsk->bhk', wa, kc)
        return (c_new, n_new, m_new), hc

    final, hs = lax.scan(step, state, (chunks(q), chunks(k), chunks(v), chunks(ig), chunks(fl)))
    return jnp.moveaxis(hs, 0, 2).reshape(b, h, l, dh), final

def bidir_mlstm(q, k, v, g, init):
    flip = lambda a: jnp.flip(a, axis=2)
    h_f, s_f = mlstm_scan(q, k, v, g[0], jax.nn.log_sigmoid(g[1]), init[0])
    h_b, s_b = mlstm_scan(flip(q), flip(k), flip(v), flip(g[2]), flip(jax.nn.log_sigmoid(g[3])), init[1])
    return h_f + flip(h_b), (s_f, s_b)

def branch_merge(p, h_m, w_fourier, w_mlstm, w_out):
    b, l, _ = p.shape
    u = p[..., OFF_F:OFF_QK].astype(jnp.float32).reshape(b, l, N_FG, FG)
    fu = jnp.fft.fft2(u, axes=(1, 3), norm='ortho').real.astype(p.dtype).reshape(b, l, D_F)
    y_f = fu @ w_fourier
    hm = h_m.transpose(0, 2, 1, 3).reshape(b, l, D_M).astype(p.dtype)
    y_m = (jax.nn.sigmoid(p[..., OFF_O:OFF_G]) * hm) @ w_mlstm
    gates = jax.nn.sigmoid(p[..., OFF_BR:])
    merged = gates[..., :D_MODEL] * y_f + gates[..., D_MODEL:] * y_m
    return merged @ w_out

def expert_choice(h, w_router, w_gate, w_up, w_down):
    b, l, _ = h.shape
    cap = CAP_FACTOR * l // N_EXPERTS
    aff = jax.nn.softmax(jnp.einsum('bld,de->ble', h, w_router).astype(jnp.float32), axis=-1)
    vals, idx = lax.top_k(jnp.swapaxes(aff, 1, 2), cap)
    bidx = jnp.arange(b)[:, None, None]
    xs = h[bidx, idx]
    hid = jax.nn.silu(jnp.einsum('becd,edf->becf', xs, w_gate)) * jnp.einsum('becd,edf->becf', xs, w_up)
    y = jnp.einsum('becf,efd->becd', hid, w_down) * vals[..., None].astype(h.dtype)
    return jnp.zeros_like(h).at[bidx, idx].add(y)

def first_inputs(seed: int = 0) -> dict:
    key = jax.random.key(seed)
    ks = jax.random.split(key, 20)
    nrm = jax.random.normal
    forget = jnp.linspace(FORGET_BIAS_LO, FORGET_BIAS_HI, N_H)
    zeros_h = jnp.zeros((N_H,))
    gate_base = jnp.stack([zeros_h, forget, zeros_h, forget])
    return {
        'x': nrm(ks[0], (BATCH, SEQ, D_MODEL), jnp.float32),
        'c': nrm(ks[1], (BATCH, D_MODEL), jnp.float32),
        'ctx': nrm(ks[2], (BATCH, CTX_LEN, D_MODEL), jnp.float32),
        'c_ctx': nrm(ks[3], (D_MODEL,), jnp.float32),
        'w_ada': nrm(ks[4], (DEPTH, D_MODEL, 6 * D_MODEL), jnp.float32) * (0.5 * D_MODEL ** -0.5),
        'b_ada': nrm(ks[5], (DEPTH, 6 * D_MODEL), jnp.float32) * 0.02,
        'g_norm1': 1.0 + 0.02 * nrm(ks[6], (DEPTH, D_MODEL), jnp.float32),
        'w_in': nrm(ks[7], (DEPTH, D_MODEL, IN_COLS), jnp.float32) * D_MODEL ** -0.5,
        'b_gates': gate_base[None] + 0.1 * nrm(ks[8], (DEPTH, N_GATE_KINDS, N_H), jnp.float32),
        'w_conv': nrm(ks[9], (DEPTH, CONV_K, CONV_K, 2 * D_M), jnp.float32) * (1.0 / CONV_K),
        'w_fourier': nrm(ks[10], (DEPTH, D_F, D_MODEL), jnp.float32) * D_F ** -0.5,
        'w_mlstm': nrm(ks[11], (DEPTH, D_M, D_MODEL), jnp.float32) * D_M ** -0.5,
        'w_out': nrm(ks[12], (DEPTH, D_MODEL, D_MODEL), jnp.float32) * D_MODEL ** -0.5,
        'g_norm2': 1.0 + 0.02 * nrm(ks[13], (DEPTH, D_MODEL), jnp.float32),
        'w_router': nrm(ks[14], (DEPTH, D_MODEL, N_EXPERTS), jnp.float32) * D_MODEL ** -0.5,
        'w_gate_e': nrm(ks[15], (DEPTH, N_EXPERTS, D_MODEL, D_FF_E), jnp.float32) * D_MODEL ** -0.5,
        'w_up_e': nrm(ks[16], (DEPTH, N_EXPERTS, D_MODEL, D_FF_E), jnp.float32) * D_MODEL ** -0.5,
        'w_down_e': nrm(ks[17], (DEPTH, N_EXPERTS, D_FF_E, D_MODEL), jnp.float32) * D_FF_E ** -0.5,
        'g_final': 1.0 + 0.02 * nrm(ks[18], (D_MODEL,), jnp.float32),
    }

def first_block(x, c, ctx, c_ctx, w_ada, b_ada, g_norm1, w_in, b_gates, w_conv, w_fourier, w_mlstm,
              w_out, g_norm2, w_router, w_gate_e, w_up_e, w_down_e, g_final):
    b, seq, _ = x.shape
    rows = seq // GRID_W
    for l in range(DEPTH):
        last = l == DEPTH - 1
        mx = (jax.nn.silu(c) @ w_ada[l] + b_ada[l])[:, None, :]
        sh1, sc1, ga1, sh2, sc2, ga2 = jnp.split(mx, 6, axis=-1)
        mc = jax.nn.silu(c_ctx) @ w_ada[l] + b_ada[l]
        csh1, csc1, cga1, csh2, csc2, cga2 = jnp.split(mc, 6, axis=-1)
        pc = modulate(rmsnorm(ctx, g_norm1[l]), csh1, csc1) @ w_in[l]
        qc, kc, vc, gc = mlstm_inputs(pc, 1, w_conv[l], b_gates[l])
        h_mc, ctx_states = bidir_mlstm(qc, kc, vc, gc, (zero_state(b), zero_state(b)))
        px = modulate(rmsnorm(x, g_norm1[l]), sh1, sc1) @ w_in[l]
        qx, kx, vx, gx = mlstm_inputs(px, rows, w_conv[l], b_gates[l])
        h_mx, _ = bidir_mlstm(qx, kx, vx, gx, ctx_states)
        x = x + ga1 * branch_merge(px, h_mx, w_fourier[l], w_mlstm[l], w_out[l])
        hx2 = modulate(rmsnorm(x, g_norm2[l]), sh2, sc2)
        x = x + ga2 * expert_choice(hx2, w_router[l], w_gate_e[l], w_up_e[l], w_down_e[l])
        if not last:
            ctx = ctx + cga1 * branch_merge(pc, h_mc, w_fourier[l], w_mlstm[l], w_out[l])
            hc2 = modulate(rmsnorm(ctx, g_norm2[l]), csh2, csc2)
            ctx = ctx + cga2 * expert_choice(hc2, w_router[l], w_gate_e[l], w_up_e[l], w_down_e[l])
    return rmsnorm(x, g_final)


MEM_LEN = 256
CONV_DIM = 512
CONV_WIDTH = 31
FOX_HEADS = 8
FOX_HEAD_DIM = 64
FOX_DIM = FOX_HEADS * FOX_HEAD_DIM
Q_BLOCK = 128
XA_HEADS = 4
XA_HEAD_DIM = 128
XA_DIM = XA_HEADS * XA_HEAD_DIM
N_GROUPS = 4
EXPERTS_PER_GROUP = 4
N_EXPERTS_2 = N_GROUPS * EXPERTS_PER_GROUP
TOP_K = 2
EXPERT_FF = 256
SPLITS = (2 * CONV_DIM, FOX_DIM, FOX_DIM, FOX_DIM, FOX_HEADS, D_MODEL, D_MODEL)
IN_COLS_2 = sum(SPLITS)


def rmsnorm_2(x, g):
    xf = x.astype(jnp.float32)
    y = xf * lax.rsqrt(jnp.mean(xf * xf, axis=-1, keepdims=True) + EPS)
    return (y * g.astype(jnp.float32)).astype(x.dtype)

def layernorm(x, g, b):
    xf = x.astype(jnp.float32)
    mu = jnp.mean(xf, axis=-1, keepdims=True)
    var = jnp.mean(jnp.square(xf - mu), axis=-1, keepdims=True)
    y = (xf - mu) * lax.rsqrt(var + EPS)
    return (y * g.astype(jnp.float32) + b.astype(jnp.float32)).astype(x.dtype)

def conformer_conv(u_glu, dw_w, dw_b, ln_g, ln_b, pw_w):
    a, gate = jnp.split(u_glu, 2, axis=-1)
    u = a * jax.nn.sigmoid(gate)
    u = lax.conv_general_dilated(
        u, dw_w[:, None, :].astype(u.dtype), window_strides=(1,),
        padding=[(CONV_WIDTH - 1, 0)],
        dimension_numbers=("NWC", "WIO", "NWC"),
        feature_group_count=CONV_DIM) + dw_b
    u = jax.nn.silu(layernorm(u, ln_g, ln_b))
    return u @ pw_w

def fox_attention(q, k, v, logf):
    B, T, H, dh = q.shape
    nb = T // Q_BLOCK
    scale = dh ** -0.5
    c = jnp.cumsum(logf, axis=1).transpose(0, 2, 1)
    qh = q.transpose(0, 2, 1, 3)
    kh = k.transpose(0, 2, 1, 3)
    vh = v.transpose(0, 2, 1, 3)
    qb = qh.reshape(B, H, nb, Q_BLOCK, dh).transpose(2, 0, 1, 3, 4)
    cb = c.reshape(B, H, nb, Q_BLOCK).transpose(2, 0, 1, 3)
    kpos = jnp.arange(T)

    def block(args):
        q_i, c_i, i = args
        s = jnp.einsum("bhqd,bhkd->bhqk", q_i, kh).astype(jnp.float32) * scale
        s = s + c_i[..., :, None] - c[:, :, None, :]
        qpos = i * Q_BLOCK + jnp.arange(Q_BLOCK)
        s = jnp.where(kpos[None, :] <= qpos[:, None], s, -jnp.inf)
        p = jax.nn.softmax(s, axis=-1)
        return jnp.einsum("bhqk,bhkd->bhqd", p.astype(vh.dtype), vh)

    o = lax.map(block, (qb, cb, jnp.arange(nb)))
    return o.transpose(1, 0, 3, 2, 4).reshape(B, T, H * dh)

def cross_attention(h, m, wq, wk, wv, wo):
    B, T, _ = h.shape
    M = m.shape[1]
    q = (h @ wq).reshape(B, T, XA_HEADS, XA_HEAD_DIM)
    k = (m @ wk).reshape(B, M, XA_HEADS, XA_HEAD_DIM)
    v = (m @ wv).reshape(B, M, XA_HEADS, XA_HEAD_DIM)
    s = jnp.einsum("bthd,bmhd->bhtm", q, k).astype(jnp.float32) * XA_HEAD_DIM ** -0.5
    p = jax.nn.softmax(s, axis=-1)
    o = jnp.einsum("bhtm,bmhd->bthd", p.astype(v.dtype), v).reshape(B, T, XA_DIM)
    return o @ wo

def hierarchical_moe(h, wg, bg, we, be, w_gate, w_up, w_down):
    B, T, D = h.shape
    hf = h.reshape(B * T, D)
    g_logits = (hf @ wg).astype(jnp.float32) + bg.astype(jnp.float32)
    p_group = jax.nn.softmax(g_logits, axis=-1)
    g_star = jnp.argmax(p_group, axis=-1)
    p_gsel = jnp.take_along_axis(p_group, g_star[:, None], axis=-1)[:, 0]
    e_logits = ((hf @ we).astype(jnp.float32) + be.astype(jnp.float32)).reshape(-1, N_GROUPS, EXPERTS_PER_GROUP)
    e_sel = jnp.take_along_axis(e_logits, g_star[:, None, None], axis=1)[:, 0]
    p_exp = jax.nn.softmax(e_sel, axis=-1)
    top_v, top_i = lax.top_k(p_exp, TOP_K)
    top_v = top_v / jnp.sum(top_v, axis=-1, keepdims=True)
    weights = p_gsel[:, None] * top_v
    expert_idx = g_star[:, None] * EXPERTS_PER_GROUP + top_i
    combine = jnp.sum(jax.nn.one_hot(expert_idx, N_EXPERTS_2, dtype=jnp.float32) * weights[..., None], axis=1)
    a = jnp.einsum("nd,edf->nef", hf, w_gate)
    b = jnp.einsum("nd,edf->nef", hf, w_up)
    u = jax.nn.silu(a) * b * combine.astype(hf.dtype)[..., None]
    y = jnp.einsum("nef,efd->nd", u, w_down)
    return y.reshape(B, T, D)

def second_inputs(seed: int = 0) -> dict:
    key = jax.random.key(seed)
    ks = jax.random.split(key, 32)
    f32 = jnp.float32

    def nrm(k, shape, fan_in):
        return jax.random.normal(k, shape, f32) * (fan_in ** -0.5)

    def gain(k, shape):
        return 1.0 + 0.1 * jax.random.normal(k, shape, f32)

    def small(k, shape, s=0.01):
        return s * jax.random.normal(k, shape, f32)

    L = DEPTH
    return {
        "x": jax.random.normal(ks[0], (BATCH, SEQ, D_MODEL), f32),
        "mem": jax.random.normal(ks[1], (BATCH, MEM_LEN, D_MODEL), f32),
        "norm_mix_g": gain(ks[2], (L, D_MODEL)),
        "w_in": nrm(ks[3], (L, D_MODEL, IN_COLS_2), D_MODEL),
        "fox_bf": jax.random.uniform(ks[4], (L, FOX_HEADS), f32, 1.0, 4.0),
        "conv_dw_w": nrm(ks[5], (L, CONV_WIDTH, CONV_DIM), CONV_WIDTH),
        "conv_dw_b": small(ks[6], (L, CONV_DIM)),
        "conv_ln_g": gain(ks[7], (L, CONV_DIM)),
        "conv_ln_b": small(ks[8], (L, CONV_DIM)),
        "conv_pw_w": nrm(ks[9], (L, CONV_DIM, D_MODEL), CONV_DIM),
        "attn_branch_w": nrm(ks[10], (L, FOX_DIM, D_MODEL), FOX_DIM),
        "w_out": nrm(ks[11], (L, D_MODEL, D_MODEL), D_MODEL),
        "norm_xa_g": gain(ks[12], (L, D_MODEL)),
        "norm_mem_g": gain(ks[13], (L, D_MODEL)),
        "xa_wq": nrm(ks[14], (L, D_MODEL, XA_DIM), D_MODEL),
        "xa_wk": nrm(ks[15], (L, D_MODEL, XA_DIM), D_MODEL),
        "xa_wv": nrm(ks[16], (L, D_MODEL, XA_DIM), D_MODEL),
        "xa_wo": nrm(ks[17], (L, XA_DIM, D_MODEL), XA_DIM),
        "norm_moe_g": gain(ks[18], (L, D_MODEL)),
        "router_group_w": nrm(ks[19], (L, D_MODEL, N_GROUPS), D_MODEL),
        "router_group_b": small(ks[20], (L, N_GROUPS)),
        "router_expert_w": nrm(ks[21], (L, D_MODEL, N_EXPERTS_2), D_MODEL),
        "router_expert_b": small(ks[22], (L, N_EXPERTS_2)),
        "expert_w_gate": nrm(ks[23], (L, N_EXPERTS_2, D_MODEL, EXPERT_FF), D_MODEL),
        "expert_w_up": nrm(ks[24], (L, N_EXPERTS_2, D_MODEL, EXPERT_FF), D_MODEL),
        "expert_w_down": nrm(ks[25], (L, N_EXPERTS_2, EXPERT_FF, D_MODEL), EXPERT_FF),
        "norm_final_g": gain(ks[26], (D_MODEL,)),
    }

def second_block(x, mem, norm_mix_g, w_in, fox_bf, conv_dw_w, conv_dw_b, conv_ln_g, conv_ln_b,
              conv_pw_w, attn_branch_w, w_out, norm_xa_g, norm_mem_g, xa_wq, xa_wk, xa_wv, xa_wo,
              norm_moe_g, router_group_w, router_group_b, router_expert_w, router_expert_b,
              expert_w_gate, expert_w_up, expert_w_down, norm_final_g):
    B, T, _ = x.shape
    cuts = np.cumsum(SPLITS)[:-1].tolist()
    for l in range(DEPTH):
        h = rmsnorm_2(x, norm_mix_g[l])
        proj = h @ w_in[l]
        u_glu, q, k, v, f_logit, gate_c, gate_a = jnp.split(proj, cuts, axis=-1)
        conv_out = conformer_conv(u_glu, conv_dw_w[l], conv_dw_b[l], conv_ln_g[l],
                                  conv_ln_b[l], conv_pw_w[l])
        logf = jax.nn.log_sigmoid(f_logit.astype(jnp.float32) + fox_bf[l].astype(jnp.float32))
        attn = fox_attention(q.reshape(B, T, FOX_HEADS, FOX_HEAD_DIM),
                             k.reshape(B, T, FOX_HEADS, FOX_HEAD_DIM),
                             v.reshape(B, T, FOX_HEADS, FOX_HEAD_DIM), logf)
        attn_out = attn @ attn_branch_w[l]
        merged = jax.nn.sigmoid(gate_c) * conv_out + jax.nn.sigmoid(gate_a) * attn_out
        x = x + merged @ w_out[l]
        x = x + cross_attention(rmsnorm_2(x, norm_xa_g[l]), rmsnorm_2(mem, norm_mem_g[l]),
                                xa_wq[l], xa_wk[l], xa_wv[l], xa_wo[l])
        x = x + hierarchical_moe(rmsnorm_2(x, norm_moe_g[l]), router_group_w[l], router_group_b[l],
                                 router_expert_w[l], router_expert_b[l], expert_w_gate[l],
                                 expert_w_up[l], expert_w_down[l])
    return rmsnorm_2(x, norm_final_g)


def setup_inputs(seed=0):
    out = dict(first_inputs(seed))
    for name, value in second_inputs(seed + 1).items():
        if name != "x":
            out[name + "_2"] = value
    return out


def reference(
    x, c, ctx, c_ctx, w_ada, b_ada, g_norm1, w_in, b_gates, w_conv, w_fourier, w_mlstm, w_out,
    g_norm2, w_router, w_gate_e, w_up_e, w_down_e, g_final, mem_2, norm_mix_g_2, w_in_2,
    fox_bf_2, conv_dw_w_2, conv_dw_b_2, conv_ln_g_2, conv_ln_b_2, conv_pw_w_2, attn_branch_w_2,
    w_out_2, norm_xa_g_2, norm_mem_g_2, xa_wq_2, xa_wk_2, xa_wv_2, xa_wo_2, norm_moe_g_2,
    router_group_w_2, router_group_b_2, router_expert_w_2, router_expert_b_2, expert_w_gate_2,
    expert_w_up_2, expert_w_down_2, norm_final_g_2,
):
    x = first_block(
        x, c, ctx, c_ctx, w_ada, b_ada, g_norm1, w_in, b_gates, w_conv, w_fourier, w_mlstm,
        w_out, g_norm2, w_router, w_gate_e, w_up_e, w_down_e, g_final,
    )
    return second_block(
        x, mem_2, norm_mix_g_2, w_in_2, fox_bf_2, conv_dw_w_2, conv_dw_b_2, conv_ln_g_2,
        conv_ln_b_2, conv_pw_w_2, attn_branch_w_2, w_out_2, norm_xa_g_2, norm_mem_g_2, xa_wq_2,
        xa_wk_2, xa_wv_2, xa_wo_2, norm_moe_g_2, router_group_w_2, router_group_b_2,
        router_expert_w_2, router_expert_b_2, expert_w_gate_2, expert_w_up_2, expert_w_down_2,
        norm_final_g_2,
    )


_drawn_inputs = setup_inputs


def setup_inputs(seed=0):
    import zlib

    import numpy as np

    out = dict(_drawn_inputs(seed))
    spreads = {}
    factors = {'ctx': 2.721,
     'c_ctx': 2.727,
     'g_norm1': 3.52,
     'g_norm2': 3.233,
     'conv_dw_b_2': 3.342,
     'conv_ln_b_2': 4.357,
     'router_group_b_2': 4.934,
     'router_expert_b_2': 3.768}
    for name, (base, spread) in spreads.items():
        noise = np.random.default_rng([zlib.crc32(name.encode()), seed]).standard_normal(out[name].shape)
        drawn = base * np.exp(spread * noise) if base else spread * noise
        out[name] = __import__('jax').numpy.asarray(drawn.astype(out[name].dtype))
    for name, factor in factors.items():
        out[name] = (out[name] * factor).astype(out[name].dtype)
    return out
```

```python
from contextlib import ExitStack

import numpy as np

import concourse.bass as bass
from concourse import mybir
from concourse.alu_op_type import AluOpType as ALU

ACT = mybir.ActivationFunctionType
F32 = mybir.dt.float32
AX_X = mybir.AxisListType.X

P = 128
T = 512
TC = 256
D = 1024
KD = D // P
TT = T // P
TA = (T + TC) // P
HALF = 512
KH = HALF // P
EPS = 1e-6
GRID_W = 64
ROWS = T // GRID_W
NH = 4
QK_SCALE = float(P) ** -0.5
OFF_F, OFF_Q, OFF_K, OFF_V, OFF_O, OFF_G, OFF_BR = 0, 512, 1024, 1536, 2048, 2560, 2576
OFF_F2 = 2560
NE = 16
CAP = 64
NPAIR = NE // 2
TAPS = 31
FOX_H = 8
FOX_SCALE = 64.0 ** -0.5
NG, EPG = 4, 4
FF = 256
W2_GLU, W2_Q, W2_K, W2_V, W2_C, W2_A = 512, 1024, 1536, 2048, 2568, 3592
E2 = NG * EPG
BLK = 64
NB2 = (2 * T + E2 * (BLK - 1)) // BLK
NPAIR2 = (NB2 + 1) // 2
NSLOT = 4

VEC = {name: KD * i for i, name in enumerate(
    ["c", "c_ctx", "g_norm1", "g_norm2", "g_final", "mix", "xa", "mem", "moe", "final2"])}
VEC["b_ada"] = 80
VEC["conv2d"] = 128
VEC["dw_b"], VEC["ln_g"], VEC["ln_b"] = 200, 204, 208
VEC["dw_w"] = 212
NVEC = 336

NORMS = {name: i for i, name in enumerate(["n1", "nc", "nm", "n2", "nf", "n3", "n4", "n5", "n6"])}


def norm_out(name, k):
    return (KD + 1) * NORMS[name] + k + 2


PRODUCT_STAGES = [
    ("vec_mm", 1), ("xT_mm", 8), ("cT_mm", 4), ("k_mm", 8), ("v_mm", 6), ("gate_mm", 1), ("u_mm", 4), ("rows_mm", 1),
    ("q_mm", 4), ("o_mm", 4), ("tokg_mm", 1), ("kc_mm", 2), ("C0_mm", 4), ("Z_mm", 8), ("fu_mm", 4), ("yf_mm", 8), ("mT_mm", 4),
    ("ym_mm", 8), ("brb_mm", 8), ("wo_mm", 8), ("logit_mm", 1), ("htok_mm", 8), ("affT_mm", 1), ("km_mm", 4), ("vm_mm", 2),
    ("slotT_mm", 1), ("glu_mm", 4), ("a_mm", 4), ("v2_mm", 4), ("q2_mm", 4), ("f_mm", 1), ("k2_mm", 4), ("lnm_mm", 1),
    ("fT_mm", 1), ("pw_mm", 8), ("gam", 8), ("ab_mm", 8), ("w2o_mm", 8), ("xq_mm", 4), ("xS_mm", 8), ("xo_mm", 8), ("rl_mm", 1),
    ("h2_mm", 8),
    ("combT_mm", 1), ("ends_mm", 1), ("which_mm", 1), ("posT_mm", 1), ("ot_mm", 8),
]
COPY_STAGES = [
    ("xT_ev", 8), ("k_silu", 8), ("v_ev", 6), ("u_ev", 4), ("q_silu", 4), ("o_ev", 4), ("C0_ev", 4), ("Z_ev", 8), ("fu_ev", 4),
    ("yf_ev", 8), ("ym_ev", 8), ("brb_ev", 8), ("htok_ev", 8), ("km_ev", 4), ("vm_ev", 2), ("glu_ev", 4), ("v2_ev", 4),
    ("q2_ev", 4), ("k2_ev", 4), ("c_ready", 4), ("ga_ev", 8), ("xq_ev", 4), ("h2_ev", 8),
]


def bases(stages):
    return {name: sum(n for _, n in stages[:i]) for i, (name, _) in enumerate(stages)}


SHARED = {"product_done": bases(PRODUCT_STAGES), "copy_done": bases(COPY_STAGES)}


CONST = {"ident": 0, "ones": 128, "s_le_j": 256, "s_ge_j": 384, "future": 512, "dft": 640, "iota": 896, "pick": 960}
NCONST = 962


def constant_tables():
    i, j = np.arange(P)[:, None], np.arange(P)[None, :]
    table = np.zeros((P, NCONST))
    table[:, 0:128] = i == j
    table[:, 128:256] = 1.0
    table[:, 256:384] = i <= j
    table[:, 384:512] = i >= j
    table[:, 512:640] = np.where(j > i, -1e30, 0.0)
    table[:, 640:768] = np.cos(2 * np.pi * (i * j % P) / P)
    table[:, 768:896] = np.sin(2 * np.pi * (i * j % P) / P)
    table[:, 896:960] = np.arange(1, 65)[None, :]
    table[:, 960] = i[:, 0] % 32 == 0
    table[:, 961] = i[:, 0] % 32 == 1
    n, m = np.arange(T)[:, None], np.arange(T)[None, :]
    angle = 2 * np.pi * (n * m % T) / T
    norm = float(T * P) ** -0.5
    dft = np.concatenate([np.cos(angle) * norm, -np.sin(angle) * norm], axis=1)
    return table.astype(np.float32), dft.astype(np.float32)


def build(nc, A, out):
    with ExitStack() as ctx:
        def sb(name, *shape):
            return ctx.enter_context(nc.sbuf_tensor(name, list(shape), F32))

        sems = {}

        def sem(name):
            name = next((shared for shared, stages in SHARED.items() if name in stages), name)
            if name not in sems:
                sems[name] = ctx.enter_context(nc.semaphore(name))
            return sems[name]

        def reached(name, value):
            return sem(name), value + next((stages[name] for stages in SHARED.values() if name in stages), 0)

        ring = sb("weight_slots", P, NSLOT, 4096)
        xT = sb("xT", P, KD, T)
        H = sb("H", P, KD, T + TC)
        R14 = sb("R14", P, 8192)
        R1, R2, R3, R4 = (R14[:, 2048 * i:2048 * (i + 1)] for i in range(4))
        R5 = sb("R5", P, 2064)
        R6 = sb("R6", P, 4096)
        R7 = sb("R7", P, 4104)
        SM = sb("SM", P, 3072)
        const = sb("const", P, NCONST)
        vec = sb("vec", P, NVEC)
        mods = sb("mods", P, 48, 2)
        gains = sb("gains", P, 3, KD)
        rowb = sb("rowb", 1, 64)
        wsmall = sb("wsmall", P, KD, 60)
        C0 = sb("C0", P, 2, NH, 129)
        Mrow = sb("Mrow", 36, T)
        tokg = sb("tokg", P, 368)
        rowsB = sb("rowsB", 16, T)
        small = sb("small", P, 64)
        block_expert = ctx.enter_context(nc.sbuf_tensor("block_expert", [1, 32], mybir.dt.int32))

        ident = const[:, 0:128]
        ones = const[:, 128:256]
        masks2 = const[:, 256:512].rearrange("p (d j) -> p d j", d=2)
        dftF = const[:, 640:896]

        def v(name, i=0, n=1):
            return vec[:, VEC[name] + i:VEC[name] + i + n]

        def slot(n, k):
            return ring[:, n % NSLOT, :].rearrange("p (k n) -> p k n", k=k)

        PS = [ctx.enter_context(nc.psum_tensor(f"bank{i}", [P, 512], F32)) for i in range(8)]

        x_tok = R6[:, :].rearrange("p (t d) -> p t d", t=TT)
        c_tok = R1[:, :].rearrange("p (t d) -> p t d", t=2)
        ctxT = R2[:, :].rearrange("p (k t) -> p k t", k=KD)
        vpack = SM[:, 0:384].rearrange("p (a n) -> p a n", a=3)
        sq = SM[:, 0:1024].rearrange("p (a n) -> p a n", a=2)
        sqc = SM[:, 1024:1536].rearrange("p (a n) -> p a n", a=2)
        std = SM[:, 1536:2304]
        rstd = R7[:, 0:768]
        silu_c = sb("silu_c", P, KD, 32)
        ada_part = SM[:, 2048:3072].rearrange("p (a n) -> p a n", a=2)
        ada_part0 = R3[:, 0:1024].rearrange("p (a n) -> p a n", a=2)
        uT = R1[:, :].rearrange("p (k t) -> p k t", k=KH)
        fuT = uT
        oT = R2[:, :].rearrange("p (k t) -> p k t", k=KH)
        qT = R3[:, :].rearrange("p (k t) -> p k t", k=KH)
        kT = R4[:, :].rearrange("p (k t) -> p k t", k=KH)
        Vx = R5[:, :].rearrange("p (t h d) -> p t h d", t=TT, h=NH)
        kcT = R7[:, 0:1024].rearrange("p (k t) -> p k t", k=KH)
        Vc = R7[:, 1024:2056].rearrange("p (t h d) -> p t h d", t=2, h=NH)
        kw = R7[:, 2056:4104].rearrange("p (t e h d) -> p t e h d", t=2, e=2, h=NH)
        acc = SM[:, 0:1024].rearrange("p (a n) -> p a n", a=2)
        gts = SM[:, 1024:1120].rearrange("p (t e c h) -> p t e c h", t=TA, e=2, c=2)
        absf = SM[:, 1120:1168].rearrange("p (t e h) -> p t e h", t=TA, e=2)
        lnp = SM[:, 1168:1216].rearrange("p (t e h) -> p t e h", t=TA, e=2)
        minf = SM[:, 1216:1264].rearrange("p (t e h) -> p t e h", t=TA, e=2)
        tok_lf = SM[:, 1280:1664].rearrange("p (t e r) -> p t e r", t=TA, e=2)
        tok_lf2 = SM[:, 1280:1664].rearrange("p (t r) -> p t r", t=TA)
        tok_ig2 = SM[:, 1664:2048].rearrange("p (t r) -> p t r", t=TA)
        pick = const[:, 960:962]
        tok_ig = SM[:, 1664:2048].rearrange("p (t e r) -> p t e r", t=TA, e=2)
        lf_r = R6[0:36, 0:768]
        ig_r = R6[0:36, 768:1536]
        cum_r = R6[0:36, 1536:2304]
        a_r = R6[0:36, 2304:3072]
        zero_r = R6[0:36, 3072:3584]
        mm_r = R6[0:36, 3584:4096]
        wa_r = SM[0:36, 2048:2304]
        Z = R6[:, :].rearrange("p (t g n) -> p t g n", t=TT, g=NH)
        PT = R6[:, :].rearrange("p (t e j) -> p t e j", t=TT, e=2)
        ymT = R6[:, :].rearrange("p (k t) -> p k t", k=KD)
        merged = R7[:, 0:4096].rearrange("p (k t) -> p k t", k=KD)
        mb = SM[:, 0:1024].rearrange("p (e j) -> p e j", e=2)
        EX = SM[:, 1024:2048].rearrange("p (e j) -> p e j", e=2)
        qd = SM[:, 2048:3072].rearrange("p (e j) -> p e j", e=2)
        sig = R1[:, 0:1024].rearrange("p (a n) -> p a n", a=2)
        hm = R1[:, 1024:1536].rearrange("p (t d) -> p t d", t=TT)
        dg = R1[:, 1536:1792].rearrange("p (e n) -> p e n", e=2)
        a_t = tokg[:, 0:144].rearrange("p (t r) -> p t r", t=TT)
        enm_t = tokg[:, 144:288].rearrange("p (t r) -> p t r", t=TT)
        wa_t = tokg[:, 288:360].rearrange("p (t r) -> p t r", t=2)
        m0_b = tokg[:, 360:368]
        mend = small[0:36, 0:1]
        nmend = small[0:36, 1:2]
        m0 = small[0:36, 2:3]
        dn = small[:, 8:16].rearrange("p (t e) -> p t e", t=TT)
        den = small[:, 24:32].rearrange("p (t e) -> p t e", t=TT)
        m_tok = R4[:, :].rearrange("p (t d) -> p t d", t=2)
        memT = R2[:, :].rearrange("p (k t) -> p k t", k=KD)
        rstd2 = SM[:, 2304:3072]
        kmT = R5[:, 0:1024].rearrange("p (h t) -> p h t", h=4)
        Vm = R5[:, 1024:2048].rearrange("p (t d) -> p t d", t=2)
        h_tok = R6[:, :].rearrange("p (t d) -> p t d", t=TT)
        logit = R1[:, 0:64].rearrange("p (t e) -> p t e", t=TT)
        aff = R1[:, 64:136].rearrange("p (t e) -> p t e", t=TT)
        slot_t = R1[:, 136:208].rearrange("p (t e) -> p t e", t=TT)
        lmax = R1[:, 208:212]
        lsum = R1[:, 212:216]
        linv = R1[:, 216:220]
        work = R1[0:NE, 512:1024]
        taken = R1[0:NE, 1024:1536]
        top8 = R1[0:NE, 224:232]
        zrow = R1[0:NE, 1536:2048]
        xs = SM[:, 0:1024].rearrange("p (k s) -> p k s", k=KD)
        hidT = SM[:, 1024:2048].rearrange("p (e i s) -> p e i s", e=2, i=4)
        sg = SM[:, 2048:3072].rearrange("p (e n) -> p e n", e=2)
        selc = R7[:, 0:512].rearrange("p (t e s) -> p t e s", t=TT, e=2)
        gc = R7[:, 512:1024].rearrange("p (t e s) -> p t e s", t=TT, e=2)
        hid = R7[:, 1024:2048].rearrange("p (e n) -> p e n", e=2)
        GT = R7[:, 2048:2560]
        ypair = R7[:, 2560:3584]
        iota = const[:, 896:960]
        sgT = R2[:, :].rearrange("p (k t) -> p k t", k=KH)
        u_pad = R6[:, 0:KH * (T + TAPS - 1)].rearrange("p (k t) -> p k t", k=KH)
        cT = R1[:, :].rearrange("p (k t) -> p k t", k=KH)
        V2 = R2[:, :].rearrange("p (t h d) -> p t h d", t=TT, h=FOX_H)
        q2 = R3[:, :].rearrange("p (k t) -> p k t", k=KH)
        k2 = R4[:, :].rearrange("p (k t) -> p k t", k=KH)
        f_tok = tokg[:, 0:32].rearrange("p (t h) -> p t h", t=TT)
        f_abs = tokg[:, 32:64].rearrange("p (t h) -> p t h", t=TT)
        f_ln = tokg[:, 64:96].rearrange("p (t h) -> p t h", t=TT)
        f_row = Mrow[0:FOX_H, :]
        zero8 = R7[0:FOX_H, 0:T]
        rt = {}
        c = 0
        for name, dims in (("log", (TT, 20)), ("gmax", (TT,)), ("gexp", (TT, 4)), ("gsel", (TT, 4)), ("run", (TT, 4)), ("mix", (TT, 4, 4)),
                           ("esel", (TT, 4)), ("emax", (TT,)), ("p", (TT, 4)), ("gsum", (TT,)), ("pg", (TT,)), ("m1", (TT, 4)),
                           ("p2", (TT, 4)), ("m2", (TT, 4)), ("comb", (TT, 4, 4))):
            n = int(np.prod(dims))
            a = R7[:, c:c + n]
            if len(dims) == 2:
                a = a.rearrange("p (t n) -> p t n", t=TT)
            if len(dims) == 3:
                a = a.rearrange("p (t g j) -> p t g j", t=TT, g=4)
            rt[name] = a
            c += n
        c_row = rowsB[:, :]
        cb = C0[:, :, :, :].rearrange("p a b c -> p (a b c)")[:, 0:1024].rearrange("p (e n) -> p e n", e=2)
        Pbuf = [SM[:, 0:2560], R6[:, 0:2560]]
        PT2 = R6[:, 2560:3840]
        nmax = tokg[:, 96:128]
        psum_ = tokg[:, 128:160]
        prec = tokg[:, 160:192]
        sigA = R6[:, :].rearrange("p (k t) -> p k t", k=KD)
        tmp2 = SM[:, 0:1024].rearrange("p (a n) -> p a n", a=2)
        Px = R6[:, :].rearrange("p (h i m) -> p h i m", h=4, i=TT)
        PTx = R7[:, 0:4096].rearrange("p (h m q) -> p h m q", h=4, m=2)
        xmax = tokg[:, 192:208].rearrange("p (h i) -> p h i", h=4)
        xsum = tokg[:, 208:224].rearrange("p (h i) -> p h i", h=4)
        xrec = tokg[:, 224:240].rearrange("p (h i) -> p h i", h=4)
        h2_tok = R6[:, :].rearrange("p (t d) -> p t d", t=TT)
        chosen = rowsB[0:E2, :]
        place = Mrow[0:E2, :]
        zero16 = R7[0:E2, 3584:4096]
        thresh = R7[0:E2, 3072:3072 + T // BLK]
        over = R7[0:E2, 3088:3088 + T // BLK]
        nblk, ends, blk_base = (R7[0:E2, 3104 + i:3105 + i] for i in range(3))
        ended = R7[0:E2, 3112:3112 + 32]
        iota2 = R7[:, 3144:3144 + 2 * BLK]
        pos_t = R7[:, 3272:3336].rearrange("p (t e) -> p t e", t=TT)
        hit_t = R7[:, 3336:3400].rearrange("p (t e) -> p t e", t=TT)
        pos2 = R7[:, 3400:3408].rearrange("p (a t) -> p a t", a=2)
        wt2 = R7[:, 3408:3416].rearrange("p (a t) -> p a t", a=2)
        xb = SM[:, 0:1024].rearrange("p (k s) -> p k s", k=KD)
        hits = [SM[:, 1024 + 512 * a:1536 + 512 * a].rearrange("p (t s) -> p t s", t=TT) for a in range(2)]
        selb = SM[:, 2048:2560].rearrange("p (t s) -> p t s", t=TT)
        gb = SM[:, 2560:3072].rearrange("p (t s) -> p t s", t=TT)
        GTb = R7[:, 1024:1536]
        yb = R7[:, 1536:2560]
        sgb = R14[:, 0:FF]
        hb = R14[:, FF:2 * FF]
        hbT = R14[:, 2 * FF:3 * FF].rearrange("p (i s) -> p i s", i=2)
        out_tok = R7[:, 0:4096].rearrange("p (t d) -> p t d", t=TT)
        rec = small[:, 16:24].rearrange("p (t e) -> p t e", t=TT)

        w_in, w_ada = A["w_in"][0], A["w_ada"][0]

        def cols(w, c0, n=512):
            return w[:, c0:c0 + n].rearrange("(k p) n -> p k n", p=P)

        W = []
        for s in range(4):
            W.append((f"ada{s}", cols(w_ada, 512 * s), "ada_mm", s + 1))
        W.append(("k", cols(w_in, OFF_K), "k_mm", 8))
        W.append(("v", cols(w_in, OFF_V), "v_mm", 6))
        W.append(("u", cols(w_in, OFF_F), "u_mm", 4))
        W.append(("q", cols(w_in, OFF_Q), "q_mm", 4))
        W.append(("o", cols(w_in, OFF_O), "o_mm", 4))
        for s in range(4, 12):
            W.append((f"ada{s}", cols(w_ada, 512 * s), "ada_mm", s + 1))
        W.append(("dft", A["dft"].rearrange("(k p) n -> p k n", p=P), "fu_mm", 4))
        W.append(("w_fourier", A["w_fourier"][0].rearrange("(k p) n -> p k n", p=P), "yf_mm", 8))
        W.append(("brA0", cols(w_in, OFF_BR), "bra_mm", 4))
        W.append(("brA1", cols(w_in, OFF_BR + 512), "bra_mm", 8))
        W.append(("w_mlstm", A["w_mlstm"][0].rearrange("(k p) n -> p k n", p=P), "ym_mm", 8))
        W.append(("brB0", cols(w_in, OFF_BR + 1024), "brb_mm", 4))
        W.append(("brB1", cols(w_in, OFF_BR + 1536), "brb_mm", 8))
        W.append(("wo0", cols(A["w_out"][0], 0), "wo_mm", 4))
        W.append(("wo1", cols(A["w_out"][0], 512), "wo_mm", 8))
        W.append(("xa_wk", cols(A["xa_wk_2"][0], 0), "km_mm", 4))
        W.append(("xa_wv", cols(A["xa_wv_2"][0], 0), "vm_mm", 2))
        w2 = A["w_in_2"][0]
        W2 = [("glu", cols(w2, W2_GLU), "glu_mm", 4), ("a", cols(w2, 0), "a_mm", 4), ("v2", cols(w2, W2_V), "v2_mm", 4),
              ("q2", cols(w2, W2_Q), "q2_mm", 4), ("k2", cols(w2, W2_K), "k2_mm", 4),
              ("gc0", cols(w2, W2_C), "gcm", 4), ("gc1", cols(w2, W2_C + 512), "gcm", 8),
              ("pw", A["conv_pw_w_2"][0].rearrange("(k p) n -> p k n", p=P), "pw_mm", 8),
              ("ga0", cols(w2, W2_A), "gam", 4), ("ga1", cols(w2, W2_A + 512), "gam", 8),
              ("ab", A["attn_branch_w_2"][0].rearrange("(k p) n -> p k n", p=P), "ab_mm", 8),
              ("w2o0", cols(A["w_out_2"][0], 0), "w2o_mm", 4), ("w2o1", cols(A["w_out_2"][0], 512), "w2o_mm", 8),
              ("xa_wq", cols(A["xa_wq_2"][0], 0), "xq_mm", 4),
              ("xa_wo", A["xa_wo_2"][0].rearrange("(k p) n -> p k n", p=P), "xo_mm", 8)]
        at = {w[0]: n for n, w in enumerate(W)}
        n_moe = len(W)
        n_two = n_moe + 12 * NPAIR
        at.update({w[0]: n_two + n for n, w in enumerate(W2)})
        n_end = n_two + len(W2)
        arrived = [sem(f"slot{i}_arrived") for i in range(NSLOT)]

        def weights(name, k):
            return slot(at[name], k)

        def wait_weights(e, name):
            n = at[name]
            e.wait_ge(arrived[n % NSLOT], 16 * (n // NSLOT + 1))

        block = ctx.enter_context(nc.Block())

        @block.sync
        def _(sp):
            row = 0
            for name, rows in (("c", 8), ("c_ctx", 8), ("g_norm1", 8), ("g_norm2", 8), ("g_final", 8),
                               ("norm_mix_g_2", 8), ("norm_xa_g_2", 8), ("norm_mem_g_2", 8),
                               ("norm_moe_g_2", 8), ("norm_final_g_2", 8), ("b_ada", 48)):
                src = A[name]
                if len(src.shape) == 1:
                    src = src.rearrange("(a n) -> a n", a=1)
                sp.dma_start(vpack[row:row + rows, 0, :],
                             src.rearrange("a (k n) -> (a k) n", n=P)).then_inc(sem("vecs_in"), 16)
                row += rows
            sp.dma_start(vpack[0:72, 1, :], A["w_conv"].rearrange("a y x (k n) -> (a y x k) n", n=P)).then_inc(sem("vecs_in"), 16)
            row = 72
            for name in ("conv_dw_b_2", "conv_ln_g_2", "conv_ln_b_2"):
                sp.dma_start(vpack[row:row + 4, 1, :], A[name].rearrange("a (k n) -> (a k) n", n=P)).then_inc(sem("vecs_in"), 16)
                row += 4
            sp.dma_start(vpack[0:124, 2, :], A["conv_dw_w_2"].rearrange("a w (k n) -> (a w k) n", n=P)).then_inc(sem("vecs_in"), 16)
            for n, (name, src, free, value) in enumerate(W):
                if n >= NSLOT:
                    sp.wait_ge(*reached(W[n - NSLOT][2], W[n - NSLOT][3]))
                sp.dma_start(ring[:, n % NSLOT, :].rearrange("p (k n) -> p k n", k=src.shape[1]), src).then_inc(arrived[n % NSLOT], 16)

            n0 = len(W)

            def expert_slot(pair, i):
                if i < 8:
                    name, e, half = ("w_gate_e", "w_up_e")[i % 4 // 2], i // 4, i % 2
                else:
                    name, e, half = "w_down_e", i % 2, (i - 8) // 2
                src = A[name][0].rearrange("(q e) (k p) n -> p q e k n", e=2, p=P)[:, bass.ds(pair, 1), e, :, 512 * half:512 * half + 512]
                s = (n0 + i) % NSLOT
                dst = ring[:, s, :].rearrange("p (q k n) -> p q k n", q=1, k=KD)
                sp.dma_start(dst, src).then_inc(arrived[s], 16)

            for i in range(4):
                w = W[n0 + i - NSLOT]
                sp.wait_ge(*reached(w[2], w[3]))
                expert_slot(0, i)
            with sp.Fori(0, NPAIR - 1) as pair:
                for i in range(4, 16):
                    sp.wait_ge(sem("moe_mm"), pair * 6 + ((i - 4) // 2 + 1))
                    sp.sem_inc(sem("sp_step"), 1)
                    expert_slot(pair if i < 12 else pair + 1, i % 12)
            for i in range(4, 12):
                sp.wait_ge(sem("moe_mm"), 6 * (NPAIR - 1) + (i - 4) // 2 + 1)
                expert_slot(NPAIR - 1, i)
            for n, (name, src, free, value) in enumerate(W2):
                if n < NSLOT:
                    sp.wait_ge(sem("moe_mm"), 6 * (NPAIR - 1) + (n + 8) // 2 + 1)
                else:
                    sp.wait_ge(*reached(W2[n - NSLOT][2], W2[n - NSLOT][3]))
                s = (n_two + n) % NSLOT
                sp.dma_start(ring[:, s, :].rearrange("p (k n) -> p k n", k=src.shape[1]), src).then_inc(arrived[s], 16)

            def expert_of(block):
                return sp.value_load(block_expert[0:1, bass.ds(block, 1)], min_val=0, max_val=E2 - 1)

            def load_gate_up(e, i):
                for j, name in enumerate(("expert_w_gate_2", "expert_w_up_2")):
                    src = A[name][0].rearrange("e (k p) n -> p e k n", p=P)[:, bass.ds(e, 1), :, :]
                    dst = ring[:, i, :].rearrange("p (q k n) -> p q k n", q=1, k=KD)[:, :, :, FF * j:FF * (j + 1)]
                    sp.dma_start(dst, src).then_inc(sem(f"gate_up{i}_in"), 16)

            def load_down(e, i):
                src = A["expert_w_down_2"][0].rearrange("e (k p) n -> p e k n", p=P)[:, bass.ds(e, 1), :, :]
                dst = ring[:, 2, 2048 * i:2048 * (i + 1)].rearrange("p (q k n) -> p q k n", q=1, k=2)
                sp.dma_start(dst, src).then_inc(sem("down_in"), 16)

            for s in range(3):
                last = max(n for n in range(n_end) if n % NSLOT == s)
                sp.wait_ge(*reached(W2[last - n_two][2], W2[last - n_two][3]))
            sp.wait_ge(sem("block_expert"), 1)
            first = [expert_of(i) for i in range(2)]
            for i in range(2):
                load_gate_up(first[i], i)
            for i in range(2):
                load_down(first[i], i)
            with sp.Fori(1, NPAIR2) as pair:
                both = [expert_of(pair * 2 + i) for i in range(2)]
                sp.wait_ge(sem("b_gate_up"), pair)
                sp.sem_inc(sem("sp_step"), 1)
                for i in range(2):
                    load_gate_up(both[i], i)
                sp.wait_ge(sem("b_down"), pair * 2)
                sp.sem_inc(sem("sp_step"), 1)
                for i in range(2):
                    load_down(both[i], i)
            for j in range(8):
                sp.wait_ge(sem("ot_ev"), j + 1)
                t, c = j // 2, 512 * (j % 2)
                sp.dma_start(out[0, 128 * t:128 * (t + 1), c:c + 512], out_tok[:, t, c:c + 512]).then_inc(sem("out_written"), 16)
            sp.wait_ge(sem("out_written"), 16 * 8)

        def rms_squares(act, name, src, buf, width, ready, prev=None):
            for k in range(KD):
                ready(k)
                if k >= 2:
                    act.wait_ge(sem("rms_sum"), KD * NORMS[name] + k - 1)
                act.activation(buf[:, k % 2, 0:width], src[:, k, 0:width], ACT.Square).then_inc(sem("rms_sq"), 1)

        def rms_root(act, name, bank, dst):
            act.wait_ge(sem("rms_sum"), KD * NORMS[name] + KD)
            act.activation(dst, bank, ACT.Sqrt, bias=small[:, 40:41], scale=1.0 / D).then_inc(sem("rms_std"), 1)

        def rms_sum(pe, name, bank, buf, width):
            for k in range(KD):
                pe.wait_ge(sem("rms_sq"), KD * NORMS[name] + k + 1)
                nc.tensor.matmul(bank[:, 0:width], ones, buf[:, k % 2, 0:width], start=(k == 0),
                                 stop=(k == KD - 1)).then_inc(sem("rms_sum"), 1)

        def rms_scale(dve, name, src, dst, width, std_, rstd_, gain):
            dve.wait_ge(sem("rms_std"), NORMS[name] + 1)
            nc.vector.reciprocal(rstd_, std_).then_inc(sem("rms_out"), 1)
            dve.wait_ge(sem("rms_out"), (KD + 1) * NORMS[name] + 1)
            for k in range(KD):
                nc.vector.scalar_tensor_tensor(out=dst(k), in0=src(k), scalar=gain(k), in1=rstd_,
                                               op0=ALU.mult, op1=ALU.mult).then_inc(sem("rms_out"), 1)

        @block.scalar
        def _(act):
            act.dma_start(const[:, :], A["consts"]).then_inc(sem("const_in"), 16)
            act.dma_start(x_tok, A["x"].rearrange("b (t p) d -> p (b t) d", p=P)).then_inc(sem("x_in"), 16)
            act.dma_start(c_tok, A["ctx"].rearrange("b (t p) d -> p (b t) d", p=P)).then_inc(sem("ctx_in"), 16)
            act.dma_start(rowb[0:1, 0:16], A["b_gates"].rearrange("a g h -> a (g h)")).then_inc(sem("rowb_in"), 16)
            act.dma_start(rowb[0:1, 16:24], A["fox_bf_2"]).then_inc(sem("rowb_in"), 16)
            act.dma_start(rowb[0:1, 24:28], A["router_group_b_2"]).then_inc(sem("rowb_in"), 16)
            act.dma_start(rowb[0:1, 28:44], A["router_expert_b_2"]).then_inc(sem("rowb_in"), 16)
            c = 0
            for src in (w_in[:, OFF_G:OFF_BR], A["w_router"][0], A["w_in_2"][0, :, OFF_F2:OFF_F2 + 8], A["router_group_w_2"][0], A["router_expert_w_2"][0]):
                n = src.shape[1]
                act.dma_start(wsmall[:, :, c:c + n], src.rearrange("(k p) n -> p k n", p=P)).then_inc(sem("wsmall_in"), 16)
                c += n
            act.wait_ge(sem("vec_ready"), 1)
            act.wait_ge(sem("zeros_ready"), 1)
            act.wait_ge(sem("boot"), 2)
            for i, name in enumerate(("c", "c_ctx")):
                act.activation(silu_c[:, :, i], v(name, 0, KD), ACT.Silu).then_inc(sem("silu_c"), 1)
            for k in range(KD):
                act.wait_ge(*reached("xT_mm", k + 1))
                act.activation(xT[:, k, :], PS[k % 4][:, :], ACT.Copy).then_inc(sem("xT_ev"), 1)
            rms_squares(act, "n1", xT, sq, T, lambda k: act.wait_ge(*reached("xT_ev", k + 1)))
            rms_root(act, "n1", PS[0][:, :], std[:, 0:T])
            rms_squares(act, "nc", ctxT, sqc, TC, lambda k: act.wait_ge(sem("cT_ev"), k // 2 + 1))
            rms_root(act, "nc", PS[1][:, 0:TC], std[:, T:T + TC])
            for k in range(KD):
                act.wait_ge(sem("rms_out"), norm_out("n1", k))
                act.wait_ge(sem("gains1"), 3)
                act.activation(H[:, k, 0:T], H[:, k, 0:T], ACT.Identity, bias=mods[:, k, 0:1]).then_inc(sem("h_ready"), 1)
                act.wait_ge(sem("rms_out"), norm_out("nc", k))
                act.activation(H[:, k, T:T + TC], H[:, k, T:T + TC], ACT.Identity, bias=mods[:, k, 1:2]).then_inc(sem("h_ready"), 1)
            for j in range(8):
                act.wait_ge(sem("conv_k"), 3 * (j + 1) if j < 4 else 12 + 9 * (j - 3))
                dst, src = (kcT[:, j, :], acc[:, j % 2, 0:TC]) if j < 4 else (kT[:, j - 4, :], acc[:, j % 2, :])
                act.activation(dst, src, ACT.Silu).then_inc(sem("k_silu"), 1)
            for t in range(TA):
                act.wait_ge(*reached("v_mm", t + 1))
                dst = Vx[:, t, :, 0:128] if t < TT else Vc[:, t - TT, :, 0:128]
                act.activation(dst, PS[(4, 5, 6, 7)[t % 4]][:, :].rearrange("p (h d) -> p h d", h=NH), ACT.Copy).then_inc(sem("v_ev"), 1)
            act.wait_ge(sem("gate_v"), 1)
            act.activation(absf, gts[:, :, :, 1, :], ACT.Abs).then_inc(sem("gate_s"), 1)
            act.wait_ge(sem("gate_s"), 1)
            act.activation(absf, absf, ACT.Exp, scale=-1.0).then_inc(sem("gate_s"), 1)
            act.wait_ge(sem("gate_s"), 2)
            act.activation(lnp, absf, ACT.Ln, bias=1.0).then_inc(sem("gate_s"), 1)
            for j in range(4):
                act.wait_ge(*reached("u_mm", j + 1))
                act.activation(uT[:, j, :], PS[4 + j][:, :], ACT.Copy).then_inc(sem("u_ev"), 1)
            act.wait_ge(*reached("rows_mm", 1))
            act.activation(ig_r[:, 0:T], PS[1][0:36, :], ACT.Copy).then_inc(sem("rows_s"), 1)
            act.wait_ge(sem("rows_v"), 11)
            act.activation(wa_r, a_r[:, T:T + TC], ACT.Exp, bias=nmend).then_inc(sem("rows_s"), 1)
            act.wait_ge(sem("rows_v"), 16)
            act.activation(mm_r, mm_r, ACT.Exp, scale=-1.0).then_inc(sem("rows_s"), 1)
            for j in range(4):
                act.wait_ge(sem("conv_q"), 9 * (j + 1))
                act.activation(qT[:, j, :], acc[:, j % 2, :], ACT.Silu).then_inc(sem("q_silu"), 1)
            for j in range(4):
                act.wait_ge(*reached("o_mm", j + 1))
                act.activation(oT[:, j, :], PS[j][:, :], ACT.Sigmoid).then_inc(sem("o_ev"), 1)
            for h in range(NH):
                act.wait_ge(*reached("C0_mm", h + 1))
                act.activation(C0[:, :, h, :], PS[2 + h % 2][:, 0:258].rearrange("p (e d) -> p e d", e=2), ACT.Copy).then_inc(sem("C0_ev"), 1)
            for j in range(8):
                act.wait_ge(*reached("Z_mm", j + 1))
                act.activation(Z[:, j // 2, 2 * (j % 2):2 * (j % 2) + 2, :], PS[4 + j % 4][:, :].rearrange("p (g n) -> p g n", g=2), ACT.Copy).then_inc(sem("Z_ev"), 1)
            for g in range(4):
                act.wait_ge(*reached("fu_mm", g + 1))
                act.activation(fuT[:, g, :], PS[g][:, :], ACT.Copy).then_inc(sem("fu_ev"), 1)
            for j in range(8):
                act.wait_ge(*reached("yf_mm", j + 1))
                act.activation(merged[:, j, :], PS[4 + j % 4][:, :], ACT.Copy).then_inc(sem("yf_ev"), 1)

            def gate_a(j):
                act.wait_ge(sem("bra_mm"), j + 1)
                if j >= 2:
                    act.wait_ge(sem("bra_v"), j - 1)
                act.activation(sig[:, j % 2, :], PS[6 + j % 2][:, :], ACT.Sigmoid).then_inc(sem("bra_ev"), 1)

            for h in range(NH):
                for e in range(2):
                    act.wait_ge(sem("mb_mm"), 2 * h + e + 1)
                    if e == 0 and h >= 1:
                        act.wait_ge(sem("attn_v"), 23 * h - 1)
                    act.activation(mb[:, e, :], PS[e][:, :], ACT.Copy).then_inc(sem("mb_ev"), 1)
                for e in range(2):
                    act.wait_ge(sem("mb_ev"), 2 * h + e + 1)
                    if e == 0 and h >= 1:
                        act.wait_ge(sem("pv_mm"), 4 * h)
                    act.activation(qd[:, e, :], mb[:, e, :], ACT.Exp, scale=-1.0, bias=m0_b[:, 4 * e + h:4 * e + h + 1]).then_inc(sem("dec_s"), 1)
                for t in range(TT):
                    if h or t:
                        act.wait_ge(sem("attn_v"), 23 * h + 2 + 5 * t if t else 23 * h - 1)
                    if t < 3:
                        act.activation(EX[:, 0, 128 * (t + 1):T], mb[:, 0, 128 * (t + 1):T], ACT.Exp, scale=-1.0, bias=a_t[:, t, h:h + 1]).then_inc(sem("E_off"), 1)
                    if t > 0:
                        act.activation(EX[:, 1, 0:128 * t], mb[:, 1, 0:128 * t], ACT.Exp, scale=-1.0, bias=a_t[:, t, 32 + h:33 + h]).then_inc(sem("E_off"), 1)
                    act.wait_ge(sem("attn_v"), 23 * h + 4 + 5 * t)
                    act.activation(EX[:, :, 128 * t:128 * (t + 1)], dg[:, :, :], ACT.Exp, scale=-1.0).then_inc(sem("E_diag"), 1)
                    if t == 1:
                        gate_a(2 * h)
                    if t == 3:
                        gate_a(2 * h + 1)
            act.wait_ge(sem("S_mm"), 16)
            act.dma_start(m_tok, A["mem_2"].rearrange("b (t p) d -> p (b t) d", p=P)).then_inc(sem("mem_in"), 16)
            rms_squares(act, "nm", memT, sqc, TC, lambda k: act.wait_ge(sem("mT_ev"), k // 2 + 1))
            rms_root(act, "nm", PS[5][:, 0:TC], std[:, T:T + TC])
            for j in range(8):
                act.wait_ge(*reached("ym_mm", j + 1))
                act.activation(ymT[:, j, :], PS[j % 4][:, :], ACT.Copy).then_inc(sem("ym_ev"), 1)
            for j in range(8):
                act.wait_ge(*reached("brb_mm", j + 1))
                if j >= 2:
                    act.wait_ge(sem("brb_v"), 2 * (j - 1))
                else:
                    act.wait_ge(sem("bra_v"), 8)
                act.activation(sig[:, j % 2, :], PS[4 + j % 4][:, :], ACT.Sigmoid).then_inc(sem("brb_ev"), 1)
            rms_squares(act, "n2", xT, sq, T, lambda k: act.wait_ge(sem("x1"), k + 1))
            rms_root(act, "n2", PS[4][:, :], std[:, 0:T])
            for k in range(KD):
                act.wait_ge(sem("rms_out"), norm_out("n2", k))
                act.activation(H[:, k, 0:T], H[:, k, 0:T], ACT.Identity, bias=mods[:, 24 + k, 0:1]).then_inc(sem("h2_ready"), 1)
            act.wait_ge(sem("aff_v"), 2)
            act.activation(logit, logit, ACT.Exp).then_inc(sem("aff_s"), 1)
            for j in range(8):
                act.wait_ge(*reached("htok_mm", j + 1))
                act.activation(h_tok[:, j // 2, 512 * (j % 2):512 * (j % 2) + 512], PS[j % 4][:, :], ACT.Copy).then_inc(sem("htok_ev"), 1)
            for j in range(4):
                act.wait_ge(*reached("km_mm", j + 1))
                act.activation(kmT[:, j, :], PS[j][:, 0:TC], ACT.Copy).then_inc(sem("km_ev"), 1)
            for j in range(2):
                act.wait_ge(*reached("vm_mm", j + 1))
                act.activation(Vm[:, j, :], PS[6 + j][:, :], ACT.Copy).then_inc(sem("vm_ev"), 1)

            def xs_copy(i, gathered):
                act.wait_ge(sem("gather_mm"), gathered)
                act.activation(xs[:, 4 * i:4 * i + 4, :], PS[i][:, :].rearrange("p (k s) -> p k s", k=4), ACT.Copy).then_inc(sem("xs_ev"), 1)

            for i in range(2):
                xs_copy(i, i + 1)
            with act.Fori(0, NPAIR) as pair:
                for e in range(2):
                    act.wait_ge(sem("moe_mm"), pair * 6 + (2 * e + 1))
                    act.wait_ge(sem("hid_v"), pair * 2 + (e + 1))
                    act.activation(sg[:, e, :], PS[2 * e][:, :], ACT.Silu).then_inc(sem("sg_s"), 1)
                act.wait_ge(sem("tr_mm"), pair * 2 + 1)
                act.activation(hidT[:, 0, :, :], PS[4][:, :].rearrange("p (i s) -> p i s", i=4), ACT.Copy).then_inc(sem("hidT_ev"), 1)
                for i in range(2):
                    xs_copy(i, pair * 2 + (3 + i))
                act.wait_ge(sem("tr_mm"), pair * 2 + 2)
                act.activation(hidT[:, 1, :, :], PS[5][:, :].rearrange("p (i s) -> p i s", i=4), ACT.Copy).then_inc(sem("hidT_ev"), 1)
                act.wait_ge(sem("gt_mm"), pair + 1)
                act.activation(GT, PS[4][:, :], ACT.Copy).then_inc(sem("gt_ev"), 1)
                act.wait_ge(sem("moe_mm"), pair * 6 + 5)
                act.activation(ypair[:, 0:512], PS[6][:, :], ACT.Copy).then_inc(sem("y0_ev"), 1)

            def norm_root(name, x_ready, bank):
                rms_squares(act, name, xT, sq, T, x_ready)
                rms_root(act, name, PS[bank][:, :], std[:, 0:T])

            act.wait_ge(sem("sc_mm"), 8 * (NPAIR + 1))
            norm_root("nf", lambda k: act.wait_ge(sem("sc_v"), 8 * (NPAIR + 1) + k + 1), 4)
            norm_root("n3", lambda k: act.wait_ge(sem("rms_out"), norm_out("nf", k)), 4)
            for j in range(4):
                act.wait_ge(*reached("glu_mm", j + 1))
                act.activation(sgT[:, j, :], PS[j][:, :], ACT.Sigmoid).then_inc(sem("glu_ev"), 1)
            for j in range(4):
                act.wait_ge(*reached("v2_mm", j + 1))
                if j == 0:
                    act.wait_ge(sem("u_v"), 5)
                act.activation(V2[:, j, :, :], PS[j][:, :].rearrange("p (h d) -> p h d", h=FOX_H), ACT.Copy).then_inc(sem("v2_ev"), 1)
            for name, dst, b0 in (("q2", q2, 4), ("k2", k2, 0)):
                for j in range(4):
                    act.wait_ge(*reached(f"{name}_mm", j + 1))
                    act.activation(dst[:, j, :], PS[b0 + j][:, :], ACT.Copy).then_inc(sem(f"{name}_ev"), 1)
            act.wait_ge(sem("f_v"), 1)
            act.activation(f_abs, f_tok, ACT.Abs).then_inc(sem("f_s"), 1)
            act.wait_ge(sem("f_s"), 1)
            act.activation(f_abs, f_abs, ACT.Exp, scale=-1.0).then_inc(sem("f_s"), 1)
            act.wait_ge(sem("f_s"), 2)
            act.activation(f_ln, f_abs, ACT.Ln, bias=1.0).then_inc(sem("f_s"), 1)
            for k in range(KH):
                act.wait_ge(sem("ln_v"), k + 1)
                if k >= 2:
                    act.wait_ge(sem("lnq_mm"), k - 1)
                act.activation(sq[:, k % 2, :], cT[:, k, :], ACT.Square).then_inc(sem("ln_sq"), 1)
            act.wait_ge(sem("lnq_mm"), KH)
            act.activation(std[:, 0:T], PS[5][:, :], ACT.Sqrt, bias=small[:, 40:41], scale=1.0 / HALF).then_inc(sem("ln_std"), 1)
            for k in range(KH):
                act.wait_ge(sem("ln_v"), KH + 2 + k)
                act.activation(cT[:, k, :], cT[:, k, :], ACT.Silu, bias=v("ln_b", k)).then_inc(sem("c_ready"), 1)

            def cb_copy(hp):
                for e in range(2):
                    act.wait_ge(sem("cb_mm"), 2 * hp + e + 1)
                    if e == 0 and hp:
                        act.wait_ge(sem("L_v"), 24 * hp)
                    act.activation(cb[:, e, :], PS[6 + e][:, :], ACT.Copy).then_inc(sem("cb_ev"), 1)

            def probs(hp):
                for i in range(TT):
                    for e in range(2):
                        n = 8 * hp + 2 * i + e
                        w = 128 * (i + 1)
                        c = 1280 * e + 64 * i * (i + 1)
                        p_ = Pbuf[hp % 2][:, c:c + w]
                        act.wait_ge(sem("L_v"), 3 * (n + 1))
                        act.activation(p_, p_, ACT.Exp, bias=nmax[:, n:n + 1], accum_out=psum_[:, n:n + 1]).then_inc(sem("exp_s"), 1)
                        if n:
                            scale_probs(n - 1)

            def scale_probs(n):
                hp, i, e = n // 8, n % 8 // 2, n % 2
                c = 1280 * e + 64 * i * (i + 1)
                p_ = Pbuf[hp % 2][:, c:c + 128 * (i + 1)]
                act.wait_ge(sem("prec_v"), n + 1)
                act.activation(p_, p_, ACT.Copy, scale=prec[:, n:n + 1]).then_inc(sem("P_ready"), 1)

            def gate_c(j):
                act.wait_ge(sem("gcm"), j + 1)
                act.activation(merged[:, j, :], PS[4 + j % 2][:, :], ACT.Sigmoid).then_inc(sem("gc_ev"), 1)

            cb_copy(0)
            probs(0)
            for hp in range(FOX_H // 2):
                if hp + 1 < FOX_H // 2:
                    cb_copy(hp + 1)
                    probs(hp + 1)
                else:
                    scale_probs(FOX_H * TT - 1)
                gate_c(2 * hp)
                gate_c(2 * hp + 1)
                for e in range(2):
                    for t in range(TT):
                        n = 8 * hp + 4 * e + t
                        act.wait_ge(sem("PT_mm"), n + 1)
                        if t == 0 and n:
                            act.wait_ge(sem("pv2_mm"), 2 * hp + e)
                        c = (0, 512, 896, 1152)[t]
                        act.activation(PT2[:, c:c + 512 - 128 * t], PS[6 + t % 2][:, 128 * t:512], ACT.Copy).then_inc(sem("PT_ev"), 1)
                act.wait_ge(sem("pv2_mm"), 2 * hp + 2)
                act.activation(q2[:, hp, :], PS[5][:, :], ACT.Copy).then_inc(sem("attn_ev"), 1)
            for j in range(8):
                act.wait_ge(*reached("gam", j + 1))
                if j == 0:
                    act.wait_ge(sem("pv2_mm"), FOX_H)
                act.activation(sigA[:, j, :], PS[4 + j % 4][:, :], ACT.Sigmoid).then_inc(sem("ga_ev"), 1)
            act.wait_ge(sem("ab_v"), 16)
            norm_root("n4", lambda k: act.wait_ge(sem("x3"), k + 1), 4)
            for j in range(4):
                act.wait_ge(*reached("xq_mm", j + 1))
                act.activation(q2[:, j, :], PS[j][:, :], ACT.Copy).then_inc(sem("xq_ev"), 1)
            for h in range(4):
                for i in range(TT):
                    n = 4 * h + i
                    act.wait_ge(sem("xmax_v"), 2 * h + 2)
                    act.activation(Px[:, h, i, :], PS[2 * h % 8 + i // 2][:, 256 * (i % 2):256 * (i % 2) + 256], ACT.Exp, scale=QK_SCALE,
                                   bias=xmax[:, h, i:i + 1], accum_out=xsum[:, h, i:i + 1]).then_inc(sem("xexp_s"), 1)
            for h in range(4):
                for i in range(TT):
                    act.wait_ge(sem("xrec_v"), 1)
                    act.activation(Px[:, h, i, :], Px[:, h, i, :], ACT.Copy, scale=xrec[:, h, i:i + 1]).then_inc(sem("xP_ready"), 1)
            for h in range(4):
                for m in range(2):
                    act.wait_ge(sem("xT2_mm"), 2 * h + m + 1)
                    act.activation(PTx[:, h, m, :], PS[2 * (h % 2) + m][:, :], ACT.Copy).then_inc(sem("xT2_ev"), 1)
            norm_root("n5", lambda k: act.wait_ge(sem("x4"), k + 1), 4)
            act.wait_ge(sem("g_v"), 3)
            act.activation(rt["gexp"], rt["gexp"], ACT.Exp).then_inc(sem("g_s"), 1)

            def h2_copy(j):
                act.wait_ge(*reached("h2_mm", j + 1))
                act.activation(h2_tok[:, j // 2, 512 * (j % 2):512 * (j % 2) + 512], PS[j % 4][:, :], ACT.Copy).then_inc(sem("h2_ev"), 1)

            for j in range(4):
                h2_copy(j)
            act.wait_ge(sem("g_v"), 14)
            act.activation(rt["p"], rt["p"], ACT.Exp).then_inc(sem("g_s"), 1)
            for j in range(4, 8):
                h2_copy(j)

            def xb_copy(i, gathered):
                act.wait_ge(sem("b_gather"), gathered)
                act.activation(xb[:, 4 * i:4 * i + 4, :], PS[i][:, :].rearrange("p (k s) -> p k s", k=4), ACT.Copy).then_inc(sem("b_x"), 1)

            for i in range(2):
                xb_copy(i, i + 1)
            with act.Fori(0, NPAIR2) as pair:
                act.wait_ge(sem("b_gate_up"), pair + 1)
                act.activation(sgb, PS[2][:, 0:FF], ACT.Silu).then_inc(sem("b_silu"), 1)
                act.wait_ge(sem("b_turn"), pair + 1)
                act.activation(hbT, PS[5][:, 0:FF].rearrange("p (i s) -> p i s", i=2), ACT.Copy).then_inc(sem("b_hidT"), 1)
                for i in range(2):
                    xb_copy(i, pair * 2 + (3 + i))
                act.wait_ge(sem("b_turn_g"), pair + 1)
                act.activation(GTb, PS[5][:, :], ACT.Copy).then_inc(sem("b_GT"), 1)
                act.wait_ge(sem("b_down"), pair * 2 + 1)
                act.activation(yb[:, 0:512], PS[6][:, :], ACT.Copy).then_inc(sem("b_y0"), 1)
            norm_root("n6", lambda k: act.wait_ge(sem("x5"), 8 * (NPAIR2 + 1) + k + 1), 4)
            for j in range(8):
                act.wait_ge(*reached("ot_mm", j + 1))
                act.activation(out_tok[:, j // 2, 512 * (j % 2):512 * (j % 2) + 512], PS[j % 4][:, :], ACT.Copy).then_inc(sem("ot_ev"), 1)

        @block.vector
        def _(dve):
            nc.vector.memset(silu_c[:, :, :], 0.0).then_inc(sem("zeros_ready"), 1)
            nc.vector.memset(small[:, :], 0.0).then_inc(sem("boot"), 1)
            dve.wait_ge(sem("boot"), 1)
            nc.vector.memset(small[:, 40:41], EPS).then_inc(sem("boot"), 1)
            nc.vector.memset(Vx[:, :, :, 128:129], 1.0).then_inc(sem("boot"), 1)
            nc.vector.memset(Mrow[:, :], 0.0).then_inc(sem("boot"), 1)
            dve.wait_ge(sem("const_in"), 16)
            dve.wait_ge(*reached("vec_mm", 1))
            nc.vector.tensor_copy(vec[:, :], PS[7][:, 0:NVEC]).then_inc(sem("vec_ready"), 1)
            for j in range(4):
                dve.wait_ge(*reached("cT_mm", j + 1))
                nc.vector.tensor_copy(ctxT[:, 2 * j:2 * j + 2, :], PS[4 + j][:, :].rearrange("p (k t) -> p k t", k=2)).then_inc(sem("cT_ev"), 1)

            def ada(s, part):
                dve.wait_ge(sem("ada_mm"), s + 1)
                nc.vector.tensor_copy(part[:, s % 2, :], PS[4 + s % 2][:, :]).then_inc(sem("ada_ev"), 1)

            def ada_bias(s):
                dve.wait_ge(sem("ada_t"), s + 1)
                for i in range(2):
                    nc.vector.tensor_tensor(mods[:, 4 * s:4 * s + 4, i], PS[6 + s % 2][:, 0:8].rearrange("p (c m) -> p c m", m=2)[:, :, i],
                                            v("b_ada", 4 * s, 4), ALU.add).then_inc(sem("mods"), 1)

            for s in range(4):
                ada(s, ada_part0)
                if s:
                    ada_bias(s - 1)
            ada_bias(3)
            dve.wait_ge(sem("mods"), 8)
            for i in range(2):
                nc.vector.scalar_tensor_tensor(out=gains[:, i, :], in0=mods[:, 8:16, i], scalar=1.0, in1=v("g_norm1", 0, KD),
                                               op0=ALU.add, op1=ALU.mult).then_inc(sem("gains1"), 1)
            dve.wait_ge(sem("gains1"), 2)
            nc.vector.memset(small[:, 41:42], 0.0).then_inc(sem("gains1"), 1)
            rms_scale(dve, "n1", lambda k: xT[:, k, :], lambda k: H[:, k, 0:T], T, std[:, 0:T], rstd[:, 0:T], lambda k: gains[:, 0, k:k + 1])
            rms_scale(dve, "nc", lambda k: ctxT[:, k, :], lambda k: H[:, k, T:T + TC], TC, std[:, T:T + TC], rstd[:, T:T + TC], lambda k: gains[:, 1, k:k + 1])

            def conv(name, j, bank, taps, width, height, tile, silu_free):
                a = acc[:, j % 2, 0:width * height].rearrange("p (r c) -> p r c", r=height)
                s = bank[:, 0:width * height].rearrange("p (r c) -> p r c", r=height)
                if silu_free:
                    dve.wait_ge(*silu_free)
                order = [(0, 0)] + [t for t in taps if t != (0, 0)]
                for i, (dy, dx) in enumerate(order):
                    w = v("conv2d", 8 * (3 * (dy + 1) + dx + 1) + tile)
                    r0, r1, c0, c1 = max(0, -dy), height - max(0, dy), max(0, -dx), width - max(0, dx)
                    if i == 0:
                        nc.vector.tensor_scalar(a, s, w, None, ALU.mult).then_inc(sem(name), 1)
                    else:
                        dve.wait_ge(sem(name), conv.done)
                        nc.vector.scalar_tensor_tensor(out=a[:, r0:r1, c0:c1], in0=s[:, r0 + dy:r1 + dy, c0 + dx:c1 + dx], scalar=w,
                                                       in1=a[:, r0:r1, c0:c1], op0=ALU.mult, op1=ALU.add).then_inc(sem(name), 1)
                    conv.done += 1

            taps3 = [(0, -1), (0, 0), (0, 1)]
            taps9 = [(dy, dx) for dy in (-1, 0, 1) for dx in (-1, 0, 1)]
            conv.done = 0
            for j in range(8):
                dve.wait_ge(*reached("k_mm", j + 1))
                if j < 4:
                    conv("conv_k", j, PS[j], taps3, TC, 1, 4 + j, reached("k_silu", j - 1) if j >= 2 else None)
                else:
                    conv("conv_k", j, PS[j - 4], taps9, GRID_W, ROWS, j, reached("k_silu", j - 1))
            nc.vector.memset(Vc[:, :, :, 128:129], 1.0).then_inc(sem("vc_ones"), 1)
            nc.vector.memset(tok_lf, 0.0).then_inc(sem("tok_zero"), 1)
            nc.vector.memset(tok_ig, 0.0).then_inc(sem("tok_zero"), 1)
            dve.wait_ge(sem("tok_zero"), 2)
            dve.wait_ge(*reached("gate_mm", 1))
            nc.vector.tensor_copy(gts, PS[0][:, 0:96].rearrange("p (t e c h) -> p t e c h", t=TA, e=2, c=2)).then_inc(sem("gate_v"), 1)
            dve.wait_ge(sem("gate_v"), 1)
            f_pre = gts[:, :, :, 1, :]
            nc.vector.tensor_scalar(minf, f_pre, 0.0, None, ALU.min).then_inc(sem("gate_v"), 1)
            nc.vector.tensor_copy(tok_ig[:, :, :, 0:4], gts[:, :, :, 0, :]).then_inc(sem("gate_v"), 1)
            dve.wait_ge(sem("gate_v"), 3)
            dve.wait_ge(sem("gate_s"), 3)
            nc.vector.tensor_tensor(tok_lf[:, :, :, 0:4], minf, lnp, ALU.subtract).then_inc(sem("gate_v"), 1)
            nc.vector.memset(cum_r, 0.0).then_inc(sem("rows_v"), 1)
            nc.vector.memset(zero_r, 0.0).then_inc(sem("rows_v"), 1)
            dve.wait_ge(*reached("rows_mm", 1))
            nc.vector.tensor_copy(lf_r[:, 0:T], PS[0][0:36, :]).then_inc(sem("rows_v"), 1)
            nc.vector.tensor_copy(lf_r[:, T:T + TC], PS[2][0:36, 0:256]).then_inc(sem("rows_v"), 1)
            nc.vector.tensor_copy(ig_r[:, T:T + TC], PS[2][0:36, 256:512]).then_inc(sem("ig_ctx"), 1)
            dve.wait_ge(sem("rows_v"), 4)
            dve.wait_ge(sem("ig_ctx"), 1)

            def scan(rows, view, src, n, c0, init, op0, second):
                a, b = src[rows, c0:c0 + n], second[rows, 0:n] if second is zero_r else second[rows, c0:c0 + n]
                o = view[rows, c0:c0 + n]
                if rows.start:
                    a, b, o = a[:, ::-1], b[:, ::-1], o[:, ::-1]
                return nc.vector.tensor_tensor_scan(o, a, b, init, op0, ALU.add if second is zero_r else op0)

            fwd, bwd = slice(0, 4), slice(32, 36)
            for rows in (fwd, bwd):
                for c0, n in ((0, T), (T, TC)):
                    scan(rows, cum_r, lf_r, n, c0, 0.0, ALU.add, zero_r).then_inc(sem("rows_v"), 1)
            dve.wait_ge(sem("rows_v"), 8)
            dve.wait_ge(sem("rows_s"), 1)
            nc.vector.tensor_tensor(a_r, ig_r, cum_r, ALU.subtract).then_inc(sem("rows_v"), 1)
            dve.wait_ge(sem("rows_v"), 9)
            nc.vector.reduce_max(mend, a_r[:, T:T + TC], AX_X).then_inc(sem("rows_v"), 1)
            dve.wait_ge(sem("rows_v"), 10)
            nc.vector.tensor_scalar(nmend, mend, 0.0, -1.0, ALU.max, ALU.mult).then_inc(sem("rows_v"), 1)
            dve.wait_ge(sem("rows_v"), 11)
            nc.vector.tensor_tensor(m0[0:4], cum_r[0:4, T + TC - 1:T + TC], nmend[0:4], ALU.subtract).then_inc(sem("rows_v"), 1)
            nc.vector.tensor_tensor(m0[32:36], cum_r[32:36, T:T + 1], nmend[32:36], ALU.subtract).then_inc(sem("rows_v"), 1)
            dve.wait_ge(sem("rows_v"), 13)
            for rows in (fwd, bwd):
                scan(rows, Mrow, a_r, T, 0, m0[rows], ALU.max, a_r).then_inc(sem("rows_v"), 1)
            dve.wait_ge(sem("rows_v"), 15)
            nc.vector.tensor_tensor(mm_r, cum_r[:, 0:T], Mrow[:, :], ALU.add).then_inc(sem("rows_v"), 1)
            conv.done = 0
            dve.wait_ge(*reached("k_silu", 8))
            for j in range(4):
                dve.wait_ge(*reached("q_mm", j + 1))
                conv("conv_q", j, PS[j], taps9, GRID_W, ROWS, j, reached("q_silu", j - 1) if j >= 2 else None)
            dve.wait_ge(*reached("tokg_mm", 1))
            nc.vector.tensor_copy(tokg[:, :], PS[3][:, 0:368]).then_inc(sem("tokg_ev"), 1)
            dve.wait_ge(sem("tokg_ev"), 1)
            for t in range(2):
                dve.wait_ge(*reached("kc_mm", t + 1))
                for e in range(2):
                    for h in range(NH):
                        nc.vector.tensor_scalar(kw[:, t, e, h, :], PS[t][:, 128 * h:128 * (h + 1)], wa_t[:, t, 32 * e + h:32 * e + h + 1],
                                                QK_SCALE, ALU.mult, ALU.mult).then_inc(sem("kw_ev"), 1)
            for s in range(4, 12):
                ada(s, ada_part)
                if s > 4:
                    ada_bias(s - 1)
            ada_bias(11)

            def gate_a(j):
                dve.wait_ge(sem("bra_ev"), j + 1)
                nc.vector.tensor_tensor(merged[:, j, :], merged[:, j, :], sig[:, j % 2, :], ALU.mult).then_inc(sem("bra_v"), 1)

            dve.wait_ge(*reached("yf_ev", 8))
            for h in range(NH):
                base = 23 * h
                for e in range(2):
                    dve.wait_ge(sem("dec_s"), 2 * h + e + 1)
                    nc.vector.tensor_tensor(qd[:, e, :], qd[:, e, :], qT[:, h, :], ALU.mult).then_inc(sem("attn_v"), 1)
                for t in range(TT):
                    b = base + 2 + 5 * t
                    if t or h:
                        dve.wait_ge(sem("E_diag"), 4 * h + t)
                    for e in range(2):
                        nc.vector.tensor_scalar(dg[:, e, :], mb[:, e, 128 * t:128 * (t + 1)], a_t[:, t, 32 * e + h:32 * e + h + 1], 0.0,
                                                ALU.subtract, ALU.max).then_inc(sem("attn_v"), 1)
                    dve.wait_ge(sem("E_diag"), 4 * h + t + 1)
                    nc.vector.tensor_tensor(EX[:, :, 128 * t:128 * (t + 1)], EX[:, :, 128 * t:128 * (t + 1)], masks2, ALU.mult).then_inc(sem("attn_v"), 1)
                    dve.wait_ge(sem("attn_v"), b + 3)
                    dve.wait_ge(sem("E_off"), 6 * h + (1, 3, 5, 6)[t])
                    dve.wait_ge(sem("S_mm"), 4 * h + t + 1)
                    if t == 0 and h:
                        dve.wait_ge(sem("pv_mm"), 4 * h)
                    nc.vector.scalar_tensor_tensor(out=PT[:, t, 0, 128 * t:T], in0=PS[2 + t % 2][:, 128 * t:T], scalar=QK_SCALE, in1=EX[:, 0, 128 * t:T],
                                                   op0=ALU.mult, op1=ALU.mult).then_inc(sem("attn_v"), 1)
                    nc.vector.scalar_tensor_tensor(out=PT[:, t, 1, 0:128 * (t + 1)], in0=PS[2 + t % 2][:, 0:128 * (t + 1)], scalar=QK_SCALE,
                                                   in1=EX[:, 1, 0:128 * (t + 1)], op0=ALU.mult, op1=ALU.mult).then_inc(sem("attn_v"), 1)
                    if t == 1:
                        gate_a(2 * h)
                    if t == 3:
                        gate_a(2 * h + 1)
                for t in range(TT):
                    o = PS[4][:, 0:258].rearrange("p (e d) -> p e d", e=2)
                    dve.wait_ge(sem("pv_mm"), 4 * h + t + 1)
                    g = 6 * (4 * h + t)
                    if t == 0 and h:
                        dve.wait_ge(sem("hmT_mm"), h)
                    nc.vector.tensor_scalar(den[:, t, :], o[:, :, 128], -1.0, None, ALU.mult).then_inc(sem("pv_v"), 1)
                    dve.wait_ge(sem("pv_v"), g + 1)
                    nc.vector.tensor_tensor(dn[:, t, :], den[:, t, :], enm_t[:, t, h::32], ALU.max).then_inc(sem("pv_v"), 1)
                    dve.wait_ge(sem("pv_v"), g + 2)
                    nc.vector.tensor_tensor(dn[:, t, :], dn[:, t, :], o[:, :, 128], ALU.max).then_inc(sem("pv_v"), 1)
                    dve.wait_ge(sem("pv_v"), g + 3)
                    nc.vector.reciprocal(rec[:, t, :], dn[:, t, :]).then_inc(sem("pv_v"), 1)
                    dve.wait_ge(sem("pv_v"), g + 4)
                    nc.vector.tensor_scalar(hm[:, t, :], o[:, 0, 0:128], rec[:, t, 0:1], None, ALU.mult).then_inc(sem("pv_v"), 1)
                    dve.wait_ge(sem("pv_v"), g + 5)
                    nc.vector.scalar_tensor_tensor(out=hm[:, t, :], in0=o[:, 1, 0:128], scalar=rec[:, t, 1:2], in1=hm[:, t, :],
                                                   op0=ALU.mult, op1=ALU.add).then_inc(sem("pv_v"), 1)
                dve.wait_ge(sem("hmT_mm"), h + 1)
                dve.wait_ge(*reached("o_ev", 4))
                nc.vector.tensor_tensor(qT[:, h, :], oT[:, h, :], PS[5][:, :], ALU.mult).then_inc(sem("attn_v"), 1)
            dve.wait_ge(sem("attn_v"), 23 * NH)
            for j in range(4):
                dve.wait_ge(*reached("mT_mm", j + 1))
                nc.vector.tensor_copy(memT[:, 2 * j:2 * j + 2, :], PS[j][:, :].rearrange("p (k t) -> p k t", k=2)).then_inc(sem("mT_ev"), 1)
            rms_scale(dve, "nm", lambda k: memT[:, k, :], lambda k: H[:, k, T:T + TC], TC, std[:, T:T + TC], rstd2[:, T:T + TC], lambda k: v("mem", k))
            for j in range(8):
                dve.wait_ge(*reached("brb_ev", j + 1))
                dve.wait_ge(*reached("ym_ev", j + 1))
                nc.vector.tensor_tensor(sig[:, j % 2, :], sig[:, j % 2, :], ymT[:, j, :], ALU.mult).then_inc(sem("brb_v"), 1)
                dve.wait_ge(sem("brb_v"), 2 * j + 1)
                nc.vector.tensor_tensor(merged[:, j, :], merged[:, j, :], sig[:, j % 2, :], ALU.add).then_inc(sem("brb_v"), 1)
            for j in range(8):
                dve.wait_ge(*reached("wo_mm", j + 1))
                nc.vector.scalar_tensor_tensor(out=xT[:, j, :], in0=PS[j % 4][:, :], scalar=mods[:, 16 + j, 0:1], in1=xT[:, j, :],
                                               op0=ALU.mult, op1=ALU.add).then_inc(sem("x1"), 1)
            nc.vector.scalar_tensor_tensor(out=gains[:, 2, :], in0=mods[:, 32:40, 0], scalar=1.0, in1=v("g_norm2", 0, KD),
                                           op0=ALU.add, op1=ALU.mult).then_inc(sem("gains2"), 1)
            dve.wait_ge(sem("gains2"), 1)
            rms_scale(dve, "n2", lambda k: xT[:, k, :], lambda k: H[:, k, 0:T], T, std[:, 0:T], rstd2[:, 0:T], lambda k: gains[:, 2, k:k + 1])
            nc.vector.memset(R1[:, 64:208], 0.0).then_inc(sem("r_zero"), 1)
            nc.vector.memset(zrow, 0.0).then_inc(sem("r_zero"), 1)
            nc.vector.memset(R7[:, 0:3584], 0.0).then_inc(sem("r_zero"), 1)
            dve.wait_ge(sem("r_zero"), 3)
            dve.wait_ge(*reached("logit_mm", 1))
            lg = PS[5][:, 0:64].rearrange("p (t e) -> p t e", t=TT)
            nc.vector.reduce_max(lmax, lg, AX_X).then_inc(sem("aff_v"), 1)
            dve.wait_ge(sem("aff_v"), 1)
            nc.vector.tensor_tensor(logit, lg, lmax.unsqueeze(2).broadcast_to([P, TT, NE]), ALU.subtract).then_inc(sem("aff_v"), 1)
            dve.wait_ge(sem("aff_s"), 1)
            nc.vector.reduce_sum(lsum, logit, AX_X).then_inc(sem("aff_v"), 1)
            dve.wait_ge(sem("aff_v"), 3)
            nc.vector.reciprocal(linv, lsum).then_inc(sem("aff_v"), 1)
            dve.wait_ge(sem("aff_v"), 4)
            nc.vector.tensor_tensor(aff[:, :, 0:NE], logit, linv.unsqueeze(2).broadcast_to([P, TT, NE]), ALU.mult).then_inc(sem("aff_v"), 1)
            dve.wait_ge(*reached("affT_mm", 1))
            nc.vector.tensor_copy(work, PS[6][0:NE, :]).then_inc(sem("top_v"), 1)
            for i in range(CAP // 8):
                dve.wait_ge(sem("top_v"), 2 * i + 1)
                nc.vector.max(top8, work).then_inc(sem("top_v"), 1)
                dve.wait_ge(sem("top_v"), 2 * i + 2)
                nc.vector.match_replace(work, top8, work, -1.0).then_inc(sem("top_v"), 1)
            n = 2 * (CAP // 8) + 1
            dve.wait_ge(sem("top_v"), n)
            nc.vector.tensor_scalar(taken, work, -1.0, None, ALU.is_equal).then_inc(sem("top_v"), 1)
            dve.wait_ge(sem("top_v"), n + 1)
            nc.vector.tensor_tensor_scan(work, taken, zrow, 0.0, ALU.add, ALU.add).then_inc(sem("top_v"), 1)
            dve.wait_ge(sem("top_v"), n + 2)
            nc.vector.tensor_tensor(taken, taken, work, ALU.mult).then_inc(sem("top_v"), 1)
            dve.wait_ge(*reached("slotT_mm", 1))
            nc.vector.tensor_copy(slot_t[:, :, 0:NE], PS[7][:, 0:64].rearrange("p (t e) -> p t e", t=TT)).then_inc(sem("slot_ready"), 1)
            dve.wait_ge(sem("slot_ready"), 1)

            def pick_slots(pair):
                nc.vector.tensor_tensor(selc, iota.unsqueeze(1).unsqueeze(1).broadcast_to([P, TT, 2, CAP]),
                                        slot_t[:, :, bass.ds(pair * 2, 2)].unsqueeze(3).broadcast_to([P, TT, 2, CAP]), ALU.is_equal).then_inc(sem("sel_v"), 1)

            def weigh_slots(pair):
                nc.vector.tensor_tensor(gc, selc, aff[:, :, bass.ds(pair * 2, 2)].unsqueeze(3).broadcast_to([P, TT, 2, CAP]), ALU.mult).then_inc(sem("gc_v"), 1)

            pick_slots(0)
            dve.wait_ge(sem("sel_v"), 1)
            weigh_slots(0)
            for name, times in (("hid_v", 2), ("sc_v", 8), ("y1_ev", 1), ("sg_s", 2), ("gt_ev", 1), ("y0_ev", 1)):
                for i in range(times):
                    dve.sem_inc(sem(name), 1)

            def scatter(j, mm):
                dve.wait_ge(sem("sc_mm"), mm)
                nc.vector.scalar_tensor_tensor(out=xT[:, j, :], in0=PS[2 + j % 2][:, :], scalar=mods[:, 40 + j, 0:1], in1=xT[:, j, :],
                                               op0=ALU.mult, op1=ALU.add).then_inc(sem("sc_v"), 1)

            with dve.Fori(0, NPAIR) as pair:
                dve.wait_ge(sem("gc_v"), pair + 1)
                dve.wait_ge(sem("gather_mm"), pair * 2 + 2)
                pick_slots(pair + 1)
                for e in range(2):
                    dve.wait_ge(sem("sg_s"), pair * 2 + (3 + e))
                    dve.wait_ge(sem("moe_mm"), pair * 6 + (2 * e + 2))
                    nc.vector.tensor_tensor(hid[:, e, :], sg[:, e, :], PS[2 * e + 1][:, :], ALU.mult).then_inc(sem("hid_v"), 1)
                for j in range(KD):
                    scatter(j, pair * 8 + (j + 1))
                dve.wait_ge(sem("gt_mm"), pair + 1)
                dve.wait_ge(sem("sel_v"), pair + 2)
                weigh_slots(pair + 1)
                dve.wait_ge(sem("moe_mm"), pair * 6 + 6)
                nc.vector.tensor_copy(ypair[:, 512:1024], PS[7][:, :]).then_inc(sem("y1_ev"), 1)
            for j in range(KD):
                scatter(j, 8 * NPAIR + j + 1)

            dve.wait_ge(sem("sc_v"), 8 * (NPAIR + 2))
            rms_scale(dve, "nf", lambda k: xT[:, k, :], lambda k: xT[:, k, :], T, std[:, 0:T], rstd2[:, 0:T], lambda k: v("g_final", k))
            rms_scale(dve, "n3", lambda k: xT[:, k, :], lambda k: H[:, k, 0:T], T, std[:, 0:T], rstd2[:, 0:T], lambda k: v("mix", k))
            nc.vector.memset(u_pad[:, :, 0:TAPS - 1], 0.0).then_inc(sem("u_v"), 1)
            for j in range(KH):
                dve.wait_ge(*reached("a_mm", j + 1))
                dve.wait_ge(*reached("glu_ev", j + 1))
                nc.vector.tensor_tensor(u_pad[:, j, TAPS - 1:], PS[4 + j][:, :], sgT[:, j, :], ALU.mult).then_inc(sem("u_v"), 1)
            dve.wait_ge(sem("u_v"), 5)
            for tap in range(TAPS):
                for k in range(KH):
                    if tap == 0:
                        nc.vector.tensor_scalar(cT[:, k, :], u_pad[:, k, 0:T], v("dw_w", k), v("dw_b", k), ALU.mult, ALU.add).then_inc(sem("dw_v"), 1)
                    else:
                        dve.wait_ge(sem("dw_v"), KH * (tap - 1) + k + 1)
                        nc.vector.scalar_tensor_tensor(out=cT[:, k, :], in0=u_pad[:, k, tap:tap + T], scalar=v("dw_w", KH * tap + k), in1=cT[:, k, :],
                                                       op0=ALU.mult, op1=ALU.add).then_inc(sem("dw_v"), 1)
            dve.wait_ge(*reached("f_mm", 1))
            nc.vector.tensor_copy(f_tok, PS[7][:, 0:32].rearrange("p (t h) -> p t h", t=TT)).then_inc(sem("f_v"), 1)
            dve.wait_ge(sem("f_v"), 1)
            nc.vector.memset(zero8, 0.0).then_inc(sem("f_v"), 1)
            dve.wait_ge(sem("f_s"), 3)
            nc.vector.tensor_scalar(f_tok, f_tok, 0.0, None, ALU.min).then_inc(sem("f_v"), 1)
            dve.wait_ge(sem("f_v"), 3)
            nc.vector.tensor_tensor(f_tok, f_tok, f_ln, ALU.subtract).then_inc(sem("f_v"), 1)
            dve.wait_ge(*reached("fT_mm", 1))
            nc.vector.tensor_copy(f_row, PS[6][0:FOX_H, :]).then_inc(sem("f_v"), 1)
            dve.wait_ge(sem("f_v"), 5)
            nc.vector.tensor_tensor_scan(c_row[0:FOX_H, :], f_row, zero8, 0.0, ALU.add, ALU.add).then_inc(sem("c_v"), 1)
            dve.wait_ge(*reached("lnm_mm", 1))
            for k in range(KH):
                nc.vector.scalar_tensor_tensor(out=cT[:, k, :], in0=PS[4][:, :], scalar=-1.0 / HALF, in1=cT[:, k, :], op0=ALU.mult, op1=ALU.add).then_inc(sem("ln_v"), 1)
            dve.wait_ge(sem("ln_std"), 1)
            nc.vector.reciprocal(rstd2[:, 0:T], std[:, 0:T]).then_inc(sem("ln_v"), 1)
            dve.wait_ge(sem("ln_v"), KH + 1)
            for k in range(KH):
                nc.vector.scalar_tensor_tensor(out=cT[:, k, :], in0=cT[:, k, :], scalar=v("ln_g", k), in1=rstd2[:, 0:T], op0=ALU.mult, op1=ALU.mult).then_inc(sem("ln_v"), 1)
            dve.wait_ge(*reached("c_ready", KH))

            def sum_recip(n):
                dve.wait_ge(sem("exp_s"), n + 1)
                nc.vector.reciprocal(prec[:, n:n + 1], psum_[:, n:n + 1]).then_inc(sem("prec_v"), 1)

            for hp in range(FOX_H // 2):
                for i in range(TT):
                    for e in range(2):
                        n = 8 * hp + 2 * i + e
                        w = 128 * (i + 1)
                        c = 1280 * e + 64 * i * (i + 1)
                        L = Pbuf[hp % 2][:, c:c + w]
                        dve.wait_ge(sem("S2_mm"), 4 * hp + i + 1)
                        dve.wait_ge(sem("cb_ev"), 2 * (hp + 1))
                        if i == 0 and e == 0 and hp >= 2:
                            dve.wait_ge(sem("PT_mm"), 8 * (hp - 1))
                        nc.vector.scalar_tensor_tensor(out=L, in0=PS[2 * (i % 2) + e][:, 0:w], scalar=FOX_SCALE, in1=cb[:, e, 0:w],
                                                       op0=ALU.mult, op1=ALU.subtract).then_inc(sem("L_v"), 1)
                        dve.wait_ge(sem("L_v"), 3 * n + 1)
                        nc.vector.tensor_tensor(L[:, 128 * i:w], L[:, 128 * i:w], const[:, 512:640], ALU.add).then_inc(sem("L_v"), 1)
                        dve.wait_ge(sem("L_v"), 3 * n + 2)
                        nc.vector.tensor_reduce(nmax[:, n:n + 1], L, AX_X, ALU.max, negate=True).then_inc(sem("L_v"), 1)
                        if n:
                            sum_recip(n - 1)
            sum_recip(FOX_H * TT - 1)
            for j in range(8):
                dve.wait_ge(*reached("pw_mm", j + 1))
                dve.wait_ge(sem("gc_ev"), 8)
                nc.vector.tensor_tensor(merged[:, j, :], merged[:, j, :], PS[j % 4][:, :], ALU.mult).then_inc(sem("pw_v"), 1)
            for j in range(8):
                dve.wait_ge(*reached("ab_mm", j + 1))
                dve.wait_ge(*reached("ga_ev", 8))
                if j >= 2:
                    dve.wait_ge(sem("ab_v"), 2 * (j - 1))
                else:
                    dve.wait_ge(sem("P_ready"), FOX_H * TT)
                nc.vector.tensor_tensor(tmp2[:, j % 2, :], sigA[:, j, :], PS[j % 4][:, :], ALU.mult).then_inc(sem("ab_v"), 1)
                dve.wait_ge(sem("ab_v"), 2 * j + 1)
                dve.wait_ge(sem("pw_v"), 8)
                nc.vector.tensor_tensor(merged[:, j, :], merged[:, j, :], tmp2[:, j % 2, :], ALU.add).then_inc(sem("ab_v"), 1)

            def residual(name, mm, j, mm_value):
                dve.wait_ge(*reached(mm, mm_value))
                nc.vector.tensor_tensor(xT[:, j, :], xT[:, j, :], PS[j % 4][:, :], ALU.add).then_inc(sem(name), 1)

            for j in range(KD):
                residual("x3", "w2o_mm", j, j + 1)
            dve.wait_ge(sem("x3"), KD)
            rms_scale(dve, "n4", lambda k: xT[:, k, :], lambda k: H[:, k, 0:T], T, std[:, 0:T], rstd2[:, 0:T], lambda k: v("xa", k))
            for h in range(4):
                for i in range(2):
                    dve.wait_ge(*reached("xS_mm", 2 * h + i + 1))
                    nc.vector.tensor_reduce(xmax[:, h, 2 * i:2 * i + 2], PS[2 * h % 8 + i][:, :].rearrange("p (i m) -> p i m", i=2), AX_X, ALU.max,
                                            negate=True).then_inc(sem("xmx"), 1)
                dve.wait_ge(sem("xmx"), 2 * h + 2)
                nc.vector.tensor_scalar(xmax[:, h, :], xmax[:, h, :], QK_SCALE, None, ALU.mult).then_inc(sem("xmax_v"), 1)
                nc.vector.memset(small[:, 50 + h:51 + h], 0.0).then_inc(sem("xmax_v"), 1)
            dve.wait_ge(sem("xexp_s"), 16)
            nc.vector.reciprocal(xrec, xsum).then_inc(sem("xrec_v"), 1)
            for h in range(4):
                dve.wait_ge(sem("xo_pv"), h + 1)
                nc.vector.tensor_copy(k2[:, h, :], PS[4 + h % 4][:, :]).then_inc(sem("ox_ev"), 1)
            for j in range(KD):
                residual("x4", "xo_mm", j, j + 1)
            dve.wait_ge(sem("x4"), KD)
            rms_scale(dve, "n5", lambda k: xT[:, k, :], lambda k: H[:, k, 0:T], T, std[:, 0:T], rstd2[:, 0:T], lambda k: v("moe", k))
            chain = [0]

            def step(ins):
                chain[0] += 1
                ins.then_inc(sem("g_v"), 1)
                dve.wait_ge(sem("g_v"), chain[0])

            def tt(o, a, b, op):
                step(nc.vector.tensor_tensor(o, a, b, op))

            def last4(a):
                return a.unsqueeze(2).broadcast_to([P, TT, 4])

            def first_of(dst, x, top, run):
                tt(run, x, last4(top), ALU.is_equal)
                for i in range(1, 4):
                    tt(run[:, :, i], run[:, :, i], run[:, :, i - 1], ALU.max)
                step(nc.vector.tensor_copy(dst[:, :, 0], run[:, :, 0]))
                tt(dst[:, :, 1:4], run[:, :, 1:4], run[:, :, 0:3], ALU.subtract)

            dve.wait_ge(*reached("rl_mm", 1))
            step(nc.vector.tensor_copy(rt["log"], PS[5][:, 0:80].rearrange("p (t n) -> p t n", t=TT)))
            gl = rt["log"][:, :, 0:4]
            el = rt["log"][:, :, 4:20].rearrange("p t (g j) -> p t g j", g=NG)
            step(nc.vector.reduce_max(rt["gmax"], gl, AX_X))
            tt(rt["gexp"], gl, last4(rt["gmax"]), ALU.subtract)
            first_of(rt["gsel"], gl, rt["gmax"], rt["run"])
            tt(rt["mix"], el, rt["gsel"].unsqueeze(3).broadcast_to([P, TT, 4, 4]), ALU.mult)
            step(nc.vector.reduce_sum(rt["esel"], rt["mix"].rearrange("p t g j -> p t j g"), AX_X))
            step(nc.vector.reduce_max(rt["emax"], rt["esel"], AX_X))
            tt(rt["p"], rt["esel"], last4(rt["emax"]), ALU.subtract)
            dve.wait_ge(sem("g_s"), 1)
            step(nc.vector.reduce_sum(rt["gsum"], rt["gexp"], AX_X))
            step(nc.vector.reciprocal(rt["pg"], rt["gsum"]))
            dve.wait_ge(sem("g_s"), 2)
            step(nc.vector.reduce_max(rt["emax"], rt["p"], AX_X))
            first_of(rt["m1"], rt["p"], rt["emax"], rt["run"])
            tt(rt["p2"], rt["p"], rt["m1"], ALU.mult)
            tt(rt["p2"], rt["p"], rt["p2"], ALU.subtract)
            tt(rt["p2"], rt["p2"], rt["m1"], ALU.subtract)
            step(nc.vector.reduce_max(rt["emax"], rt["p2"], AX_X))
            first_of(rt["m2"], rt["p2"], rt["emax"], rt["run"])
            tt(rt["m1"], rt["m1"], rt["m2"], ALU.add)
            tt(rt["p"], rt["p"], rt["m1"], ALU.mult)
            step(nc.vector.reduce_sum(rt["emax"], rt["p"], AX_X))
            step(nc.vector.reciprocal(rt["emax"], rt["emax"]))
            tt(rt["emax"], rt["emax"], rt["pg"], ALU.mult)
            tt(rt["p"], rt["p"], last4(rt["emax"]), ALU.mult)
            tt(rt["comb"], rt["gsel"].unsqueeze(3).broadcast_to([P, TT, 4, 4]), rt["p"].unsqueeze(2).broadcast_to([P, TT, 4, 4]), ALU.mult)
            dve.sem_inc(sem("comb_ready"), 1)
            dve.wait_ge(*reached("combT_mm", 1))
            nc.vector.tensor_scalar(chosen, PS[6][0:E2, :], 0.0, None, ALU.is_gt).then_inc(sem("chosen"), 1)
            dve.wait_ge(sem("chosen"), 1)
            step(nc.vector.memset(zero16, 0.0))
            step(nc.vector.tensor_tensor_scan(place, chosen, zero16, 0.0, ALU.add, ALU.add))
            step(nc.vector.tensor_scalar(thresh, iota[0:E2, 0:T // BLK], -1.0, float(BLK), ALU.add, ALU.mult))
            step(nc.vector.tensor_tensor(over, thresh, place[:, T - 1:T].broadcast_to([E2, T // BLK]), ALU.is_lt))
            nc.vector.reduce_sum(nblk, over, AX_X).then_inc(sem("block_counts"), 1)
            dve.wait_ge(*reached("ends_mm", 1))
            nc.vector.tensor_copy(ends, PS[7][0:E2, 0:1]).then_inc(sem("ends_v"), 1)
            dve.wait_ge(sem("ends_v"), 1)
            nc.vector.tensor_scalar(ended, iota[0:E2, 0:32], ends, None, ALU.is_gt).then_inc(sem("ended"), 1)
            step(nc.vector.tensor_tensor(blk_base, ends, nblk, ALU.subtract))
            step(nc.vector.tensor_scalar(blk_base, blk_base, float(BLK), None, ALU.mult))
            nc.vector.scalar_tensor_tensor(out=place, in0=place, scalar=blk_base, in1=chosen, op0=ALU.add, op1=ALU.mult).then_inc(sem("places"), 1)
            dve.wait_ge(*reached("which_mm", 1))
            nc.vector.tensor_scalar(block_expert[:, :], PS[6][0:1, 0:32], float(E2 - 1), None, ALU.min).then_inc(sem("block_expert"), 1)
            step(nc.vector.tensor_copy(iota2[:, 0:BLK], iota))
            step(nc.vector.tensor_scalar(iota2[:, BLK:2 * BLK], iota, float(BLK), None, ALU.add))
            dve.wait_ge(*reached("posT_mm", 1))
            nc.vector.tensor_copy(pos_t, PS[5][:, 0:TT * E2].rearrange("p (t e) -> p t e", t=TT)).then_inc(sem("pos_v"), 1)
            dve.wait_ge(sem("pos_v"), 1)
            comb = rt["comb"].rearrange("p t g j -> p t (g j)")
            step(nc.vector.reduce_max(pos2[:, 0, :], pos_t, AX_X))
            step(nc.vector.reduce_sum(pos2[:, 1, :], pos_t, AX_X))
            tt(pos2[:, 1, :], pos2[:, 1, :], pos2[:, 0, :], ALU.subtract)
            for a in range(2):
                tt(hit_t, pos_t, pos2[:, a, :].unsqueeze(2).broadcast_to([P, TT, E2]), ALU.is_equal)
                tt(hit_t, hit_t, comb, ALU.mult)
                step(nc.vector.reduce_sum(wt2[:, a, :], hit_t, AX_X))
            step(nc.vector.memset(R7[:, 1024:2560], 0.0))

            def by_slot(a):
                return a.unsqueeze(2).broadcast_to([P, TT, 2 * BLK])

            def pick_blocks(n):
                for a in range(2):
                    nc.vector.tensor_tensor(hits[a], iota2.unsqueeze(1).broadcast_to([P, TT, 2 * BLK]), by_slot(pos2[:, a, :]), ALU.is_equal).then_inc(sem("b_v"), 1)
                dve.wait_ge(sem("b_v"), n + 2)
                nc.vector.tensor_tensor(selb, hits[0], hits[1], ALU.add).then_inc(sem("b_sel"), 1)

            def weigh_blocks(n, done):
                dve.wait_ge(sem("b_sel"), done)
                for a in range(2):
                    nc.vector.tensor_tensor(hits[a], hits[a], by_slot(wt2[:, a, :]), ALU.mult).then_inc(sem("b_v"), 1)
                dve.wait_ge(sem("b_v"), n + 2)
                nc.vector.tensor_tensor(gb, hits[0], hits[1], ALU.add).then_inc(sem("b_gates"), 1)

            dve.sem_inc(sem("b_v"), 1)
            pick_blocks(1)
            weigh_blocks(3, 1)
            for name, times in (("b_hid", 1), ("x5", 8), ("b_y1", 1), ("b_GT", 1), ("b_y0", 1)):
                for i in range(times):
                    dve.sem_inc(sem(name), 1)

            def add_out(j, mm):
                dve.wait_ge(sem("b_scatter"), mm)
                nc.vector.tensor_tensor(xT[:, j, :], xT[:, j, :], PS[3 + j % 2][:, :], ALU.add).then_inc(sem("x5"), 1)

            with dve.Fori(0, NPAIR2) as pair:
                dve.wait_ge(sem("b_gates"), pair + 1)
                nc.vector.tensor_scalar(pos2, pos2, -2.0 * BLK, None, ALU.add).then_inc(sem("b_v"), 1)
                dve.wait_ge(sem("b_v"), pair * 5 + 6)
                dve.wait_ge(sem("b_gather"), pair * 2 + 2)
                pick_blocks(pair * 5 + 6)
                dve.wait_ge(sem("b_silu"), pair + 1)
                nc.vector.tensor_tensor(hb, sgb, PS[2][:, FF:2 * FF], ALU.mult).then_inc(sem("b_hid"), 1)
                for j in range(KD):
                    add_out(j, pair * 8 + (j + 1))
                dve.wait_ge(sem("b_turn_g"), pair + 1)
                weigh_blocks(pair * 5 + 8, pair + 2)
                dve.wait_ge(sem("b_down"), pair * 2 + 2)
                nc.vector.tensor_copy(yb[:, 512:1024], PS[7][:, :]).then_inc(sem("b_y1"), 1)
            for j in range(KD):
                add_out(j, 8 * NPAIR2 + j + 1)
            dve.wait_ge(sem("x5"), 8 * (NPAIR2 + 2))
            rms_scale(dve, "n6", lambda k: xT[:, k, :], lambda k: H[:, k, 0:T], T, std[:, 0:T], rstd2[:, 0:T], lambda k: v("final2", k))

        @block.tensor
        def _(pe):
            freed = {}

            def take(bank, s, value):
                if bank in freed:
                    pe.wait_ge(*freed[bank])
                freed[bank] = reached(s, value)
                return PS[bank]

            def product(dst, pairs):
                for i, (lhsT, rhs) in enumerate(pairs):
                    ins = nc.tensor.matmul(dst, lhsT, rhs, start=(i == 0), stop=(i == len(pairs) - 1))
                return ins

            pe.wait_ge(sem("const_in"), 16)
            pe.wait_ge(sem("vecs_in"), 16 * 16)
            b = take(7, "vec_ready", 1)
            for i, (n, c) in enumerate(((128, 0), (84, 128), (124, 212))):
                ins = nc.tensor.transpose(b[:, c:c + n], vpack[0:n, i, :], ident[0:n, 0:n])
            ins.then_inc(sem("vec_mm"), 1)
            pe.wait_ge(sem("x_in"), 16)
            for k in range(KD):
                b = take(k % 4, "xT_ev", k + 1)
                for t in range(TT):
                    ins = nc.tensor.transpose(b[:, 128 * t:128 * (t + 1)], x_tok[:, t, 128 * k:128 * (k + 1)], ident)
                ins.then_inc(sem("xT_mm"), 1)
            pe.wait_ge(sem("ctx_in"), 16)
            for j in range(4):
                b = take(4 + j, "cT_ev", j + 1)
                for i in range(4):
                    k, t = 2 * j + i // 2, i % 2
                    ins = nc.tensor.transpose(b[:, 128 * i:128 * (i + 1)], c_tok[:, t, 128 * k:128 * (k + 1)], ident)
                ins.then_inc(sem("cT_mm"), 1)
            rms_sum(pe, "n1", take(0, "rms_std", NORMS["n1"] + 1), sq, T)
            rms_sum(pe, "nc", take(1, "rms_std", NORMS["nc"] + 1), sqc, TC)

            def ada(s):
                w = weights(f"ada{s}", KD)
                wait_weights(pe, f"ada{s}")
                b = take(4 + s % 2, "ada_ev", s + 1)
                for k in range(KD):
                    g = k % 4
                    ins = nc.tensor.matmul(b[32 * g:32 * g + 32, :], silu_c[:, k, :], w[:, k, :], start=(k < 4), stop=(k >= 4),
                                           tile_position=(0, 32 * g))
                ins.then_inc(sem("ada_mm"), 1)

            def ada_sum(s, part):
                pe.wait_ge(sem("ada_ev"), s + 1)
                b = take(6 + s % 2, "mods", 2 * (s + 1))
                for c in range(4):
                    ins = nc.tensor.matmul(b[:, 2 * c:2 * c + 2], part[:, s % 2, 128 * c:128 * (c + 1)], pick, start=True, stop=True)
                ins.then_inc(sem("ada_t"), 1)

            pe.wait_ge(sem("silu_c"), 2)
            for s in range(4):
                ada(s)
                if s:
                    ada_sum(s - 1, ada_part0)
            ada_sum(3, ada_part0)
            pe.wait_ge(sem("h_ready"), 2 * KD)
            w = weights("k", KD)
            wait_weights(pe, "k")
            for j in range(8):
                b = take(j % 4, "conv_k", 3 * (j + 1) if j < 4 else 12 + 9 * (j - 3))
                c = 128 * (j % 4)
                toks = slice(T, T + TC) if j < 4 else slice(0, T)
                n = TC if j < 4 else T
                product(b[:, 0:n], [(w[:, k, c:c + 128], H[:, k, toks]) for k in range(KD)]).then_inc(sem("k_mm"), 1)
            w = weights("v", KD)
            wait_weights(pe, "v")
            for t in range(TA):
                b = take(4 + t % 4, "v_ev", t + 1)
                product(b[:, :], [(H[:, k, 128 * t:128 * (t + 1)], w[:, k, :]) for k in range(KD)]).then_inc(sem("v_mm"), 1)
            pe.wait_ge(sem("wsmall_in"), 80)
            pe.wait_ge(sem("rowb_in"), 64)
            b = take(0, "gate_v", 1)
            for t in range(TA):
                ins = product(b[:, 16 * t:16 * (t + 1)], [(ones[0:1, :], rowb[0:1, 0:16])] +
                              [(H[:, k, 128 * t:128 * (t + 1)], wsmall[:, k, 0:16]) for k in range(KD)])
            ins.then_inc(sem("gate_mm"), 1)
            w = weights("u", KD)
            wait_weights(pe, "u")
            for j in range(4):
                b = take(4 + j, "u_ev", j + 1)
                product(b[:, :], [(w[:, k, 128 * j:128 * (j + 1)], H[:, k, 0:T]) for k in range(KD)]).then_inc(sem("u_mm"), 1)
            pe.wait_ge(sem("gate_v"), 4)
            b0, b1, b2 = take(0, "rows_v", 4), take(1, "rows_s", 1), take(2, "ig_ctx", 1)
            for t in range(TA):
                lf_dst = b0[0:36, 128 * t:128 * (t + 1)] if t < TT else b2[0:36, 128 * (t - TT):128 * (t - TT + 1)]
                ig_dst = b1[0:36, 128 * t:128 * (t + 1)] if t < TT else b2[0:36, 256 + 128 * (t - TT):256 + 128 * (t - TT + 1)]
                nc.tensor.transpose(lf_dst, tok_lf2[:, t, 0:36], ident)
                ins = nc.tensor.transpose(ig_dst, tok_ig2[:, t, 0:36], ident)
            ins.then_inc(sem("rows_mm"), 1)
            pe.wait_ge(sem("rows_v"), 4)
            w = weights("q", KD)
            wait_weights(pe, "q")
            for j in range(4):
                b = take(j, "conv_q", 9 * (j + 1))
                product(b[:, :], [(w[:, k, 128 * j:128 * (j + 1)], H[:, k, 0:T]) for k in range(KD)]).then_inc(sem("q_mm"), 1)
            w = weights("o", KD)
            wait_weights(pe, "o")
            for j in range(4):
                b = take(j, "o_ev", j + 1)
                product(b[:, :], [(w[:, k, 128 * j:128 * (j + 1)], H[:, k, 0:T]) for k in range(KD)]).then_inc(sem("o_mm"), 1)
            pe.wait_ge(sem("rows_s"), 3)
            pe.wait_ge(sem("rows_v"), 16)
            b = take(3, "tokg_ev", 1)
            for i, (src, tiles) in enumerate(((a_r, 4), (mm_r, 4), (wa_r, 2))):
                for t in range(tiles):
                    c = 144 * i + 36 * t
                    nc.tensor.transpose(b[:, c:c + 36], src[:, 128 * t:128 * (t + 1)], ident[0:36, 0:36])
            for r in range(8):
                row = 32 * (r // 4) + r % 4
                ins = nc.tensor.matmul(b[:, 360 + r:361 + r], ident[0:36, row:row + 1].broadcast_to([36, 128]), m0, start=True, stop=True)
            ins.then_inc(sem("tokg_mm"), 1)
            pe.wait_ge(*reached("k_silu", 8))
            for t in range(2):
                b = take(t, "kw_ev", 8 * (t + 1))
                for h in range(NH):
                    ins = nc.tensor.transpose(b[:, 128 * h:128 * (h + 1)], kcT[:, h, 128 * t:128 * (t + 1)], ident)
                ins.then_inc(sem("kc_mm"), 1)
            pe.wait_ge(sem("kw_ev"), 16)
            pe.wait_ge(sem("vc_ones"), 1)
            for h in range(NH):
                b = take(2 + h % 2, "C0_ev", h + 1)
                for e in range(2):
                    ins = product(b[:, 129 * e:129 * (e + 1)], [(kw[:, t, e, h, :], Vc[:, t, h, :]) for t in range(2)])
                ins.then_inc(sem("C0_mm"), 1)
            for s in range(4, 12):
                ada(s)
                if s > 4:
                    ada_sum(s - 1, ada_part)
            ada_sum(11, ada_part)
            pe.wait_ge(*reached("u_ev", 4))
            for j in range(8):
                b = take(4 + j % 4, "Z_ev", j + 1)
                for i in range(2):
                    g = 2 * (j % 2) + i
                    ins = nc.tensor.matmul(b[:, 256 * i:256 * (i + 1)], uT[:, g, 128 * (j // 2):128 * (j // 2) + 128], dftF, start=True, stop=True)
                ins.then_inc(sem("Z_mm"), 1)
            w = weights("dft", TT)
            wait_weights(pe, "dft")
            pe.wait_ge(*reached("Z_ev", 8))
            for g in range(4):
                b = take(g, "fu_ev", g + 1)
                product(b[:, :], [(Z[:, t, g, 128 * s:128 * (s + 1)], w[:, t, 512 * s:512 * (s + 1)]) for t in range(TT) for s in range(2)]).then_inc(sem("fu_mm"), 1)
            w = weights("w_fourier", KH)
            wait_weights(pe, "w_fourier")
            pe.wait_ge(*reached("fu_ev", 4))
            for j in range(8):
                b = take(4 + j % 4, "yf_ev", j + 1)
                product(b[:, :], [(w[:, k, 128 * j:128 * (j + 1)], fuT[:, k, :]) for k in range(KH)]).then_inc(sem("yf_mm"), 1)

            def gate_a(j):
                name = f"brA{j // 4}"
                if j % 4 == 0:
                    wait_weights(pe, name)
                w = weights(name, KD)
                b = take(6 + j % 2, "bra_ev", j + 1)
                c = 128 * (j % 4)
                product(b[:, :], [(w[:, k, c:c + 128], H[:, k, 0:T]) for k in range(KD)]).then_inc(sem("bra_mm"), 1)

            pe.wait_ge(*reached("q_silu", 4))
            pe.wait_ge(*reached("C0_ev", 4))
            for h in range(NH):
                for e in range(2):
                    b = take(e, "mb_ev", 2 * h + e + 1)
                    r = 32 * e + h
                    nc.tensor.matmul(b[:, :], ident[0:36, r:r + 1].broadcast_to([36, 128]), Mrow[:, :], start=True, stop=True).then_inc(sem("mb_mm"), 1)
                for t in range(TT):
                    b = take(2 + t % 2, "attn_v", 23 * h + 2 + 5 * (t + 1))
                    nc.tensor.matmul(b[:, :], kT[:, h, 128 * t:128 * (t + 1)], qT[:, h, :], start=True, stop=True).then_inc(sem("S_mm"), 1)
                    if t == 1:
                        gate_a(2 * h)
                    if t == 3:
                        gate_a(2 * h + 1)
                pe.wait_ge(sem("attn_v"), 23 * h + 22)
                for j in range(TT):
                    b = take(4, "pv_v", 6 * (4 * h + j + 1))
                    jt = slice(128 * j, 128 * (j + 1))
                    for e in range(2):
                        keys = range(j + 1) if e == 0 else range(j, TT)
                        ins = product(b[:, 129 * e:129 * (e + 1)], [(qd[:, e, jt], C0[:, e, h, :])] +
                                      [(PT[:, t, e, jt], Vx[:, t, h, :]) for t in keys])
                    ins.then_inc(sem("pv_mm"), 1)
                b = take(5, "attn_v", 23 * h + 23)
                pe.wait_ge(sem("pv_v"), 24 * (h + 1))
                for t in range(TT):
                    ins = nc.tensor.transpose(b[:, 128 * t:128 * (t + 1)], hm[:, t, :], ident)
                ins.then_inc(sem("hmT_mm"), 1)
            pe.wait_ge(sem("mem_in"), 16)
            for j in range(4):
                b = take(j, "mT_ev", j + 1)
                for i in range(4):
                    k, t = 2 * j + i // 2, i % 2
                    ins = nc.tensor.transpose(b[:, 128 * i:128 * (i + 1)], m_tok[:, t, 128 * k:128 * (k + 1)], ident)
                ins.then_inc(sem("mT_mm"), 1)
            rms_sum(pe, "nm", take(5, "rms_std", NORMS["nm"] + 1), sqc, TC)
            w = weights("w_mlstm", KH)
            wait_weights(pe, "w_mlstm")
            pe.wait_ge(sem("attn_v"), 23 * 4)
            for j in range(8):
                b = take(j % 4, "ym_ev", j + 1)
                product(b[:, :], [(w[:, k, 128 * j:128 * (j + 1)], qT[:, k, :]) for k in range(KH)]).then_inc(sem("ym_mm"), 1)
            for j in range(8):
                name = f"brB{j // 4}"
                if j % 4 == 0:
                    wait_weights(pe, name)
                w = weights(name, KD)
                b = take(4 + j % 4, "brb_ev", j + 1)
                c = 128 * (j % 4)
                product(b[:, :], [(w[:, k, c:c + 128], H[:, k, 0:T]) for k in range(KD)]).then_inc(sem("brb_mm"), 1)
            pe.wait_ge(sem("brb_v"), 16)
            for j in range(8):
                name = f"wo{j // 4}"
                if j % 4 == 0:
                    wait_weights(pe, name)
                w = weights(name, KD)
                b = take(j % 4, "x1", j + 1)
                c = 128 * (j % 4)
                product(b[:, :], [(w[:, k, c:c + 128], merged[:, k, :]) for k in range(KD)]).then_inc(sem("wo_mm"), 1)

            rms_sum(pe, "n2", take(4, "rms_std", NORMS["n2"] + 1), sq, T)
            pe.wait_ge(sem("h2_ready"), KD)
            b = take(5, "aff_v", 2)
            for t in range(TT):
                ins = product(b[:, 16 * t:16 * (t + 1)], [(H[:, k, 128 * t:128 * (t + 1)], wsmall[:, k, 16:32]) for k in range(KD)])
            ins.then_inc(sem("logit_mm"), 1)
            for j in range(8):
                b = take(j % 4, "htok_ev", j + 1)
                for i in range(4):
                    k, t = 4 * (j % 2) + i, j // 2
                    ins = nc.tensor.transpose(b[:, 128 * i:128 * (i + 1)], H[:, k, 128 * t:128 * (t + 1)], ident)
                ins.then_inc(sem("htok_mm"), 1)
            pe.wait_ge(sem("aff_v"), 5)
            b = take(6, "top_v", 1)
            for t in range(TT):
                ins = nc.tensor.transpose(b[0:NE, 128 * t:128 * (t + 1)], aff[:, t, 0:NE], ident)
            ins.then_inc(sem("affT_mm"), 1)
            w = weights("xa_wk", KD)
            wait_weights(pe, "xa_wk")
            for j in range(4):
                b = take(j, "km_ev", j + 1)
                product(b[:, 0:TC], [(w[:, k, 128 * j:128 * (j + 1)], H[:, k, T:T + TC]) for k in range(KD)]).then_inc(sem("km_mm"), 1)
            w = weights("xa_wv", KD)
            wait_weights(pe, "xa_wv")
            for j in range(2):
                b = take(6 + j, "vm_ev", j + 1)
                product(b[:, :], [(H[:, k, T + 128 * j:T + 128 * (j + 1)], w[:, k, :]) for k in range(KD)]).then_inc(sem("vm_mm"), 1)
            pe.wait_ge(sem("top_v"), 2 * (CAP // 8) + 4)
            b = take(7, "slot_ready", 1)
            for t in range(TT):
                ins = nc.tensor.transpose(b[:, 16 * t:16 * (t + 1)], taken[:, 128 * t:128 * (t + 1)], ident[0:NE, 0:NE])
            ins.then_inc(sem("slotT_mm"), 1)
            for name, value in (("km_ev", 4), ("vm_ev", 2), ("slot_ready", 1), ("rms_std", NORMS["n2"] + 1), ("htok_ev", 8)):
                pe.wait_ge(*reached(name, value))

            def gather(sel):
                pe.wait_ge(sem("sel_v"), sel)
                for i in range(2):
                    for k in range(4 * i, 4 * i + 4):
                        c = 128 * (k - 4 * i)
                        ins = product(PS[i][:, c:c + 128], [(h_tok[:, t, 128 * k:128 * (k + 1)], selc[:, t, :, :]) for t in range(TT)])
                    ins.then_inc(sem("gather_mm"), 1)

            def scatter(done):
                for j in range(KD):
                    if j >= 2:
                        pe.wait_ge(sem("sc_v"), done(j))
                    nc.tensor.matmul(PS[2 + j % 2][:, :], ypair[:, 128 * j:128 * (j + 1)], GT, start=True, stop=True).then_inc(sem("sc_mm"), 1)

            n0 = len(W)

            def expert_weights(pair, i):
                s = (n0 + i) % NSLOT
                pe.wait_ge(arrived[s], pair * (16 * 12 // NSLOT) + 16 * ((n0 + i) // NSLOT + 1))
                return ring[:, s, :].rearrange("p (k n) -> p k n", k=KD)

            gather(1)
            with pe.Fori(0, NPAIR) as pair:
                pe.wait_ge(sem("xs_ev"), pair * 2 + 2)
                for e in range(2):
                    for i in range(2):
                        if e == 1:
                            pe.wait_ge(sem("sc_v"), pair * 8 + 8)
                        b = PS[2 * e + i]
                        w2 = [expert_weights(pair, 4 * e + 2 * i + half) for half in range(2)]
                        for k in range(KD):
                            for half in range(2):
                                ins = nc.tensor.matmul(b[64 * half:64 * half + 64, :], xs[:, k, 64 * e:64 * e + 64], w2[half][:, k, :],
                                                       start=(k == 0), stop=(k == KD - 1), tile_position=(0, 64 * half))
                        ins.then_inc(sem("moe_mm"), 1)

                def turn(e):
                    pe.wait_ge(sem("hid_v"), pair * 2 + (3 + e))
                    for i in range(4):
                        ins = nc.tensor.transpose(PS[4 + e][:, 128 * i:128 * (i + 1)], hid[:, e, 128 * i:128 * (i + 1)], ident)
                    ins.then_inc(sem("tr_mm"), 1)

                pe.wait_ge(sem("gt_ev"), pair + 1)
                turn(0)
                gather(pair + 2)
                turn(1)
                pe.wait_ge(sem("y0_ev"), pair + 1)
                pe.wait_ge(sem("y1_ev"), pair + 1)
                scatter(lambda j: pair * 8 + (7 + j))
                pe.wait_ge(sem("hidT_ev"), pair * 2 + 2)
                pe.wait_ge(sem("gc_v"), pair + 1)
                for t in range(TT):
                    ins = nc.tensor.transpose(PS[4][:, 128 * t:128 * (t + 1)], gc[:, t, :, :], ident)
                ins.then_inc(sem("gt_mm"), 1)
                for half in range(2):
                    w2 = [expert_weights(pair, 8 + 2 * half + e) for e in range(2)]
                    for k in range(KD):
                        for e in range(2):
                            ins = nc.tensor.matmul(PS[6 + half][64 * e:64 * e + 64, :], hidT[:, e, k % 4, 64 * (k // 4):64 * (k // 4) + 64],
                                                   w2[e][:, k, :], start=(k == 0), stop=(k == KD - 1), tile_position=(0, 64 * e))
                    ins.then_inc(sem("moe_mm"), 1)
            pe.wait_ge(sem("gt_ev"), NPAIR + 1)
            pe.wait_ge(sem("y0_ev"), NPAIR + 1)
            pe.wait_ge(sem("y1_ev"), NPAIR + 1)
            pe.wait_ge(sem("sc_v"), 8 * (NPAIR + 1))
            pe.wait_ge(sem("xs_ev"), 2 * (NPAIR + 1))
            scatter(lambda j: 8 * NPAIR + 7 + j)

            def project(name, dst_bank, evac, tiles=4, k=KD, act_in=None, j0=0, mm=None):
                w = weights(name, k)
                wait_weights(pe, name)
                for j in range(tiles):
                    b = take(dst_bank(j + j0), evac(j + j0)[0], evac(j + j0)[1])
                    product(b[:, :], [(w[:, i, 128 * j:128 * (j + 1)], act_in(i)) for i in range(k)]).then_inc(sem(mm), 1)

            hx = lambda i: H[:, i, 0:T]
            for i in (2, 3):
                freed[i] = (sem("sc_v"), 8 * (NPAIR + 2))
            for i in (0, 1, 4, 5, 6, 7):
                freed.pop(i, None)
            rms_sum(pe, "nf", take(4, "rms_std", NORMS["nf"] + 1), sq, T)
            rms_sum(pe, "n3", take(4, "rms_std", NORMS["n3"] + 1), sq, T)
            pe.wait_ge(sem("rms_out"), norm_out("n3", KD - 1))
            project("glu", lambda j: j, lambda j: ("glu_ev", j + 1), act_in=hx, mm="glu_mm")
            project("a", lambda j: 4 + j, lambda j: ("u_v", j + 2), act_in=hx, mm="a_mm")
            w = weights("v2", KD)
            wait_weights(pe, "v2")
            for t in range(TT):
                b = take(t, "v2_ev", t + 1)
                product(b[:, :], [(H[:, k, 128 * t:128 * (t + 1)], w[:, k, :]) for k in range(KD)]).then_inc(sem("v2_mm"), 1)
            project("q2", lambda j: 4 + j, lambda j: ("q2_ev", j + 1), act_in=hx, mm="q2_mm")
            b = take(7, "f_v", 1)
            for t in range(TT):
                ins = product(b[:, 8 * t:8 * (t + 1)], [(ones[0:1, :], rowb[0:1, 16:24])] +
                              [(H[:, k, 128 * t:128 * (t + 1)], wsmall[:, k, 32:40]) for k in range(KD)])
            ins.then_inc(sem("f_mm"), 1)
            project("k2", lambda j: j, lambda j: ("k2_ev", j + 1), act_in=hx, mm="k2_mm")
            pe.wait_ge(sem("dw_v"), KH * TAPS)
            product(take(4, "ln_v", KH)[:, :], [(ones, cT[:, k, :]) for k in range(KH)]).then_inc(sem("lnm_mm"), 1)
            pe.wait_ge(sem("f_v"), 4)
            b = take(6, "f_v", 5)
            for t in range(TT):
                ins = nc.tensor.transpose(b[0:FOX_H, 128 * t:128 * (t + 1)], f_tok[:, t, :], ident)
            ins.then_inc(sem("fT_mm"), 1)
            b = take(5, "ln_std", 1)
            for k in range(KH):
                pe.wait_ge(sem("ln_sq"), k + 1)
                nc.tensor.matmul(b[:, :], ones, sq[:, k % 2, :], start=(k == 0), stop=(k == KH - 1)).then_inc(sem("lnq_mm"), 1)

            def logits(hp):
                for e in range(2):
                    b = take(6 + e, "cb_ev", 2 * hp + e + 1)
                    h = 2 * hp + e
                    nc.tensor.matmul(b[:, :], ident[0:FOX_H, h:h + 1].broadcast_to([FOX_H, 128]), c_row[0:FOX_H, :], start=True, stop=True).then_inc(sem("cb_mm"), 1)
                for i in range(TT):
                    w = 128 * (i + 1)
                    bs = [take(2 * (i % 2) + e, "L_v", 3 * (8 * hp + 2 * i + e) + 1) for e in range(2)]
                    for e in range(2):
                        r = slice(64 * e, 64 * e + 64)
                        ins = nc.tensor.matmul(bs[e][:, 0:w], q2[r, hp, 128 * i:128 * (i + 1)], k2[r, hp, 0:w], start=True, stop=True)
                    ins.then_inc(sem("S2_mm"), 1)

            def gate_c(j):
                name = f"gc{j // 4}"
                if j % 4 == 0:
                    wait_weights(pe, name)
                w = weights(name, KD)
                b = take(4 + j % 2, "gc_ev", j + 1)
                product(b[:, :], [(w[:, k, 128 * (j % 4):128 * (j % 4) + 128], H[:, k, 0:T]) for k in range(KD)]).then_inc(sem("gcm"), 1)

            pe.wait_ge(*reached("q2_ev", 4))
            pe.wait_ge(*reached("k2_ev", 4))
            pe.wait_ge(sem("c_v"), 1)
            logits(0)
            for hp in range(FOX_H // 2):
                if hp + 1 < FOX_H // 2:
                    logits(hp + 1)
                gate_c(2 * hp)
                gate_c(2 * hp + 1)
                pe.wait_ge(sem("P_ready"), 8 * (hp + 1))
                out_b = take(5, "attn_ev", hp + 1)
                for e in range(2):
                    for t in range(TT):
                        b = take(6 + t % 2, "PT_ev", 8 * hp + 4 * e + t + 1)
                        for i in range(t, TT):
                            c = 1280 * e + 64 * i * (i + 1) + 128 * t
                            ins = nc.tensor.transpose(b[:, 128 * i:128 * (i + 1)], Pbuf[hp % 2][:, c:c + 128], ident)
                        ins.then_inc(sem("PT_mm"), 1)
                    for t in range(TT):
                        pe.wait_ge(sem("PT_ev"), 8 * hp + 4 * e + t + 1)
                        c = (0, 512, 896, 1152)[t]
                        ins = nc.tensor.matmul(out_b[64 * e:64 * e + 64, 128 * t:T], V2[:, t, 2 * hp + e, :], PT2[:, c:c + 512 - 128 * t],
                                               start=(t == 0), stop=(t == TT - 1), tile_position=(0, 64 * e))
                    ins.then_inc(sem("pv2_mm"), 1)
            pe.wait_ge(*reached("c_ready", KH))
            w = weights("pw", KH)
            wait_weights(pe, "pw")
            for j in range(8):
                b = take(j % 4, "pw_v", j + 1)
                product(b[:, :], [(w[:, k, 128 * j:128 * (j + 1)], cT[:, k, :]) for k in range(KH)]).then_inc(sem("pw_mm"), 1)
            for s in range(2):
                project(f"ga{s}", lambda j: 4 + j % 4, lambda j: ("ga_ev", j + 1), act_in=hx, j0=4 * s, mm="gam")
            pe.wait_ge(sem("attn_ev"), 4)
            project("ab", lambda j: j % 4, lambda j: ("ab_v", 2 * j + 1), tiles=8, k=KH, act_in=lambda i: q2[:, i, :], mm="ab_mm")
            pe.wait_ge(sem("ab_v"), 16)
            for s in range(2):
                project(f"w2o{s}", lambda j: j % 4, lambda j: ("x3", j + 1), act_in=lambda i: merged[:, i, :], j0=4 * s, mm="w2o_mm")

            def xpv(h):
                pe.wait_ge(sem("xT2_ev"), 2 * (h + 1))
                b = take(4 + h, "ox_ev", h + 1)
                product(b[:, :], [(Vm[:, m, 128 * h:128 * (h + 1)], PTx[:, h, m, :]) for m in range(2)]).then_inc(sem("xo_pv"), 1)

            rms_sum(pe, "n4", take(4, "rms_std", NORMS["n4"] + 1), sq, T)
            pe.wait_ge(sem("rms_out"), norm_out("n4", KD - 1))
            project("xa_wq", lambda j: j, lambda j: ("xq_ev", j + 1), act_in=hx, mm="xq_mm")
            pe.wait_ge(*reached("xq_ev", 4))
            for h in range(4):
                for i in range(2):
                    b = take((2 * h + i) % 8, "xexp_s", 4 * h + 2 * i + 2)
                    for j in range(2):
                        q = 128 * (2 * i + j)
                        ins = nc.tensor.matmul(b[:, 256 * j:256 * (j + 1)], q2[:, h, q:q + 128], kmT[:, h, :], start=True, stop=True)
                    ins.then_inc(sem("xS_mm"), 1)
            for h in range(4):
                pe.wait_ge(sem("xP_ready"), 4 * (h + 1))
                for m in range(2):
                    b = take(2 * (h % 2) + m, "xT2_ev", 2 * h + m + 1)
                    for i in range(TT):
                        ins = nc.tensor.transpose(b[:, 128 * i:128 * (i + 1)], Px[:, h, i, 128 * m:128 * (m + 1)], ident)
                    ins.then_inc(sem("xT2_mm"), 1)
                if h:
                    xpv(h - 1)
            xpv(3)
            pe.wait_ge(sem("ox_ev"), 4)
            project("xa_wo", lambda j: j % 4, lambda j: ("x4", j + 1), tiles=8, k=KH, act_in=lambda i: k2[:, i, :], mm="xo_mm")
            rms_sum(pe, "n5", take(4, "rms_std", NORMS["n5"] + 1), sq, T)
            pe.wait_ge(sem("rms_out"), norm_out("n5", KD - 1))
            b = take(5, "g_v", 1)
            for t in range(TT):
                ins = product(b[:, 20 * t:20 * (t + 1)], [(ones[0:1, :], rowb[0:1, 24:44])] +
                              [(H[:, k, 128 * t:128 * (t + 1)], wsmall[:, k, 40:60]) for k in range(KD)])
            ins.then_inc(sem("rl_mm"), 1)
            for j in range(8):
                b = take(j % 4, "h2_ev", j + 1)
                for i in range(4):
                    k, t = 4 * (j % 2) + i, j // 2
                    ins = nc.tensor.transpose(b[:, 128 * i:128 * (i + 1)], H[:, k, 128 * t:128 * (t + 1)], ident)
                ins.then_inc(sem("h2_mm"), 1)
            pe.wait_ge(sem("comb_ready"), 1)
            b = take(6, "chosen", 1)
            for t in range(TT):
                ins = nc.tensor.transpose(b[0:16, 128 * t:128 * (t + 1)], rt["comb"][:, t, :, :], ident)
            ins.then_inc(sem("combT_mm"), 1)
            pe.wait_ge(sem("block_counts"), 1)
            nc.tensor.matmul(take(7, "ends_v", 1)[0:E2, 0:1], const[0:E2, CONST["s_le_j"]:CONST["s_le_j"] + E2], nblk, start=True, stop=True).then_inc(sem("ends_mm"), 1)
            pe.wait_ge(sem("ended"), 1)
            nc.tensor.matmul(take(6, "block_expert", 1)[0:1, 0:32], ones[0:E2, 0:1], ended, start=True, stop=True).then_inc(sem("which_mm"), 1)
            pe.wait_ge(sem("places"), 1)
            b = take(5, "pos_v", 1)
            for t in range(TT):
                ins = nc.tensor.transpose(b[:, E2 * t:E2 * (t + 1)], place[:, 128 * t:128 * (t + 1)], ident[0:E2, 0:E2])
            ins.then_inc(sem("posT_mm"), 1)
            for name, value in (("h2_ev", 8), ("rms_std", NORMS["n5"] + 1), ("pos_v", 1), ("block_expert", 1), ("ends_v", 1)):
                pe.wait_ge(*reached(name, value))

            def gather_blocks(sel):
                pe.wait_ge(sem("b_sel"), sel)
                for i in range(2):
                    for k in range(4 * i, 4 * i + 4):
                        c = 128 * (k - 4 * i)
                        ins = product(PS[i][:, c:c + 128], [(h2_tok[:, t, 128 * k:128 * (k + 1)], selb[:, t, :]) for t in range(TT)])
                    ins.then_inc(sem("b_gather"), 1)

            def scatter_blocks(pair):
                for name in ("b_GT", "b_y0", "b_y1"):
                    pe.wait_ge(sem(name), pair + 1)
                for j in range(KD):
                    pe.wait_ge(sem("x5"), pair * 8 + (7 + j))
                    nc.tensor.matmul(PS[3 + j % 2][:, :], yb[:, 128 * j:128 * (j + 1)], GTb, start=True, stop=True).then_inc(sem("b_scatter"), 1)

            gather_blocks(1)
            with pe.Fori(0, NPAIR2) as pair:
                pe.wait_ge(sem("b_x"), pair * 2 + 2)
                pe.wait_ge(sem("b_hid"), pair + 1)
                for i in range(2):
                    pe.wait_ge(sem(f"gate_up{i}_in"), pair * 32 + 32)
                for k in range(KD):
                    for i in range(2):
                        ins = nc.tensor.matmul(PS[2][BLK * i:BLK * (i + 1), :], xb[:, k, BLK * i:BLK * (i + 1)], ring[:, i, 512 * k:512 * (k + 1)],
                                               start=(k == 0), stop=(k == KD - 1), tile_position=(0, BLK * i))
                ins.then_inc(sem("b_gate_up"), 1)
                scatter_blocks(pair)
                pe.wait_ge(sem("b_hid"), pair + 2)
                for i in range(2):
                    ins = nc.tensor.transpose(PS[5][:, 128 * i:128 * (i + 1)], hb[:, 128 * i:128 * (i + 1)], ident)
                ins.then_inc(sem("b_turn"), 1)
                gather_blocks(pair + 2)
                pe.wait_ge(sem("b_hidT"), pair + 1)
                pe.wait_ge(sem("b_gates"), pair + 1)
                for t in range(TT):
                    ins = nc.tensor.transpose(PS[5][:, 128 * t:128 * (t + 1)], gb[:, t, :], ident)
                ins.then_inc(sem("b_turn_g"), 1)
                pe.wait_ge(sem("down_in"), pair * 32 + 32)
                for half in range(2):
                    for f in range(2):
                        for i in range(2):
                            c = 2048 * i + 1024 * f + 512 * half
                            ins = nc.tensor.matmul(PS[6 + half][BLK * i:BLK * (i + 1), :], hbT[:, f, BLK * i:BLK * (i + 1)], ring[:, 2, c:c + 512],
                                                   start=(f == 0), stop=(f == 1), tile_position=(0, BLK * i))
                    ins.then_inc(sem("b_down"), 1)
            scatter_blocks(NPAIR2)
            freed.clear()
            for i, (name, value) in enumerate((("b_x", 2 * NPAIR2 + 2), ("b_x", 2 * NPAIR2 + 2), ("b_hid", NPAIR2 + 1), ("x5", 8 * (NPAIR2 + 2)), ("x5", 8 * (NPAIR2 + 2)))):
                freed[i] = (sem(name), value)
            rms_sum(pe, "n6", take(4, "rms_std", NORMS["n6"] + 1), sq, T)
            for j in range(8):
                b = take(j % 4, "ot_ev", j + 1)
                t = j // 2
                for i in range(4):
                    k = 4 * (j % 2) + i
                    pe.wait_ge(sem("rms_out"), norm_out("n6", k))
                    ins = nc.tensor.transpose(b[:, 128 * i:128 * (i + 1)], H[:, k, 128 * t:128 * (t + 1)], ident)
                ins.then_inc(sem("ot_mm"), 1)


def kernel(**inputs):
    import concourse.bacc as bacc
    from concourse.bass_utils import run_bass_kernel_spmd

    nc = bacc.Bacc("TRN2", target_bir_lowering=False, num_devices=1)
    sent = {name: np.ascontiguousarray(a) for name, a in inputs.items()}
    sent["consts"], sent["dft"] = constant_tables()
    arrays, A = {}, {}
    for name, a in sent.items():
        arrays[f"in_{name}"] = a
        A[name] = nc.dram_tensor(f"in_{name}", a.shape, mybir.dt.from_np(a.dtype), kind="ExternalInput").ap()
    out = nc.dram_tensor("out", (1, T, D), F32, kind="ExternalOutput").ap()
    build(nc, A, out)
    result = run_bass_kernel_spmd(nc, [arrays], core_ids=[0])
    return result.results[0]["out"]
```

```python
from contextlib import ExitStack

import numpy as np

import concourse.bass as bass
from concourse import mybir
from concourse.alu_op_type import AluOpType as ALU

ACT = mybir.ActivationFunctionType
F32 = mybir.dt.float32
F32R = mybir.dt.float32r
AX_X = mybir.AxisListType.X

P = 128
T = 512
TC = 256
D = 1024
KD = D // P
TT = T // P
TA = (T + TC) // P
HALF = 512
KH = HALF // P
EPS = 1e-6
GRID_W = 64
ROWS = T // GRID_W
NH = 4
QK_SCALE = float(P) ** -0.5
OFF_F, OFF_Q, OFF_K, OFF_V, OFF_O, OFF_G, OFF_BR = 0, 512, 1024, 1536, 2048, 2560, 2576
OFF_F2 = 2560
NE = 16
CAP = 64
NPAIR = NE // 2
TAPS = 31
FOX_H = 8
FOX_SCALE = 64.0 ** -0.5
NG, EPG = 4, 4
FF = 256
W2_GLU, W2_Q, W2_K, W2_V, W2_C, W2_A = 512, 1024, 1536, 2048, 2568, 3592
E2 = NG * EPG
BLK = 64
NB2 = (2 * T + E2 * (BLK - 1)) // BLK
NPAIR2 = (NB2 + 1) // 2
NSLOT = 4

VEC = {name: KD * i for i, name in enumerate(
    ["c", "c_ctx", "g_norm1", "g_norm2", "g_final", "mix", "xa", "mem", "moe", "final2"])}
VEC["b_ada"] = 80
VEC["conv2d"] = 128
VEC["dw_b"], VEC["ln_g"], VEC["ln_b"] = 200, 204, 208
VEC["dw_w"] = 212
NVEC = 336

NORMS = {name: i for i, name in enumerate(["nc", "n1", "nm", "n2", "nf", "n3", "n4", "n5", "n6"])}

PART_BANK = 5
PV_BANKS = (4, 0, 1, 4)

WIDE = {name: i + 1 for i, name in enumerate(["n1", "n2", "nf", "n3", "n4", "n5", "n6"])}


def norm_out(name, k):
    return (KD + 1) * NORMS[name] + k + 2


PRODUCT_STAGES = [
    ("cT_mm", 4), ("xT_mm", 8), ("vec_mm", 1), ("k_mm", 8), ("v_mm", 6), ("u_mm", 4), ("gate_mm", 1), ("rows_mm", 1),
    ("q_mm", 4), ("o_mm", 4), ("tokg_mm", 1), ("kc_mm", 2), ("C0_mm", 4), ("Z_mm", 8), ("fu_mm", 4), ("yf_mm", 8), ("mT_mm", 4),
    ("ym_mm", 8), ("brb_mm", 8), ("wo_mm", 8), ("logit_mm", 1), ("htok_mm", 8), ("affT_mm", 1), ("km_mm", 4), ("vm_mm", 2),
    ("slotT_mm", 1), ("glu_mm", 4), ("a_mm", 4), ("v2_mm", 4), ("q2_mm", 4), ("f_mm", 1), ("k2_mm", 4), ("lnm_mm", 1),
    ("fT_mm", 1), ("pw_mm", 8), ("gam", 8), ("ab_mm", 8), ("w2o_mm", 8), ("xq_mm", 4), ("xS_mm", 8), ("xo_mm", 8), ("rl_mm", 1),
    ("h2_mm", 8),
    ("combT_mm", 1), ("ends_mm", 1), ("which_mm", 1), ("posT_mm", 1), ("ot_mm", 8),
]
COPY_STAGES = [
    ("xT_ev", 8), ("k_silu", 8), ("v_ev", 6), ("u_ev", 4), ("q_silu", 4), ("o_ev", 4), ("C0_ev", 4), ("Z_ev", 8), ("fu_ev", 4),
    ("yf_ev", 8), ("ym_ev", 8), ("brb_ev", 8), ("htok_ev", 8), ("km_ev", 4), ("vm_ev", 2), ("glu_ev", 4), ("v2_ev", 4),
    ("q2_ev", 4), ("k2_ev", 4), ("c_ready", 4), ("ga_ev", 8), ("xq_ev", 4), ("h2_ev", 8),
]


def bases(stages):
    return {name: sum(n for _, n in stages[:i]) for i, (name, _) in enumerate(stages)}


SHARED = {"product_done": bases(PRODUCT_STAGES), "copy_done": bases(COPY_STAGES)}


CONST = {"ident": 0, "ones": 128, "s_le_j": 256, "s_ge_j": 384, "future": 512, "dft": 640, "iota": 896, "pick": 960, "fold": 962}
NCONST = 982


def constant_tables():
    i, j = np.arange(P)[:, None], np.arange(P)[None, :]
    table = np.zeros((P, NCONST))
    table[:, 0:128] = i == j
    table[:, 128:256] = 1.0
    table[:, 256:384] = i <= j
    table[:, 384:512] = i >= j
    table[:, 512:640] = np.where(j > i, -1e30, 0.0)
    table[:, 640:768] = np.cos(2 * np.pi * (i * j % P) / P)
    table[:, 768:896] = np.sin(2 * np.pi * (i * j % P) / P)
    table[:, 896:960] = np.arange(1, 65)[None, :]
    table[:, 960] = i[:, 0] % 32 == 0
    table[:, 961] = i[:, 0] % 32 == 1
    table[:, 962:982] = i % 32 == np.arange(20)[None, :]
    n, m = np.arange(T)[:, None], np.arange(T)[None, :]
    angle = 2 * np.pi * (n * m % T) / T
    norm = float(T * P) ** -0.5
    dft = np.concatenate([np.cos(angle) * norm, -np.sin(angle) * norm], axis=1)
    return table.astype(np.float32), dft.astype(np.float32)


def build(nc, A, out):
    with ExitStack() as ctx:
        def sb(name, *shape):
            return ctx.enter_context(nc.sbuf_tensor(name, list(shape), F32))

        sems = {}

        def sem(name):
            name = next((shared for shared, stages in SHARED.items() if name in stages), name)
            if name not in sems:
                sems[name] = ctx.enter_context(nc.semaphore(name))
            return sems[name]

        def reached(name, value):
            return sem(name), value + next((stages[name] for stages in SHARED.values() if name in stages), 0)

        place_of = {}

        def area(name, n):
            place_of[name] = -(-nc.sbuf_base // 32) * 32
            return sb(name, P, n)

        def rounded_in(name, where, column, n):
            return nc.alloc_sbuf_tensor_at(name, [P, n], F32R, offset=place_of[where] + 4 * column)[:, :]

        ring = sb("weight_slots", P, NSLOT, 4096)
        xT = sb("xT", P, KD, T)
        H = sb("H", P, KD, T + TC)
        R14 = area("R14", 8192)
        R1, R2, R3, R4 = (R14[:, 2048 * i:2048 * (i + 1)] for i in range(4))
        R5 = sb("R5", P, 2064)
        R6 = area("R6", 4096)
        R7 = area("R7", 4104)
        SM = area("SM", 3072)
        const = sb("const", P, NCONST)
        vec = sb("vec", P, NVEC)
        mods = sb("mods", P, 48, 2)
        gains = sb("gains", P, 3, KD)
        rowb = sb("rowb", 1, 64)
        wsmall = sb("wsmall", P, KD, 72)
        thin = SM[:, 0:T]
        C0 = sb("C0", P, 2, NH, 129)
        Mrow = sb("Mrow", 36, T)
        tokg = sb("tokg", P, 368)
        rowsB = sb("rowsB", 16, T)
        small = sb("small", P, 64)

        block_expert = ctx.enter_context(nc.sbuf_tensor("block_expert", [1, 32], mybir.dt.int32))

        def full(a):
            return a.bitcast(F32)

        ident = const[:, 0:128]
        ones = const[:, 128:256]
        masks2 = const[:, 256:512].rearrange("p (d j) -> p d j", d=2)
        fold = const[:, CONST["fold"]:CONST["fold"] + 20]
        thin_gates = SM[:, 2048:2048 + T + TC]
        dftF = const[:, 640:896]

        def v(name, i=0, n=1):
            return vec[:, VEC[name] + i:VEC[name] + i + n]

        def slot(n, k):
            return ring[:, n % NSLOT, :].rearrange("p (k n) -> p k n", k=k)

        PS = [ctx.enter_context(nc.psum_tensor(f"bank{i}", [P, 512], F32)) for i in range(8)]

        x_tok = R6[:, :].rearrange("p (t d) -> p t d", t=TT)
        c_tok = R1[:, :].rearrange("p (t d) -> p t d", t=2)
        ctxT = R2[:, :].rearrange("p (k t) -> p k t", k=KD)
        vpack = SM[:, 0:384].rearrange("p (a n) -> p a n", a=3)
        sq = SM[:, 0:1024].rearrange("p (a n) -> p a n", a=2)
        sqc = SM[:, 1024:1536].rearrange("p (a n) -> p a n", a=2)
        std = SM[:, 1536:2304]
        sum_parts = SM[:, 0:T]
        rstd = R7[:, 0:768]
        silu_c = sb("silu_c", P, KD, 32)
        ada_part = SM[:, 2048:3072].rearrange("p (a n) -> p a n", a=2)
        ada_part0 = R3[:, 0:1024].rearrange("p (a n) -> p a n", a=2)
        uT = R1[:, :].rearrange("p (k t) -> p k t", k=KH)
        fuT = uT
        oT = R2[:, :].rearrange("p (k t) -> p k t", k=KH)
        qT = R3[:, :].rearrange("p (k t) -> p k t", k=KH)
        kT = R4[:, :].rearrange("p (k t) -> p k t", k=KH)
        Vx = R5[:, :].rearrange("p (t h d) -> p t h d", t=TT, h=NH)
        kcT = R7[:, 0:1024].rearrange("p (k t) -> p k t", k=KH)
        Vc = R7[:, 1024:2056].rearrange("p (t h d) -> p t h d", t=2, h=NH)
        kw = R7[:, 2056:4104].rearrange("p (t e h d) -> p t e h d", t=2, e=2, h=NH)
        acc = SM[:, 0:1024].rearrange("p (a n) -> p a n", a=2)
        gts = SM[:, 1024:1120].rearrange("p (t e c h) -> p t e c h", t=TA, e=2, c=2)
        absf = SM[:, 1120:1168].rearrange("p (t e h) -> p t e h", t=TA, e=2)
        lnp = SM[:, 1168:1216].rearrange("p (t e h) -> p t e h", t=TA, e=2)
        minf = SM[:, 1216:1264].rearrange("p (t e h) -> p t e h", t=TA, e=2)
        tok_lf = SM[:, 1280:1664].rearrange("p (t e r) -> p t e r", t=TA, e=2)
        tok_lf2 = SM[:, 1280:1664].rearrange("p (t r) -> p t r", t=TA)
        tok_ig2 = SM[:, 1664:2048].rearrange("p (t r) -> p t r", t=TA)
        pick = const[:, 960:962]
        tok_ig = SM[:, 1664:2048].rearrange("p (t e r) -> p t e r", t=TA, e=2)
        lf_r = R6[0:36, 0:768]
        ig_r = R6[0:36, 768:1536]
        cum_r = R6[0:36, 1536:2304]
        a_r = R6[0:36, 2304:3072]
        zero_r = R6[0:36, 3072:3584]
        mm_r = R6[0:36, 3584:4096]
        wa_r = SM[0:36, 2048:2304]
        Z = R6[:, :].rearrange("p (t g n) -> p t g n", t=TT, g=NH)
        PT = R6[:, :].rearrange("p (t e j) -> p t e j", t=TT, e=2)
        ymT = R6[:, :].rearrange("p (k t) -> p k t", k=KD)
        merged = R7[:, 0:4096].rearrange("p (k t) -> p k t", k=KD)
        mb = SM[:, 0:1024].rearrange("p (e j) -> p e j", e=2)
        EX = SM[:, 1024:2048].rearrange("p (e j) -> p e j", e=2)
        qd = SM[:, 2048:3072].rearrange("p (e j) -> p e j", e=2)
        sig = R1[:, 0:1024].rearrange("p (a n) -> p a n", a=2)
        hm = R1[:, 1024:1536].rearrange("p (t d) -> p t d", t=TT)
        dg = R1[:, 1536:1792].rearrange("p (e n) -> p e n", e=2)
        a_t = tokg[:, 0:144].rearrange("p (t r) -> p t r", t=TT)
        enm_t = tokg[:, 144:288].rearrange("p (t r) -> p t r", t=TT)
        wa_t = tokg[:, 288:360].rearrange("p (t r) -> p t r", t=2)
        m0_b = tokg[:, 360:368]
        mend = small[0:36, 0:1]
        nmend = small[0:36, 1:2]
        m0 = small[0:36, 2:3]
        dn = small[:, 8:16].rearrange("p (t e) -> p t e", t=TT)
        den = small[:, 24:32].rearrange("p (t e) -> p t e", t=TT)
        m_tok = R4[:, :].rearrange("p (t d) -> p t d", t=2)
        memT = R2[:, :].rearrange("p (k t) -> p k t", k=KD)
        rstd2 = SM[:, 2304:3072]
        kmT = R5[:, 0:1024].rearrange("p (h t) -> p h t", h=4)
        Vm = R5[:, 1024:2048].rearrange("p (t d) -> p t d", t=2)
        h_tok = R6[:, :].rearrange("p (t d) -> p t d", t=TT)
        logit = R1[:, 0:64].rearrange("p (t e) -> p t e", t=TT)
        aff = R1[:, 64:136].rearrange("p (t e) -> p t e", t=TT)
        slot_t = R1[:, 136:208].rearrange("p (t e) -> p t e", t=TT)
        lmax = R1[:, 208:212]
        lsum = R1[:, 212:216]
        linv = R1[:, 216:220]
        work = R1[0:NE, 512:1024]
        taken = R1[0:NE, 1024:1536]
        top8 = R1[0:NE, 224:232]
        zrow = R1[0:NE, 1536:2048]
        xs = SM[:, 0:1024].rearrange("p (k s) -> p k s", k=KD)
        hidT = SM[:, 1024:2048].rearrange("p (e i s) -> p e i s", e=2, i=4)
        sg = SM[:, 2048:3072].rearrange("p (e n) -> p e n", e=2)
        selc = R7[:, 0:512].rearrange("p (t e s) -> p t e s", t=TT, e=2)
        gc = R7[:, 512:1024].rearrange("p (t e s) -> p t e s", t=TT, e=2)
        hid = R7[:, 1024:2048].rearrange("p (e n) -> p e n", e=2)
        GT = R7[:, 2048:2560]
        ypair = R7[:, 2560:3584]
        iota = const[:, 896:960]
        sgT = R2[:, :].rearrange("p (k t) -> p k t", k=KH)
        u_pad = R6[:, 0:KH * (T + TAPS - 1)].rearrange("p (k t) -> p k t", k=KH)
        cT = R1[:, :].rearrange("p (k t) -> p k t", k=KH)
        V2 = R2[:, :].rearrange("p (t h d) -> p t h d", t=TT, h=FOX_H)
        q2 = R3[:, :].rearrange("p (k t) -> p k t", k=KH)
        k2 = R4[:, :].rearrange("p (k t) -> p k t", k=KH)
        f_tok = tokg[:, 0:32].rearrange("p (t h) -> p t h", t=TT)
        f_abs = tokg[:, 32:64].rearrange("p (t h) -> p t h", t=TT)
        f_ln = tokg[:, 64:96].rearrange("p (t h) -> p t h", t=TT)
        f_row = Mrow[0:FOX_H, :]
        zero8 = R7[0:FOX_H, 0:T]
        rt = {}
        c = 0
        for name, dims in (("log", (TT, 20)), ("gmax", (TT,)), ("gexp", (TT, 4)), ("gsel", (TT, 4)), ("run", (TT, 4)), ("mix", (TT, 4, 4)),
                           ("esel", (TT, 4)), ("emax", (TT,)), ("p", (TT, 4)), ("gsum", (TT,)), ("pg", (TT,)), ("m1", (TT, 4)),
                           ("p2", (TT, 4)), ("m2", (TT, 4)), ("comb", (TT, 4, 4))):
            n = int(np.prod(dims))
            a = R7[:, c:c + n]
            if len(dims) == 2:
                a = a.rearrange("p (t n) -> p t n", t=TT)
            if len(dims) == 3:
                a = a.rearrange("p (t g j) -> p t g j", t=TT, g=4)
            rt[name] = a
            c += n
        c_row = rowsB[:, :]
        cb = C0[:, :, :, :].rearrange("p a b c -> p (a b c)")[:, 0:1024].rearrange("p (e n) -> p e n", e=2)
        Pbuf = [SM[:, 0:2560], R6[:, 0:2560]]
        PT2 = R6[:, 2560:3840]
        nmax = tokg[:, 96:128]
        psum_ = tokg[:, 128:160]
        prec = tokg[:, 160:192]
        sigA = R6[:, :].rearrange("p (k t) -> p k t", k=KD)
        tmp2 = SM[:, 0:1024].rearrange("p (a n) -> p a n", a=2)
        Px = R6[:, :].rearrange("p (h i m) -> p h i m", h=4, i=TT)
        PTx = R7[:, 0:4096].rearrange("p (h m q) -> p h m q", h=4, m=2)
        xmax = tokg[:, 192:208].rearrange("p (h i) -> p h i", h=4)
        xsum = tokg[:, 208:224].rearrange("p (h i) -> p h i", h=4)
        xrec = tokg[:, 224:240].rearrange("p (h i) -> p h i", h=4)
        h2_high, h2_low = (rounded_in(f"h2_{part}", where, column, 4096).rearrange("p (t d) -> p t d", t=TT)
                           for part, where, column in (("high", "R6", 0), ("low", "R14", 4096)))
        h2_all = R14[:, 0:4096].rearrange("p (t d) -> p t d", t=TT)
        chosen = rowsB[0:E2, :]
        place = Mrow[0:E2, :]
        thresh = R7[0:E2, 3072:3072 + T // BLK]
        over = R7[0:E2, 3088:3088 + T // BLK]
        nblk, ends, blk_base = (R7[0:E2, 3104 + i:3105 + i] for i in range(3))
        ended = R7[0:E2, 3112:3112 + 32]
        iota2 = R7[:, 3144:3144 + 2 * BLK]
        pos_t = R7[:, 3272:3336].rearrange("p (t e) -> p t e", t=TT)
        hit_t = R7[:, 3336:3400].rearrange("p (t e) -> p t e", t=TT)
        pos2 = R7[:, 3400:3408].rearrange("p (a t) -> p a t", a=2)
        wt2 = R7[:, 3408:3416].rearrange("p (a t) -> p a t", a=2)
        xb = SM[:, 0:1024].rearrange("p (k s) -> p k s", k=KD)
        hits = [SM[:, 1024 + 512 * a:1536 + 512 * a].rearrange("p (t s) -> p t s", t=TT) for a in range(2)]
        selb = rounded_in("picks", "SM", 2048, 512).rearrange("p (t s) -> p t s", t=TT)
        GTb = [rounded_in("GT_even", "R7", 1024, 512), rounded_in("GT_odd", "R7", 2560, 512)]
        y_high = rounded_in("y_high", "R7", 1536, 1024)
        sgb = R7[:, 0:FF]
        hb = R7[:, FF:2 * FF]
        w_slot = [R7[:, 1020 + i:1021 + i] for i in range(2)]
        gb = H[:, 0:4, T:T + 2 * BLK]
        unused = H[:, 4:8, T:T + 2 * BLK]
        x_rows = C0[:, :, :, :].rearrange("p a b c -> p (a b c)")[:, 0:1024]
        down2 = R14[:, 0:4096]
        y_low = [rounded_in("y_low0", "R7", 3584, 512), rounded_in("y_low1", "SM", 2560, 512)]
        hbT = R7[:, 2 * FF:3 * FF].rearrange("p (i s) -> p i s", i=2)
        out_tok = R7[:, 0:4096].rearrange("p (t d) -> p t d", t=TT)
        rec = small[:, 16:24].rearrange("p (t e) -> p t e", t=TT)

        w_in, w_ada = A["w_in"][0], A["w_ada"][0]

        def cols(w, c0, n=512):
            return w[:, c0:c0 + n].rearrange("(k p) n -> p k n", p=P)

        W = []
        for s in range(4):
            W.append((f"ada{s}", cols(w_ada, 512 * s), "ada_mm", s + 1))
        W.append(("k", cols(w_in, OFF_K), "k_mm", 8))
        W.append(("v", cols(w_in, OFF_V), "v_mm", 6))
        W.append(("u", cols(w_in, OFF_F), "u_mm", 4))
        W.append(("q", cols(w_in, OFF_Q), "q_mm", 4))
        for s in (4, 5):
            W.append((f"ada{s}", cols(w_ada, 512 * s), "ada_mm", s + 1))
        W.append(("o", cols(w_in, OFF_O), "o_mm", 4))
        for s in range(6, 12):
            W.append((f"ada{s}", cols(w_ada, 512 * s), "ada_mm", s + 1))
        W.append(("dft", A["dft"].rearrange("(k p) n -> p k n", p=P), "fu_mm", 4))
        W.append(("w_fourier", A["w_fourier"][0].rearrange("(k p) n -> p k n", p=P), "yf_mm", 8))
        W.append(("brA0", cols(w_in, OFF_BR), "bra_mm", 4))
        W.append(("brA1", cols(w_in, OFF_BR + 512), "bra_mm", 8))
        W.append(("w_mlstm", A["w_mlstm"][0].rearrange("(k p) n -> p k n", p=P), "ym_mm", 8))
        W.append(("brB0", cols(w_in, OFF_BR + 1024), "brb_mm", 4))
        W.append(("brB1", cols(w_in, OFF_BR + 1536), "brb_mm", 8))
        W.append(("wo0", cols(A["w_out"][0], 0), "wo_mm", 4))
        W.append(("wo1", cols(A["w_out"][0], 512), "wo_mm", 8))
        W.append(("xa_wk", cols(A["xa_wk_2"][0], 0), "km_mm", 4))
        W.append(("xa_wv", cols(A["xa_wv_2"][0], 0), "vm_mm", 2))
        w2 = A["w_in_2"][0]
        W2 = [("glu", cols(w2, W2_GLU), "glu_mm", 4), ("a", cols(w2, 0), "a_mm", 4), ("v2", cols(w2, W2_V), "v2_mm", 4),
              ("q2", cols(w2, W2_Q), "q2_mm", 4), ("k2", cols(w2, W2_K), "k2_mm", 4),
              ("gc0", cols(w2, W2_C), "gcm", 4), ("gc1", cols(w2, W2_C + 512), "gcm", 8),
              ("pw", A["conv_pw_w_2"][0].rearrange("(k p) n -> p k n", p=P), "pw_mm", 8),
              ("ga0", cols(w2, W2_A), "gam", 4), ("ga1", cols(w2, W2_A + 512), "gam", 8),
              ("ab", A["attn_branch_w_2"][0].rearrange("(k p) n -> p k n", p=P), "ab_mm", 8),
              ("w2o0", cols(A["w_out_2"][0], 0), "w2o_mm", 4), ("w2o1", cols(A["w_out_2"][0], 512), "w2o_mm", 8),
              ("xa_wq", cols(A["xa_wq_2"][0], 0), "xq_mm", 4),
              ("xa_wo", A["xa_wo_2"][0].rearrange("(k p) n -> p k n", p=P), "xo_mm", 8)]
        at = {w[0]: n for n, w in enumerate(W)}
        n_moe = len(W)
        n_two = n_moe + 12 * NPAIR
        at.update({w[0]: n_two + n for n, w in enumerate(W2)})
        n_end = n_two + len(W2)
        arrived = [sem(f"slot{i}_arrived") for i in range(NSLOT)]

        def weights(name, k):
            return slot(at[name], k)

        def wait_weights(e, name):
            n = at[name]
            e.wait_ge(arrived[n % NSLOT], 16 * (n // NSLOT + 1))

        block = ctx.enter_context(nc.Block())

        @block.sync
        def _(sp):
            row = 0
            for name, rows in (("c", 8), ("c_ctx", 8), ("g_norm1", 8), ("g_norm2", 8), ("g_final", 8),
                               ("norm_mix_g_2", 8), ("norm_xa_g_2", 8), ("norm_mem_g_2", 8),
                               ("norm_moe_g_2", 8), ("norm_final_g_2", 8), ("b_ada", 48)):
                src = A[name]
                if len(src.shape) == 1:
                    src = src.rearrange("(a n) -> a n", a=1)
                sp.dma_start(vpack[row:row + rows, 0, :],
                             src.rearrange("a (k n) -> (a k) n", n=P)).then_inc(sem("vecs_in"), 16)
                row += rows
            sp.dma_start(vpack[0:72, 1, :], A["w_conv"].rearrange("a y x (k n) -> (a y x k) n", n=P)).then_inc(sem("vecs_in"), 16)
            row = 72
            for name in ("conv_dw_b_2", "conv_ln_g_2", "conv_ln_b_2"):
                sp.dma_start(vpack[row:row + 4, 1, :], A[name].rearrange("a (k n) -> (a k) n", n=P)).then_inc(sem("vecs_in"), 16)
                row += 4
            sp.dma_start(vpack[0:124, 2, :], A["conv_dw_w_2"].rearrange("a w (k n) -> (a w k) n", n=P)).then_inc(sem("vecs_in"), 16)
            for n, (name, src, free, value) in enumerate(W):
                if n >= NSLOT:
                    sp.wait_ge(*reached(W[n - NSLOT][2], W[n - NSLOT][3]))
                sp.dma_start(ring[:, n % NSLOT, :].rearrange("p (k n) -> p k n", k=src.shape[1]), src).then_inc(arrived[n % NSLOT], 16)

            n0 = len(W)

            def expert_slot(pair, i):
                if i < 8:
                    name, e, half = ("w_gate_e", "w_up_e")[i % 4 // 2], i // 4, i % 2
                else:
                    name, e, half = "w_down_e", i % 2, (i - 8) // 2
                src = A[name][0].rearrange("(q e) (k p) n -> p q e k n", e=2, p=P)[:, bass.ds(pair, 1), e, :, 512 * half:512 * half + 512]
                s = (n0 + i) % NSLOT
                dst = ring[:, s, :].rearrange("p (q k n) -> p q k n", q=1, k=KD)
                sp.dma_start(dst, src).then_inc(arrived[s], 16)

            for i in range(4):
                w = W[n0 + i - NSLOT]
                sp.wait_ge(*reached(w[2], w[3]))
                expert_slot(0, i)
            with sp.Fori(0, NPAIR - 1) as pair:
                for i in range(4, 16):
                    sp.wait_ge(sem("moe_mm"), pair * 6 + ((i - 4) // 2 + 1))
                    sp.sem_inc(sem("sp_step"), 1)
                    expert_slot(pair if i < 12 else pair + 1, i % 12)
            for i in range(4, 12):
                sp.wait_ge(sem("moe_mm"), 6 * (NPAIR - 1) + (i - 4) // 2 + 1)
                expert_slot(NPAIR - 1, i)
            for n, (name, src, free, value) in enumerate(W2):
                if n < NSLOT:
                    sp.wait_ge(sem("moe_mm"), 6 * (NPAIR - 1) + (n + 8) // 2 + 1)
                else:
                    sp.wait_ge(*reached(W2[n - NSLOT][2], W2[n - NSLOT][3]))
                s = (n_two + n) % NSLOT
                sp.dma_start(ring[:, s, :].rearrange("p (k n) -> p k n", k=src.shape[1]), src).then_inc(arrived[s], 16)

            def expert_of(block):
                return sp.value_load(block_expert[0:1, bass.ds(block, 1)], min_val=0, max_val=E2 - 1)

            def load_gate_up(e, s):
                for j, name in enumerate(("expert_w_gate_2", "expert_w_up_2")):
                    src = A[name][0].rearrange("e (k p) n -> p e k n", p=P)[:, bass.ds(e, 1), :, :]
                    dst = ring[:, s, :].rearrange("p (q k n) -> p q k n", q=1, k=KD)[:, :, :, FF * j:FF * (j + 1)]
                    sp.dma_start(dst, src).then_inc(sem(f"gate_up{s}_in"), 16)

            def load_down(e, i):
                src = A["expert_w_down_2"][0].rearrange("e (k p) n -> p e k n", p=P)[:, bass.ds(e, 1), :, :]
                dst = down2[:, 2048 * i:2048 * (i + 1)].rearrange("p (q k n) -> p q k n", q=1, k=2)
                sp.dma_start(dst, src).then_inc(sem("down_in"), 16)

            for s in range(NSLOT):
                last = max(n for n in range(n_end) if n % NSLOT == s)
                sp.wait_ge(*reached(W2[last - n_two][2], W2[last - n_two][3]))
            sp.wait_ge(sem("block_expert"), 1)
            first = [expert_of(i) for i in range(4)]
            for i in range(2):
                load_gate_up(first[i], i)
            sp.wait_ge(sem("h2_low"), 8)
            for i in range(2):
                load_down(first[i], i)
            for i in range(2, 4):
                load_gate_up(first[i], i)
            with sp.Fori(0, NPAIR2 // 2 - 1) as step2:
                for odd in range(2):
                    down = [expert_of(step2 * 4 + (2 * odd + 2 + i)) for i in range(2)]
                    ahead = [expert_of(step2 * 4 + (2 * odd + 4 + i)) for i in range(2)]
                    sp.wait_ge(sem("b_gate_up"), step2 * 2 + (odd + 1))
                    sp.sem_inc(sem("sp_step"), 1)
                    for i in range(2):
                        load_gate_up(ahead[i], 2 * odd + i)
                    sp.wait_ge(sem("b_down"), step2 * 4 + (2 * odd + 2))
                    sp.sem_inc(sem("sp_step"), 1)
                    for i in range(2):
                        load_down(down[i], i)
            down = [expert_of(2 * NPAIR2 - 2 + i) for i in range(2)]
            sp.wait_ge(sem("b_down"), 2 * NPAIR2 - 2)
            for i in range(2):
                load_down(down[i], i)
            for j in range(8):
                sp.wait_ge(sem("ot_ev"), j + 1)
                t, c = j // 2, 512 * (j % 2)
                sp.dma_start(out[0, 128 * t:128 * (t + 1), c:c + 512], out_tok[:, t, c:c + 512]).then_inc(sem("out_written"), 16)
            sp.wait_ge(sem("out_written"), 16 * 8)

        def rms_squares(act, name, src, buf, width, ready, prev=None):
            for k in range(KD):
                ready(k)
                if k >= 2:
                    act.wait_ge(sem("rms_sum"), KD * NORMS[name] + k - 1)
                act.activation(buf[:, k % 2, 0:width], src[:, k, 0:width], ACT.Square).then_inc(sem("rms_sq"), 1)

        def rms_root(act, name, bank, dst):
            act.wait_ge(sem("rms_sum"), KD * NORMS[name] + KD)
            act.activation(dst, bank, ACT.Sqrt, bias=small[:, 40:41], scale=1.0 / D).then_inc(sem("rms_std"), 1)

        def rms_sum(pe, name, bank, buf, width):
            for k in range(KD):
                pe.wait_ge(sem("rms_sq"), KD * NORMS[name] + k + 1)
                nc.tensor.matmul(bank[:, 0:width], ones, buf[:, k % 2, 0:width], start=(k == 0),
                                 stop=(k == KD - 1)).then_inc(sem("rms_sum"), 1)

        def wide_squares(act, name, ready, bank):
            for k in range(KD):
                ready(k)
                act.activation(H[:, k, 0:T], xT[:, k, :], ACT.Square).then_inc(sem("rms_sq"), 1)
            act.wait_ge(sem("rms_sum"), KD * NORMS[name] + KD)
            act.activation(sum_parts, PS[PART_BANK][:, :], ACT.Copy).then_inc(sem("rms_part"), 1)
            act.wait_ge(sem("rms_fold"), WIDE[name])
            act.activation(std[:, 0:T], PS[bank][:, :], ACT.Sqrt, bias=small[:, 40:41], scale=1.0 / D).then_inc(sem("rms_std"), 1)

        def wide_sum(pe, name, part_bank, bank):
            for k in range(KD):
                g = k % 4
                pe.wait_ge(sem("rms_sq"), KD * NORMS[name] + k + 1)
                nc.tensor.matmul(part_bank[32 * g:32 * g + 32, :], ones[:, 0:32], H[:, k, 0:T], start=(k < 4), stop=(k >= 4),
                                 tile_position=(0, 32 * g)).then_inc(sem("rms_sum"), 1)
            pe.wait_ge(sem("rms_part"), WIDE[name])
            nc.tensor.matmul(bank[:, :], pick[:, 0:1].broadcast_to([P, P]), sum_parts, start=True, stop=True).then_inc(sem("rms_fold"), 1)

        def rms_scale(dve, name, src, dst, width, std_, rstd_, gain):
            dve.wait_ge(sem("rms_std"), NORMS[name] + 1)
            nc.vector.reciprocal(rstd_, std_).then_inc(sem("rms_out"), 1)
            dve.wait_ge(sem("rms_out"), (KD + 1) * NORMS[name] + 1)
            for k in range(KD):
                nc.vector.scalar_tensor_tensor(out=dst(k), in0=src(k), scalar=gain(k), in1=rstd_,
                                               op0=ALU.mult, op1=ALU.mult).then_inc(sem("rms_out"), 1)

        @block.scalar
        def _(act):
            act.dma_start(const[:, :], A["consts"]).then_inc(sem("const_in"), 16)
            act.dma_start(c_tok, A["ctx"].rearrange("b (t p) d -> p (b t) d", p=P)).then_inc(sem("ctx_in"), 16)
            act.dma_start(x_tok, A["x"].rearrange("b (t p) d -> p (b t) d", p=P)).then_inc(sem("x_in"), 16)
            act.wait_ge(sem("boot"), 2)
            rms_squares(act, "nc", ctxT, sqc, TC, lambda k: act.wait_ge(sem("cT_ev"), k // 2 + 1))
            rms_root(act, "nc", PS[1][:, 0:TC], std[:, T:T + TC])
            for k in range(KD):
                act.wait_ge(*reached("xT_mm", k + 1))
                act.activation(xT[:, k, :], PS[k % 4][:, :], ACT.Copy).then_inc(sem("xT_ev"), 1)
            act.wait_ge(sem("vec_ready"), 1)
            act.wait_ge(sem("zeros_ready"), 1)
            for i, name in enumerate(("c", "c_ctx")):
                act.activation(silu_c[:, :, i], v(name, 0, KD), ACT.Silu).then_inc(sem("silu_c"), 1)
            wide_squares(act, "n1", lambda k: act.wait_ge(*reached("xT_ev", k + 1)), 0)
            act.dma_start(rowb[0:1, 0:16], A["b_gates"].rearrange("a g h -> a (g h)")).then_inc(sem("rowb_in"), 16)
            act.dma_start(rowb[0:1, 16:24], A["fox_bf_2"]).then_inc(sem("rowb_in"), 16)
            act.dma_start(rowb[0:1, 24:28], A["router_group_b_2"]).then_inc(sem("rowb_in"), 16)
            act.dma_start(rowb[0:1, 28:44], A["router_expert_b_2"]).then_inc(sem("rowb_in"), 16)
            c = 0
            for src in (w_in[:, OFF_G:OFF_BR], A["w_router"][0], A["w_in_2"][0, :, OFF_F2:OFF_F2 + 8], A["router_group_w_2"][0], A["router_expert_w_2"][0]):
                n = src.shape[1]
                act.dma_start(wsmall[:, :, c:c + n], src.rearrange("(k p) n -> p k n", p=P)).then_inc(sem("wsmall_in"), 16)
                c += n
            act.wait_ge(sem("gains1"), 2)
            for k in range(KD):
                act.wait_ge(sem("rms_out"), norm_out("nc", k))
                act.activation(H[:, k, T:T + TC], H[:, k, T:T + TC], ACT.Identity, bias=mods[:, k, 1:2]).then_inc(sem("h_ready"), 1)
            for k in range(KD):
                act.wait_ge(sem("rms_out"), norm_out("n1", k))
                act.activation(H[:, k, 0:T], H[:, k, 0:T], ACT.Identity, bias=mods[:, k, 0:1]).then_inc(sem("h_ready"), 1)
            def thin_copy(stage, dst, bank):
                act.wait_ge(sem("thin_mm"), stage)
                act.activation(dst, bank, ACT.Copy).then_inc(sem("thin_ev"), 1)

            for j in range(8):
                act.wait_ge(sem("conv_k"), 3 * (j + 1) if j < 4 else 12 + 9 * (j - 3))
                dst, src = (kcT[:, j, :], acc[:, j % 2, 0:TC]) if j < 4 else (kT[:, j - 4, :], acc[:, j % 2, :])
                act.activation(dst, src, ACT.Silu).then_inc(sem("k_silu"), 1)
            for t in range(TA):
                act.wait_ge(*reached("v_mm", t + 1))
                dst = Vx[:, t, :, 0:128] if t < TT else Vc[:, t - TT, :, 0:128]
                act.activation(dst, PS[(4, 5, 6, 7)[t % 4]][:, :].rearrange("p (h d) -> p h d", h=NH), ACT.Copy).then_inc(sem("v_ev"), 1)
            thin_copy(1, thin_gates[:, 0:T], PS[6][:, :])
            thin_copy(1, thin_gates[:, T:T + TC], PS[7][:, 0:TC])
            for j in range(4):
                act.wait_ge(*reached("u_mm", j + 1))
                act.activation(uT[:, j, :], PS[4 + j][:, :], ACT.Copy).then_inc(sem("u_ev"), 1)
            act.wait_ge(sem("gate_v"), 1)
            act.activation(absf, gts[:, :, :, 1, :], ACT.Abs).then_inc(sem("gate_s"), 1)
            act.wait_ge(sem("gate_s"), 1)
            act.activation(absf, absf, ACT.Exp, scale=-1.0).then_inc(sem("gate_s"), 1)
            act.wait_ge(sem("gate_s"), 2)
            act.activation(lnp, absf, ACT.Ln, bias=1.0).then_inc(sem("gate_s"), 1)
            act.wait_ge(*reached("rows_mm", 1))
            act.activation(ig_r[:, 0:T], PS[1][0:36, :], ACT.Copy).then_inc(sem("rows_s"), 1)
            act.wait_ge(sem("rows_v"), 11)
            act.activation(wa_r, a_r[:, T:T + TC], ACT.Exp, bias=nmend).then_inc(sem("rows_s"), 1)
            act.wait_ge(sem("rows_v"), 16)
            act.activation(mm_r, mm_r, ACT.Exp, scale=-1.0).then_inc(sem("rows_s"), 1)
            for j in range(4):
                act.wait_ge(sem("conv_q"), 9 * (j + 1))
                act.activation(qT[:, j, :], acc[:, j % 2, :], ACT.Silu).then_inc(sem("q_silu"), 1)
            for j in range(4):
                act.wait_ge(*reached("o_mm", j + 1))
                act.activation(oT[:, j, :], PS[j][:, :], ACT.Sigmoid).then_inc(sem("o_ev"), 1)
            for h in range(NH):
                act.wait_ge(*reached("C0_mm", h + 1))
                act.activation(C0[:, :, h, :], PS[2 + h % 2][:, 0:258].rearrange("p (e d) -> p e d", e=2), ACT.Copy).then_inc(sem("C0_ev"), 1)
            for j in range(8):
                act.wait_ge(*reached("Z_mm", j + 1))
                act.activation(Z[:, j // 2, 2 * (j % 2):2 * (j % 2) + 2, :], PS[4 + j % 4][:, :].rearrange("p (g n) -> p g n", g=2), ACT.Copy).then_inc(sem("Z_ev"), 1)
            for g in range(4):
                act.wait_ge(*reached("fu_mm", g + 1))
                act.activation(fuT[:, g, :], PS[g][:, :], ACT.Copy).then_inc(sem("fu_ev"), 1)
            for j in range(8):
                act.wait_ge(*reached("yf_mm", j + 1))
                act.activation(merged[:, j, :], PS[4 + j % 4][:, :], ACT.Copy).then_inc(sem("yf_ev"), 1)

            def gate_a(j):
                act.wait_ge(sem("bra_mm"), j + 1)
                if j >= 2:
                    act.wait_ge(sem("bra_v"), j - 1)
                act.activation(sig[:, j % 2, :], PS[6 + j % 2][:, :], ACT.Sigmoid).then_inc(sem("bra_ev"), 1)

            for h in range(NH):
                for e in range(2):
                    act.wait_ge(sem("mb_mm"), 2 * h + e + 1)
                    if e == 0 and h >= 1:
                        act.wait_ge(sem("attn_v"), 23 * h - 1)
                    act.activation(mb[:, e, :], PS[e][:, :], ACT.Copy).then_inc(sem("mb_ev"), 1)
                for e in range(2):
                    act.wait_ge(sem("mb_ev"), 2 * h + e + 1)
                    if e == 0 and h >= 1:
                        act.wait_ge(sem("pv_mm"), 4 * h)
                    act.activation(qd[:, e, :], mb[:, e, :], ACT.Exp, scale=-1.0, bias=m0_b[:, 4 * e + h:4 * e + h + 1]).then_inc(sem("dec_s"), 1)
                for t in range(TT):
                    if h or t:
                        act.wait_ge(sem("attn_v"), 23 * h + 2 + 5 * t if t else 23 * h - 1)
                    if t < 3:
                        act.activation(EX[:, 0, 128 * (t + 1):T], mb[:, 0, 128 * (t + 1):T], ACT.Exp, scale=-1.0, bias=a_t[:, t, h:h + 1]).then_inc(sem("E_off"), 1)
                    if t > 0:
                        act.activation(EX[:, 1, 0:128 * t], mb[:, 1, 0:128 * t], ACT.Exp, scale=-1.0, bias=a_t[:, t, 32 + h:33 + h]).then_inc(sem("E_off"), 1)
                    act.wait_ge(sem("attn_v"), 23 * h + 4 + 5 * t)
                    act.activation(EX[:, :, 128 * t:128 * (t + 1)], dg[:, :, :], ACT.Exp, scale=-1.0).then_inc(sem("E_diag"), 1)
                    if t == 1:
                        gate_a(2 * h)
                    if t == 3:
                        gate_a(2 * h + 1)
            act.wait_ge(sem("S_mm"), 16)
            act.dma_start(m_tok, A["mem_2"].rearrange("b (t p) d -> p (b t) d", p=P)).then_inc(sem("mem_in"), 16)
            rms_squares(act, "nm", memT, sqc, TC, lambda k: act.wait_ge(sem("mT_ev"), k // 2 + 1))
            rms_root(act, "nm", PS[5][:, 0:TC], std[:, T:T + TC])
            for j in range(8):
                act.wait_ge(*reached("ym_mm", j + 1))
                act.activation(ymT[:, j, :], PS[j % 4][:, :], ACT.Copy).then_inc(sem("ym_ev"), 1)
            for j in range(8):
                act.wait_ge(*reached("brb_mm", j + 1))
                if j >= 2:
                    act.wait_ge(sem("brb_v"), 2 * (j - 1))
                else:
                    act.wait_ge(sem("bra_v"), 8)
                act.activation(sig[:, j % 2, :], PS[4 + j % 4][:, :], ACT.Sigmoid).then_inc(sem("brb_ev"), 1)
            wide_squares(act, "n2", lambda k: act.wait_ge(sem("x1"), k + 1), 4)
            for k in range(KD):
                act.wait_ge(sem("rms_out"), norm_out("n2", k))
                act.activation(H[:, k, 0:T], H[:, k, 0:T], ACT.Identity, bias=mods[:, 24 + k, 0:1]).then_inc(sem("h2_ready"), 1)
            thin_copy(2, thin, PS[6][:, :])
            act.wait_ge(sem("aff_v"), 2)
            act.activation(logit, logit, ACT.Exp).then_inc(sem("aff_s"), 1)
            for j in range(8):
                act.wait_ge(*reached("htok_mm", j + 1))
                act.activation(h_tok[:, j // 2, 512 * (j % 2):512 * (j % 2) + 512], PS[j % 4][:, :], ACT.Copy).then_inc(sem("htok_ev"), 1)
            for j in range(4):
                act.wait_ge(*reached("km_mm", j + 1))
                act.activation(kmT[:, j, :], PS[j][:, 0:TC], ACT.Copy).then_inc(sem("km_ev"), 1)
            for j in range(2):
                act.wait_ge(*reached("vm_mm", j + 1))
                act.activation(Vm[:, j, :], PS[6 + j][:, :], ACT.Copy).then_inc(sem("vm_ev"), 1)

            def xs_copy(i, gathered):
                act.wait_ge(sem("gather_mm"), gathered)
                act.activation(xs[:, 4 * i:4 * i + 4, :], PS[i][:, :].rearrange("p (k s) -> p k s", k=4), ACT.Copy).then_inc(sem("xs_ev"), 1)

            for i in range(2):
                xs_copy(i, i + 1)
            with act.Fori(0, NPAIR) as pair:
                for e in range(2):
                    act.wait_ge(sem("moe_mm"), pair * 6 + (2 * e + 1))
                    act.wait_ge(sem("hid_v"), pair * 2 + (e + 1))
                    act.activation(sg[:, e, :], PS[2 * e][:, :], ACT.Silu).then_inc(sem("sg_s"), 1)
                act.wait_ge(sem("tr_mm"), pair * 2 + 1)
                act.activation(hidT[:, 0, :, :], PS[4][:, :].rearrange("p (i s) -> p i s", i=4), ACT.Copy).then_inc(sem("hidT_ev"), 1)
                for i in range(2):
                    xs_copy(i, pair * 2 + (3 + i))
                act.wait_ge(sem("tr_mm"), pair * 2 + 2)
                act.activation(hidT[:, 1, :, :], PS[5][:, :].rearrange("p (i s) -> p i s", i=4), ACT.Copy).then_inc(sem("hidT_ev"), 1)
                act.wait_ge(sem("gt_mm"), pair + 1)
                act.activation(GT, PS[4][:, :], ACT.Copy).then_inc(sem("gt_ev"), 1)
                act.wait_ge(sem("moe_mm"), pair * 6 + 5)
                act.activation(ypair[:, 0:512], PS[6][:, :], ACT.Copy).then_inc(sem("y0_ev"), 1)

            act.wait_ge(sem("sc_mm"), 8 * (NPAIR + 1))
            wide_squares(act, "nf", lambda k: act.wait_ge(sem("sc_v"), 8 * (NPAIR + 1) + k + 1), 4)
            wide_squares(act, "n3", lambda k: act.wait_ge(sem("rms_out"), norm_out("nf", k)), 4)
            for j in range(4):
                act.wait_ge(*reached("glu_mm", j + 1))
                act.activation(sgT[:, j, :], PS[j][:, :], ACT.Sigmoid).then_inc(sem("glu_ev"), 1)
            for j in range(4):
                act.wait_ge(*reached("v2_mm", j + 1))
                if j == 0:
                    act.wait_ge(sem("u_v"), 5)
                act.activation(V2[:, j, :, :], PS[j][:, :].rearrange("p (h d) -> p h d", h=FOX_H), ACT.Copy).then_inc(sem("v2_ev"), 1)
            thin_copy(3, thin, PS[6][:, :])
            for name, dst, b0 in (("q2", q2, 4), ("k2", k2, 0)):
                for j in range(4):
                    act.wait_ge(*reached(f"{name}_mm", j + 1))
                    act.activation(dst[:, j, :], PS[b0 + j][:, :], ACT.Copy).then_inc(sem(f"{name}_ev"), 1)
            act.wait_ge(sem("f_v"), 1)
            act.activation(f_abs, f_tok, ACT.Abs).then_inc(sem("f_s"), 1)
            act.wait_ge(sem("f_s"), 1)
            act.activation(f_abs, f_abs, ACT.Exp, scale=-1.0).then_inc(sem("f_s"), 1)
            act.wait_ge(sem("f_s"), 2)
            act.activation(f_ln, f_abs, ACT.Ln, bias=1.0).then_inc(sem("f_s"), 1)
            for k in range(KH):
                act.wait_ge(sem("ln_v"), k + 1)
                if k >= 2:
                    act.wait_ge(sem("lnq_mm"), k - 1)
                act.activation(sq[:, k % 2, :], cT[:, k, :], ACT.Square).then_inc(sem("ln_sq"), 1)
            act.wait_ge(sem("lnq_mm"), KH)
            act.activation(std[:, 0:T], PS[5][:, :], ACT.Sqrt, bias=small[:, 40:41], scale=1.0 / HALF).then_inc(sem("ln_std"), 1)
            for k in range(KH):
                act.wait_ge(sem("ln_v"), KH + 2 + k)
                act.activation(cT[:, k, :], cT[:, k, :], ACT.Silu, bias=v("ln_b", k)).then_inc(sem("c_ready"), 1)

            def cb_copy(hp):
                for e in range(2):
                    act.wait_ge(sem("cb_mm"), 2 * hp + e + 1)
                    if e == 0 and hp:
                        act.wait_ge(sem("L_v"), 24 * hp)
                    act.activation(cb[:, e, :], PS[6 + e][:, :], ACT.Copy).then_inc(sem("cb_ev"), 1)

            def probs(hp):
                for i in range(TT):
                    for e in range(2):
                        n = 8 * hp + 2 * i + e
                        w = 128 * (i + 1)
                        c = 1280 * e + 64 * i * (i + 1)
                        p_ = Pbuf[hp % 2][:, c:c + w]
                        act.wait_ge(sem("L_v"), 3 * (n + 1))
                        act.activation(p_, p_, ACT.Exp, bias=nmax[:, n:n + 1], accum_out=psum_[:, n:n + 1]).then_inc(sem("exp_s"), 1)
                        if n:
                            scale_probs(n - 1)

            def scale_probs(n):
                hp, i, e = n // 8, n % 8 // 2, n % 2
                c = 1280 * e + 64 * i * (i + 1)
                p_ = Pbuf[hp % 2][:, c:c + 128 * (i + 1)]
                act.wait_ge(sem("prec_v"), n + 1)
                act.activation(p_, p_, ACT.Copy, scale=prec[:, n:n + 1]).then_inc(sem("P_ready"), 1)

            def gate_c(j):
                act.wait_ge(sem("gcm"), j + 1)
                act.activation(merged[:, j, :], PS[4 + j % 2][:, :], ACT.Sigmoid).then_inc(sem("gc_ev"), 1)

            cb_copy(0)
            probs(0)
            for hp in range(FOX_H // 2):
                if hp + 1 < FOX_H // 2:
                    cb_copy(hp + 1)
                    probs(hp + 1)
                else:
                    scale_probs(FOX_H * TT - 1)
                gate_c(2 * hp)
                gate_c(2 * hp + 1)
                for e in range(2):
                    for t in range(TT):
                        n = 8 * hp + 4 * e + t
                        act.wait_ge(sem("PT_mm"), n + 1)
                        if t == 0 and n:
                            act.wait_ge(sem("pv2_mm"), 2 * hp + e)
                        c = (0, 512, 896, 1152)[t]
                        act.activation(PT2[:, c:c + 512 - 128 * t], PS[6 + t % 2][:, 128 * t:512], ACT.Copy).then_inc(sem("PT_ev"), 1)
                act.wait_ge(sem("pv2_mm"), 2 * hp + 2)
                act.activation(q2[:, hp, :], PS[5][:, :], ACT.Copy).then_inc(sem("attn_ev"), 1)
            for j in range(8):
                act.wait_ge(*reached("gam", j + 1))
                if j == 0:
                    act.wait_ge(sem("pv2_mm"), FOX_H)
                act.activation(sigA[:, j, :], PS[4 + j % 4][:, :], ACT.Sigmoid).then_inc(sem("ga_ev"), 1)
            act.wait_ge(sem("ab_v"), 16)
            wide_squares(act, "n4", lambda k: act.wait_ge(sem("x3"), k + 1), 4)
            for j in range(4):
                act.wait_ge(*reached("xq_mm", j + 1))
                act.activation(q2[:, j, :], PS[j][:, :], ACT.Copy).then_inc(sem("xq_ev"), 1)
            for h in range(4):
                for i in range(TT):
                    n = 4 * h + i
                    act.wait_ge(sem("xmax_v"), 2 * h + 2)
                    act.activation(Px[:, h, i, :], PS[2 * h % 8 + i // 2][:, 256 * (i % 2):256 * (i % 2) + 256], ACT.Exp, scale=QK_SCALE,
                                   bias=xmax[:, h, i:i + 1], accum_out=xsum[:, h, i:i + 1]).then_inc(sem("xexp_s"), 1)
            for h in range(4):
                for i in range(TT):
                    act.wait_ge(sem("xrec_v"), 1)
                    act.activation(Px[:, h, i, :], Px[:, h, i, :], ACT.Copy, scale=xrec[:, h, i:i + 1]).then_inc(sem("xP_ready"), 1)
            for h in range(4):
                for m in range(2):
                    act.wait_ge(sem("xT2_mm"), 2 * h + m + 1)
                    act.activation(PTx[:, h, m, :], PS[2 * (h % 2) + m][:, :], ACT.Copy).then_inc(sem("xT2_ev"), 1)
            wide_squares(act, "n5", lambda k: act.wait_ge(sem("x4"), k + 1), 4)
            thin_copy(4, thin, PS[6][:, :])
            act.wait_ge(sem("g_v"), 3)
            act.activation(rt["gexp"], rt["gexp"], ACT.Exp).then_inc(sem("g_s"), 1)

            def h2_copy(j):
                act.wait_ge(*reached("h2_mm", j + 1))
                c = 512 * (j % 2)
                act.activation(h2_all[:, j // 2, c:c + 512], PS[j % 4][:, :], ACT.Copy).then_inc(sem("h2_full"), 1)
                act.activation(h2_high[:, j // 2, c:c + 512], PS[j % 4][:, :], ACT.Copy).then_inc(sem("h2_ev"), 1)

            for j in range(4):
                h2_copy(j)
            act.wait_ge(sem("g_v"), 14)
            act.activation(rt["p"], rt["p"], ACT.Exp).then_inc(sem("g_s"), 1)
            for j in range(4, 8):
                h2_copy(j)

            def x_rows_copy(i, gathered):
                act.wait_ge(sem("b_gather"), gathered)
                act.activation(x_rows[:, 512 * i:512 * (i + 1)], PS[i][:, :], ACT.Copy).then_inc(sem("b_x_rows"), 1)

            def xb_copy(i, turned):
                act.wait_ge(sem("b_turn_x"), turned)
                act.activation(xb[:, 4 * i:4 * i + 4, :], PS[i][:, :].rearrange("p (k s) -> p k s", k=4), ACT.Copy).then_inc(sem("b_x"), 1)

            for i in range(2):
                x_rows_copy(i, i + 1)
            for i in range(2):
                xb_copy(i, i + 1)
            with act.Fori(0, NPAIR2 // 2) as step2:
                for odd in range(2):
                    pair = step2 * 2 + odd
                    act.wait_ge(sem("b_turn_g"), pair + 1)
                    act.activation(unused, PS[5][:, :].rearrange("p (t s) -> p t s", t=TT), ACT.Copy, accum_out=w_slot[odd]).then_inc(sem("b_w"), 1)
                    act.wait_ge(sem("b_gate_up"), pair + 1)
                    act.activation(sgb, PS[2][:, 0:FF], ACT.Silu).then_inc(sem("b_silu"), 1)
                    for i in range(2):
                        x_rows_copy(i, step2 * 4 + (3 + 2 * odd + i))
                    act.wait_ge(sem("b_turn"), pair + 1)
                    act.activation(hbT, PS[5][:, 0:FF].rearrange("p (i s) -> p i s", i=2), ACT.Copy).then_inc(sem("b_hidT"), 1)
                    for i in range(2):
                        xb_copy(i, step2 * 4 + (3 + 2 * odd + i))
                    act.wait_ge(sem("b_w"), pair + 1)
                    for half in range(2):
                        act.wait_ge(sem("b_down"), step2 * 4 + (2 * odd + half + 1))
                        act.activation(y_high[:, 512 * half:512 * (half + 1)], PS[6 + half][:, :], ACT.Copy, scale=w_slot[odd]).then_inc(sem("b_y_high"), 1)
            wide_squares(act, "n6", lambda k: act.wait_ge(sem("x5"), 8 * (NPAIR2 + 1) + k + 1), 4)
            for j in range(8):
                act.wait_ge(*reached("ot_mm", j + 1))
                act.activation(out_tok[:, j // 2, 512 * (j % 2):512 * (j % 2) + 512], PS[j % 4][:, :], ACT.Copy).then_inc(sem("ot_ev"), 1)

        @block.vector
        def _(dve):
            nc.vector.memset(silu_c[:, :, :], 0.0).then_inc(sem("zeros_ready"), 1)
            nc.vector.memset(small[:, :], 0.0).then_inc(sem("boot"), 1)
            dve.wait_ge(sem("boot"), 1)
            nc.vector.memset(small[:, 40:41], EPS).then_inc(sem("boot"), 1)
            nc.vector.memset(Vx[:, :, :, 128:129], 1.0).then_inc(sem("boot"), 1)
            nc.vector.memset(Mrow[:, :], 0.0).then_inc(sem("boot"), 1)
            dve.wait_ge(sem("const_in"), 16)
            for j in range(4):
                dve.wait_ge(*reached("cT_mm", j + 1))
                nc.vector.tensor_copy(ctxT[:, 2 * j:2 * j + 2, :], PS[4 + j][:, :].rearrange("p (k t) -> p k t", k=2)).then_inc(sem("cT_ev"), 1)
            dve.wait_ge(*reached("vec_mm", 1))
            nc.vector.tensor_copy(vec[:, :], PS[7][:, 0:NVEC]).then_inc(sem("vec_ready"), 1)

            def ada(s, part):
                dve.wait_ge(sem("ada_mm"), s + 1)
                nc.vector.tensor_copy(part[:, s % 2, :], PS[4 + s % 2][:, :]).then_inc(sem("ada_ev"), 1)

            def ada_bias(s):
                dve.wait_ge(sem("ada_t"), s + 1)
                for i in range(2):
                    nc.vector.tensor_tensor(mods[:, 4 * s:4 * s + 4, i], PS[6 + s % 2][:, 0:8].rearrange("p (c m) -> p c m", m=2)[:, :, i],
                                            v("b_ada", 4 * s, 4), ALU.add).then_inc(sem("mods"), 1)

            def root_inverse(name, width, std_, rstd_):
                dve.wait_ge(sem("rms_std"), NORMS[name] + 1)
                nc.vector.reciprocal(rstd_, std_).then_inc(sem("rstd"), 1)

            ada(0, ada_part0)
            ada(1, ada_part0)
            ada_bias(0)
            root_inverse("nc", TC, std[:, T:T + TC], rstd[:, T:T + TC])
            ada(2, ada_part0)
            ada_bias(1)
            ada(3, ada_part0)
            ada_bias(2)
            ada_bias(3)
            dve.wait_ge(sem("mods"), 8)
            for i in range(2):
                nc.vector.scalar_tensor_tensor(out=gains[:, i, :], in0=mods[:, 8:16, i], scalar=1.0, in1=v("g_norm1", 0, KD),
                                               op0=ALU.add, op1=ALU.mult).then_inc(sem("gains1"), 1)
            dve.wait_ge(sem("gains1"), 2)
            for name, src, c, width, i in (("nc", ctxT, T, TC, 1), ("n1", xT, 0, T, 0)):
                if name == "n1":
                    root_inverse("n1", T, std[:, 0:T], rstd[:, 0:T])
                    dve.wait_ge(sem("rms_out"), KD + 1)
                dve.wait_ge(sem("rstd"), NORMS[name] + 1)
                dve.sem_inc(sem("rms_out"), 1)
                for k in range(KD):
                    nc.vector.scalar_tensor_tensor(out=H[:, k, c:c + width], in0=src[:, k, :], scalar=gains[:, i, k:k + 1], in1=rstd[:, c:c + width],
                                                   op0=ALU.mult, op1=ALU.mult).then_inc(sem("rms_out"), 1)

            def conv(name, j, bank, taps, width, height, tile, silu_free):
                a = acc[:, j % 2, 0:width * height].rearrange("p (r c) -> p r c", r=height)
                s = bank[:, 0:width * height].rearrange("p (r c) -> p r c", r=height)
                if silu_free:
                    dve.wait_ge(*silu_free)
                order = [(0, 0)] + [t for t in taps if t != (0, 0)]
                for i, (dy, dx) in enumerate(order):
                    w = v("conv2d", 8 * (3 * (dy + 1) + dx + 1) + tile)
                    r0, r1, c0, c1 = max(0, -dy), height - max(0, dy), max(0, -dx), width - max(0, dx)
                    if i == 0:
                        nc.vector.tensor_scalar(a, s, w, None, ALU.mult).then_inc(sem(name), 1)
                    else:
                        dve.wait_ge(sem(name), conv.done)
                        nc.vector.scalar_tensor_tensor(out=a[:, r0:r1, c0:c1], in0=s[:, r0 + dy:r1 + dy, c0 + dx:c1 + dx], scalar=w,
                                                       in1=a[:, r0:r1, c0:c1], op0=ALU.mult, op1=ALU.add).then_inc(sem(name), 1)
                    conv.done += 1

            taps3 = [(0, -1), (0, 0), (0, 1)]
            taps9 = [(dy, dx) for dy in (-1, 0, 1) for dx in (-1, 0, 1)]
            conv.done = 0
            for j in range(8):
                dve.wait_ge(*reached("k_mm", j + 1))
                if j < 4:
                    conv("conv_k", j, PS[j], taps3, TC, 1, 4 + j, reached("k_silu", j - 1) if j >= 2 else None)
                else:
                    conv("conv_k", j, PS[j - 4], taps9, GRID_W, ROWS, j, reached("k_silu", j - 1))
            nc.vector.memset(Vc[:, :, :, 128:129], 1.0).then_inc(sem("boot"), 1)
            nc.vector.memset(tok_lf, 0.0).then_inc(sem("tok_zero"), 1)
            nc.vector.memset(tok_ig, 0.0).then_inc(sem("tok_zero"), 1)
            dve.wait_ge(sem("tok_zero"), 2)
            dve.wait_ge(*reached("gate_mm", 1))
            nc.vector.tensor_copy(gts, PS[0][:, 0:96].rearrange("p (t e c h) -> p t e c h", t=TA, e=2, c=2)).then_inc(sem("gate_v"), 1)
            dve.wait_ge(sem("gate_v"), 1)
            f_pre = gts[:, :, :, 1, :]
            nc.vector.tensor_scalar(minf, f_pre, 0.0, None, ALU.min).then_inc(sem("gate_v"), 1)
            nc.vector.tensor_copy(tok_ig[:, :, :, 0:4], gts[:, :, :, 0, :]).then_inc(sem("gate_v"), 1)
            dve.wait_ge(sem("gate_v"), 3)
            dve.wait_ge(sem("gate_s"), 3)
            nc.vector.tensor_tensor(tok_lf[:, :, :, 0:4], minf, lnp, ALU.subtract).then_inc(sem("gate_v"), 1)
            nc.vector.memset(cum_r, 0.0).then_inc(sem("rows_v"), 1)
            nc.vector.memset(zero_r, 0.0).then_inc(sem("rows_v"), 1)
            dve.wait_ge(*reached("rows_mm", 1))
            nc.vector.tensor_copy(lf_r[:, 0:T], PS[0][0:36, :]).then_inc(sem("rows_v"), 1)
            nc.vector.tensor_copy(lf_r[:, T:T + TC], PS[2][0:36, 0:256]).then_inc(sem("rows_v"), 1)
            nc.vector.tensor_copy(ig_r[:, T:T + TC], PS[2][0:36, 256:512]).then_inc(sem("ig_ctx"), 1)
            dve.wait_ge(sem("rows_v"), 4)
            dve.wait_ge(sem("ig_ctx"), 1)

            def scan(rows, view, src, n, c0, init, op0, second):
                a, b = src[rows, c0:c0 + n], second[rows, 0:n] if second is zero_r else second[rows, c0:c0 + n]
                o = view[rows, c0:c0 + n]
                if rows.start:
                    a, b, o = a[:, ::-1], b[:, ::-1], o[:, ::-1]
                return nc.vector.tensor_tensor_scan(o, a, b, init, op0, ALU.add if second is zero_r else op0)

            fwd, bwd = slice(0, 4), slice(32, 36)
            for rows in (fwd, bwd):
                for c0, n in ((0, T), (T, TC)):
                    scan(rows, cum_r, lf_r, n, c0, 0.0, ALU.add, zero_r).then_inc(sem("rows_v"), 1)
            dve.wait_ge(sem("rows_v"), 8)
            dve.wait_ge(sem("rows_s"), 1)
            nc.vector.tensor_tensor(a_r, ig_r, cum_r, ALU.subtract).then_inc(sem("rows_v"), 1)
            dve.wait_ge(sem("rows_v"), 9)
            nc.vector.reduce_max(mend, a_r[:, T:T + TC], AX_X).then_inc(sem("rows_v"), 1)
            dve.wait_ge(sem("rows_v"), 10)
            nc.vector.tensor_scalar(nmend, mend, 0.0, -1.0, ALU.max, ALU.mult).then_inc(sem("rows_v"), 1)
            dve.wait_ge(sem("rows_v"), 11)
            nc.vector.tensor_tensor(m0[0:4], cum_r[0:4, T + TC - 1:T + TC], nmend[0:4], ALU.subtract).then_inc(sem("rows_v"), 1)
            nc.vector.tensor_tensor(m0[32:36], cum_r[32:36, T:T + 1], nmend[32:36], ALU.subtract).then_inc(sem("rows_v"), 1)
            dve.wait_ge(sem("rows_v"), 13)
            for rows in (fwd, bwd):
                scan(rows, Mrow, a_r, T, 0, m0[rows], ALU.max, a_r).then_inc(sem("rows_v"), 1)
            dve.wait_ge(sem("rows_v"), 15)
            nc.vector.tensor_tensor(mm_r, cum_r[:, 0:T], Mrow[:, :], ALU.add).then_inc(sem("rows_v"), 1)
            conv.done = 0
            dve.wait_ge(*reached("k_silu", 8))
            for j in range(4):
                dve.wait_ge(*reached("q_mm", j + 1))
                conv("conv_q", j, PS[j], taps9, GRID_W, ROWS, j, reached("q_silu", j - 1) if j >= 2 else None)
            dve.wait_ge(*reached("tokg_mm", 1))
            nc.vector.tensor_copy(tokg[:, :], PS[3][:, 0:368]).then_inc(sem("tokg_ev"), 1)
            dve.wait_ge(sem("tokg_ev"), 1)
            for t in range(2):
                dve.wait_ge(*reached("kc_mm", t + 1))
                for e in range(2):
                    for h in range(NH):
                        nc.vector.tensor_scalar(kw[:, t, e, h, :], PS[t][:, 128 * h:128 * (h + 1)], wa_t[:, t, 32 * e + h:32 * e + h + 1],
                                                QK_SCALE, ALU.mult, ALU.mult).then_inc(sem("kw_ev"), 1)
            for s in range(4, 12):
                ada(s, ada_part)
                if s > 4:
                    ada_bias(s - 1)
            ada_bias(11)

            def gate_a(j):
                dve.wait_ge(sem("bra_ev"), j + 1)
                nc.vector.tensor_tensor(merged[:, j, :], merged[:, j, :], sig[:, j % 2, :], ALU.mult).then_inc(sem("bra_v"), 1)

            dve.wait_ge(*reached("yf_ev", 8))
            for h in range(NH):
                base = 23 * h
                for e in range(2):
                    dve.wait_ge(sem("dec_s"), 2 * h + e + 1)
                    nc.vector.tensor_tensor(qd[:, e, :], qd[:, e, :], qT[:, h, :], ALU.mult).then_inc(sem("attn_v"), 1)
                for t in range(TT):
                    b = base + 2 + 5 * t
                    if t or h:
                        dve.wait_ge(sem("E_diag"), 4 * h + t)
                    for e in range(2):
                        nc.vector.tensor_scalar(dg[:, e, :], mb[:, e, 128 * t:128 * (t + 1)], a_t[:, t, 32 * e + h:32 * e + h + 1], 0.0,
                                                ALU.subtract, ALU.max).then_inc(sem("attn_v"), 1)
                    dve.wait_ge(sem("E_diag"), 4 * h + t + 1)
                    nc.vector.tensor_tensor(EX[:, :, 128 * t:128 * (t + 1)], EX[:, :, 128 * t:128 * (t + 1)], masks2, ALU.mult).then_inc(sem("attn_v"), 1)
                    dve.wait_ge(sem("attn_v"), b + 3)
                    dve.wait_ge(sem("E_off"), 6 * h + (1, 3, 5, 6)[t])
                    dve.wait_ge(sem("S_mm"), 4 * h + t + 1)
                    if t == 0 and h:
                        dve.wait_ge(sem("pv_mm"), 4 * h)
                    nc.vector.scalar_tensor_tensor(out=PT[:, t, 0, 128 * t:T], in0=PS[2 + t % 2][:, 128 * t:T], scalar=QK_SCALE, in1=EX[:, 0, 128 * t:T],
                                                   op0=ALU.mult, op1=ALU.mult).then_inc(sem("attn_v"), 1)
                    nc.vector.scalar_tensor_tensor(out=PT[:, t, 1, 0:128 * (t + 1)], in0=PS[2 + t % 2][:, 0:128 * (t + 1)], scalar=QK_SCALE,
                                                   in1=EX[:, 1, 0:128 * (t + 1)], op0=ALU.mult, op1=ALU.mult).then_inc(sem("attn_v"), 1)
                    if t == 1:
                        gate_a(2 * h)
                    if t == 3:
                        gate_a(2 * h + 1)
                for t in range(TT):
                    o = PS[PV_BANKS[t]][:, 0:258].rearrange("p (e d) -> p e d", e=2)
                    dve.wait_ge(sem("pv_mm"), 4 * h + t + 1)
                    g = 6 * (4 * h + t)
                    if t == 0 and h:
                        dve.wait_ge(sem("hmT_mm"), h)
                    nc.vector.tensor_scalar(den[:, t, :], o[:, :, 128], -1.0, None, ALU.mult).then_inc(sem("pv_v"), 1)
                    dve.wait_ge(sem("pv_v"), g + 1)
                    nc.vector.tensor_tensor(dn[:, t, :], den[:, t, :], enm_t[:, t, h::32], ALU.max).then_inc(sem("pv_v"), 1)
                    dve.wait_ge(sem("pv_v"), g + 2)
                    nc.vector.tensor_tensor(dn[:, t, :], dn[:, t, :], o[:, :, 128], ALU.max).then_inc(sem("pv_v"), 1)
                    dve.wait_ge(sem("pv_v"), g + 3)
                    nc.vector.reciprocal(rec[:, t, :], dn[:, t, :]).then_inc(sem("pv_v"), 1)
                    dve.wait_ge(sem("pv_v"), g + 4)
                    nc.vector.tensor_scalar(hm[:, t, :], o[:, 0, 0:128], rec[:, t, 0:1], None, ALU.mult).then_inc(sem("pv_v"), 1)
                    dve.wait_ge(sem("pv_v"), g + 5)
                    nc.vector.scalar_tensor_tensor(out=hm[:, t, :], in0=o[:, 1, 0:128], scalar=rec[:, t, 1:2], in1=hm[:, t, :],
                                                   op0=ALU.mult, op1=ALU.add).then_inc(sem("pv_v"), 1)
                dve.wait_ge(sem("hmT_mm"), h + 1)
                dve.wait_ge(*reached("o_ev", 4))
                nc.vector.tensor_tensor(qT[:, h, :], oT[:, h, :], PS[5][:, :], ALU.mult).then_inc(sem("attn_v"), 1)
            dve.wait_ge(sem("attn_v"), 23 * NH)
            for j in range(4):
                dve.wait_ge(*reached("mT_mm", j + 1))
                nc.vector.tensor_copy(memT[:, 2 * j:2 * j + 2, :], PS[j][:, :].rearrange("p (k t) -> p k t", k=2)).then_inc(sem("mT_ev"), 1)
            rms_scale(dve, "nm", lambda k: memT[:, k, :], lambda k: H[:, k, T:T + TC], TC, std[:, T:T + TC], rstd2[:, T:T + TC], lambda k: v("mem", k))
            for j in range(8):
                dve.wait_ge(*reached("brb_ev", j + 1))
                dve.wait_ge(*reached("ym_ev", j + 1))
                nc.vector.tensor_tensor(sig[:, j % 2, :], sig[:, j % 2, :], ymT[:, j, :], ALU.mult).then_inc(sem("brb_v"), 1)
                dve.wait_ge(sem("brb_v"), 2 * j + 1)
                nc.vector.tensor_tensor(merged[:, j, :], merged[:, j, :], sig[:, j % 2, :], ALU.add).then_inc(sem("brb_v"), 1)
            for j in range(8):
                dve.wait_ge(*reached("wo_mm", j + 1))
                nc.vector.scalar_tensor_tensor(out=xT[:, j, :], in0=PS[j % 4][:, :], scalar=mods[:, 16 + j, 0:1], in1=xT[:, j, :],
                                               op0=ALU.mult, op1=ALU.add).then_inc(sem("x1"), 1)
            nc.vector.scalar_tensor_tensor(out=gains[:, 2, :], in0=mods[:, 32:40, 0], scalar=1.0, in1=v("g_norm2", 0, KD),
                                           op0=ALU.add, op1=ALU.mult).then_inc(sem("gains2"), 1)
            dve.wait_ge(sem("gains2"), 1)
            rms_scale(dve, "n2", lambda k: xT[:, k, :], lambda k: H[:, k, 0:T], T, std[:, 0:T], rstd2[:, 0:T], lambda k: gains[:, 2, k:k + 1])
            nc.vector.memset(R1[:, 64:208], 0.0).then_inc(sem("r_zero"), 1)
            nc.vector.memset(zrow, 0.0).then_inc(sem("r_zero"), 1)
            nc.vector.memset(R7[:, 0:3584], 0.0).then_inc(sem("r_zero"), 1)
            dve.wait_ge(sem("r_zero"), 3)
            dve.wait_ge(*reached("logit_mm", 1))
            lg = PS[5][:, 0:64].rearrange("p (t e) -> p t e", t=TT)
            nc.vector.reduce_max(lmax, lg, AX_X).then_inc(sem("aff_v"), 1)
            dve.wait_ge(sem("aff_v"), 1)
            nc.vector.tensor_tensor(logit, lg, lmax.unsqueeze(2).broadcast_to([P, TT, NE]), ALU.subtract).then_inc(sem("aff_v"), 1)
            dve.wait_ge(sem("aff_s"), 1)
            nc.vector.reduce_sum(lsum, logit, AX_X).then_inc(sem("aff_v"), 1)
            dve.wait_ge(sem("aff_v"), 3)
            nc.vector.reciprocal(linv, lsum).then_inc(sem("aff_v"), 1)
            dve.wait_ge(sem("aff_v"), 4)
            nc.vector.tensor_tensor(aff[:, :, 0:NE], logit, linv.unsqueeze(2).broadcast_to([P, TT, NE]), ALU.mult).then_inc(sem("aff_v"), 1)
            dve.wait_ge(*reached("affT_mm", 1))
            nc.vector.tensor_copy(work, PS[6][0:NE, :]).then_inc(sem("top_v"), 1)
            for i in range(CAP // 8):
                dve.wait_ge(sem("top_v"), 2 * i + 1)
                nc.vector.max(top8, work).then_inc(sem("top_v"), 1)
                dve.wait_ge(sem("top_v"), 2 * i + 2)
                nc.vector.match_replace(work, top8, work, -1.0).then_inc(sem("top_v"), 1)
            n = 2 * (CAP // 8) + 1
            dve.wait_ge(sem("top_v"), n)
            nc.vector.tensor_scalar(taken, work, -1.0, None, ALU.is_equal).then_inc(sem("top_v"), 1)
            dve.wait_ge(sem("top_v"), n + 1)
            nc.vector.tensor_tensor_scan(work, taken, zrow, 0.0, ALU.add, ALU.add).then_inc(sem("top_v"), 1)
            dve.wait_ge(sem("top_v"), n + 2)
            nc.vector.tensor_tensor(taken, taken, work, ALU.mult).then_inc(sem("top_v"), 1)
            dve.wait_ge(*reached("slotT_mm", 1))
            nc.vector.tensor_copy(slot_t[:, :, 0:NE], PS[7][:, 0:64].rearrange("p (t e) -> p t e", t=TT)).then_inc(sem("slot_ready"), 1)
            dve.wait_ge(sem("slot_ready"), 1)

            def pick_slots(pair):
                nc.vector.tensor_tensor(selc, iota.unsqueeze(1).unsqueeze(1).broadcast_to([P, TT, 2, CAP]),
                                        slot_t[:, :, bass.ds(pair * 2, 2)].unsqueeze(3).broadcast_to([P, TT, 2, CAP]), ALU.is_equal).then_inc(sem("sel_v"), 1)

            def weigh_slots(pair):
                nc.vector.tensor_tensor(gc, selc, aff[:, :, bass.ds(pair * 2, 2)].unsqueeze(3).broadcast_to([P, TT, 2, CAP]), ALU.mult).then_inc(sem("gc_v"), 1)

            pick_slots(0)
            dve.wait_ge(sem("sel_v"), 1)
            weigh_slots(0)
            for name, times in (("hid_v", 2), ("sc_v", 8), ("y1_ev", 1), ("sg_s", 2), ("gt_ev", 1), ("y0_ev", 1)):
                for i in range(times):
                    dve.sem_inc(sem(name), 1)

            def scatter(j, mm):
                dve.wait_ge(sem("sc_mm"), mm)
                nc.vector.scalar_tensor_tensor(out=xT[:, j, :], in0=PS[2 + j % 2][:, :], scalar=mods[:, 40 + j, 0:1], in1=xT[:, j, :],
                                               op0=ALU.mult, op1=ALU.add).then_inc(sem("sc_v"), 1)

            with dve.Fori(0, NPAIR) as pair:
                dve.wait_ge(sem("gc_v"), pair + 1)
                dve.wait_ge(sem("gather_mm"), pair * 2 + 2)
                pick_slots(pair + 1)
                for e in range(2):
                    dve.wait_ge(sem("sg_s"), pair * 2 + (3 + e))
                    dve.wait_ge(sem("moe_mm"), pair * 6 + (2 * e + 2))
                    nc.vector.tensor_tensor(hid[:, e, :], sg[:, e, :], PS[2 * e + 1][:, :], ALU.mult).then_inc(sem("hid_v"), 1)
                    if e == 0:
                        for j in range(KD):
                            scatter(j, pair * 8 + (j + 1))
                dve.wait_ge(sem("gt_mm"), pair + 1)
                dve.wait_ge(sem("sel_v"), pair + 2)
                weigh_slots(pair + 1)
                dve.wait_ge(sem("moe_mm"), pair * 6 + 6)
                nc.vector.tensor_copy(ypair[:, 512:1024], PS[7][:, :]).then_inc(sem("y1_ev"), 1)
            for j in range(KD):
                scatter(j, 8 * NPAIR + j + 1)

            dve.wait_ge(sem("sc_v"), 8 * (NPAIR + 2))
            rms_scale(dve, "nf", lambda k: xT[:, k, :], lambda k: xT[:, k, :], T, std[:, 0:T], rstd2[:, 0:T], lambda k: v("g_final", k))
            rms_scale(dve, "n3", lambda k: xT[:, k, :], lambda k: H[:, k, 0:T], T, std[:, 0:T], rstd2[:, 0:T], lambda k: v("mix", k))
            nc.vector.memset(u_pad[:, :, 0:TAPS - 1], 0.0).then_inc(sem("u_v"), 1)
            for j in range(KH):
                dve.wait_ge(*reached("a_mm", j + 1))
                dve.wait_ge(*reached("glu_ev", j + 1))
                nc.vector.tensor_tensor(u_pad[:, j, TAPS - 1:], PS[4 + j][:, :], sgT[:, j, :], ALU.mult).then_inc(sem("u_v"), 1)
            dve.wait_ge(sem("u_v"), 5)
            for tap in range(TAPS):
                for k in range(KH):
                    if tap == 0:
                        nc.vector.tensor_scalar(cT[:, k, :], u_pad[:, k, 0:T], v("dw_w", k), v("dw_b", k), ALU.mult, ALU.add).then_inc(sem("dw_v"), 1)
                    else:
                        dve.wait_ge(sem("dw_v"), KH * (tap - 1) + k + 1)
                        nc.vector.scalar_tensor_tensor(out=cT[:, k, :], in0=u_pad[:, k, tap:tap + T], scalar=v("dw_w", KH * tap + k), in1=cT[:, k, :],
                                                       op0=ALU.mult, op1=ALU.add).then_inc(sem("dw_v"), 1)
            dve.wait_ge(*reached("f_mm", 1))
            nc.vector.tensor_copy(f_tok, PS[7][:, 0:32].rearrange("p (t h) -> p t h", t=TT)).then_inc(sem("f_v"), 1)
            dve.wait_ge(sem("f_v"), 1)
            nc.vector.memset(zero8, 0.0).then_inc(sem("f_v"), 1)
            dve.wait_ge(sem("f_s"), 3)
            nc.vector.tensor_scalar(f_tok, f_tok, 0.0, None, ALU.min).then_inc(sem("f_v"), 1)
            dve.wait_ge(sem("f_v"), 3)
            nc.vector.tensor_tensor(f_tok, f_tok, f_ln, ALU.subtract).then_inc(sem("f_v"), 1)
            dve.wait_ge(*reached("fT_mm", 1))
            nc.vector.tensor_copy(f_row, PS[6][0:FOX_H, :]).then_inc(sem("f_v"), 1)
            dve.wait_ge(sem("f_v"), 5)
            nc.vector.tensor_tensor_scan(c_row[0:FOX_H, :], f_row, zero8, 0.0, ALU.add, ALU.add).then_inc(sem("c_v"), 1)
            dve.wait_ge(*reached("lnm_mm", 1))
            for k in range(KH):
                nc.vector.scalar_tensor_tensor(out=cT[:, k, :], in0=PS[4][:, :], scalar=-1.0 / HALF, in1=cT[:, k, :], op0=ALU.mult, op1=ALU.add).then_inc(sem("ln_v"), 1)
            dve.wait_ge(sem("ln_std"), 1)
            nc.vector.reciprocal(rstd2[:, 0:T], std[:, 0:T]).then_inc(sem("ln_v"), 1)
            dve.wait_ge(sem("ln_v"), KH + 1)
            for k in range(KH):
                nc.vector.scalar_tensor_tensor(out=cT[:, k, :], in0=cT[:, k, :], scalar=v("ln_g", k), in1=rstd2[:, 0:T], op0=ALU.mult, op1=ALU.mult).then_inc(sem("ln_v"), 1)
            dve.wait_ge(*reached("c_ready", KH))

            def sum_recip(n):
                dve.wait_ge(sem("exp_s"), n + 1)
                nc.vector.reciprocal(prec[:, n:n + 1], psum_[:, n:n + 1]).then_inc(sem("prec_v"), 1)

            for hp in range(FOX_H // 2):
                for i in range(TT):
                    for e in range(2):
                        n = 8 * hp + 2 * i + e
                        w = 128 * (i + 1)
                        c = 1280 * e + 64 * i * (i + 1)
                        L = Pbuf[hp % 2][:, c:c + w]
                        dve.wait_ge(sem("S2_mm"), 4 * hp + i + 1)
                        dve.wait_ge(sem("cb_ev"), 2 * (hp + 1))
                        if i == 0 and e == 0 and hp >= 2:
                            dve.wait_ge(sem("PT_mm"), 8 * (hp - 1))
                        nc.vector.scalar_tensor_tensor(out=L, in0=PS[2 * (i % 2) + e][:, 0:w], scalar=FOX_SCALE, in1=cb[:, e, 0:w],
                                                       op0=ALU.mult, op1=ALU.subtract).then_inc(sem("L_v"), 1)
                        dve.wait_ge(sem("L_v"), 3 * n + 1)
                        nc.vector.tensor_tensor(L[:, 128 * i:w], L[:, 128 * i:w], const[:, 512:640], ALU.add).then_inc(sem("L_v"), 1)
                        dve.wait_ge(sem("L_v"), 3 * n + 2)
                        nc.vector.tensor_reduce(nmax[:, n:n + 1], L, AX_X, ALU.max, negate=True).then_inc(sem("L_v"), 1)
                        if n:
                            sum_recip(n - 1)
            sum_recip(FOX_H * TT - 1)
            for j in range(8):
                dve.wait_ge(*reached("pw_mm", j + 1))
                dve.wait_ge(sem("gc_ev"), 8)
                nc.vector.tensor_tensor(merged[:, j, :], merged[:, j, :], PS[j % 4][:, :], ALU.mult).then_inc(sem("pw_v"), 1)
            for j in range(8):
                dve.wait_ge(*reached("ab_mm", j + 1))
                dve.wait_ge(*reached("ga_ev", 8))
                if j >= 2:
                    dve.wait_ge(sem("ab_v"), 2 * (j - 1))
                else:
                    dve.wait_ge(sem("P_ready"), FOX_H * TT)
                nc.vector.tensor_tensor(tmp2[:, j % 2, :], sigA[:, j, :], PS[j % 4][:, :], ALU.mult).then_inc(sem("ab_v"), 1)
                dve.wait_ge(sem("ab_v"), 2 * j + 1)
                dve.wait_ge(sem("pw_v"), 8)
                nc.vector.tensor_tensor(merged[:, j, :], merged[:, j, :], tmp2[:, j % 2, :], ALU.add).then_inc(sem("ab_v"), 1)

            def residual(name, mm, j, mm_value):
                dve.wait_ge(*reached(mm, mm_value))
                nc.vector.tensor_tensor(xT[:, j, :], xT[:, j, :], PS[j % 4][:, :], ALU.add).then_inc(sem(name), 1)

            for j in range(KD):
                residual("x3", "w2o_mm", j, j + 1)
            dve.wait_ge(sem("x3"), KD)
            rms_scale(dve, "n4", lambda k: xT[:, k, :], lambda k: H[:, k, 0:T], T, std[:, 0:T], rstd2[:, 0:T], lambda k: v("xa", k))
            for h in range(4):
                for i in range(2):
                    dve.wait_ge(*reached("xS_mm", 2 * h + i + 1))
                    nc.vector.tensor_reduce(xmax[:, h, 2 * i:2 * i + 2], PS[2 * h % 8 + i][:, :].rearrange("p (i m) -> p i m", i=2), AX_X, ALU.max,
                                            negate=True).then_inc(sem("xmx"), 1)
                dve.wait_ge(sem("xmx"), 2 * h + 2)
                nc.vector.tensor_scalar(xmax[:, h, :], xmax[:, h, :], QK_SCALE, None, ALU.mult).then_inc(sem("xmax_v"), 1)
                nc.vector.memset(small[:, 50 + h:51 + h], 0.0).then_inc(sem("xmax_v"), 1)
            dve.wait_ge(sem("xexp_s"), 16)
            nc.vector.reciprocal(xrec, xsum).then_inc(sem("xrec_v"), 1)
            for h in range(4):
                dve.wait_ge(sem("xo_pv"), h + 1)
                nc.vector.tensor_copy(k2[:, h, :], PS[4 + h % 4][:, :]).then_inc(sem("ox_ev"), 1)
            for j in range(KD):
                residual("x4", "xo_mm", j, j + 1)
            dve.wait_ge(sem("x4"), KD)
            rms_scale(dve, "n5", lambda k: xT[:, k, :], lambda k: H[:, k, 0:T], T, std[:, 0:T], rstd2[:, 0:T], lambda k: v("moe", k))
            chain = [0]

            def step(ins):
                chain[0] += 1
                ins.then_inc(sem("g_v"), 1)
                dve.wait_ge(sem("g_v"), chain[0])

            def tt(o, a, b, op):
                step(nc.vector.tensor_tensor(o, a, b, op))

            def last4(a):
                return a.unsqueeze(2).broadcast_to([P, TT, 4])

            def first_of(dst, x, top, run):
                tt(run, x, last4(top), ALU.is_equal)
                for i in range(1, 4):
                    tt(run[:, :, i], run[:, :, i], run[:, :, i - 1], ALU.max)
                step(nc.vector.tensor_copy(dst[:, :, 0], run[:, :, 0]))
                tt(dst[:, :, 1:4], run[:, :, 1:4], run[:, :, 0:3], ALU.subtract)

            dve.wait_ge(*reached("rl_mm", 1))
            step(nc.vector.tensor_copy(rt["log"], PS[5][:, 0:80].rearrange("p (t n) -> p t n", t=TT)))
            gl = rt["log"][:, :, 0:4]
            el = rt["log"][:, :, 4:20].rearrange("p t (g j) -> p t g j", g=NG)
            step(nc.vector.reduce_max(rt["gmax"], gl, AX_X))
            tt(rt["gexp"], gl, last4(rt["gmax"]), ALU.subtract)
            first_of(rt["gsel"], gl, rt["gmax"], rt["run"])
            tt(rt["mix"], el, rt["gsel"].unsqueeze(3).broadcast_to([P, TT, 4, 4]), ALU.mult)
            step(nc.vector.reduce_sum(rt["esel"], rt["mix"].rearrange("p t g j -> p t j g"), AX_X))
            step(nc.vector.reduce_max(rt["emax"], rt["esel"], AX_X))
            tt(rt["p"], rt["esel"], last4(rt["emax"]), ALU.subtract)
            dve.wait_ge(sem("g_s"), 1)
            step(nc.vector.reduce_sum(rt["gsum"], rt["gexp"], AX_X))
            step(nc.vector.reciprocal(rt["pg"], rt["gsum"]))
            dve.wait_ge(sem("g_s"), 2)
            step(nc.vector.reduce_max(rt["emax"], rt["p"], AX_X))
            first_of(rt["m1"], rt["p"], rt["emax"], rt["run"])
            tt(rt["p2"], rt["p"], rt["m1"], ALU.mult)
            tt(rt["p2"], rt["p"], rt["p2"], ALU.subtract)
            tt(rt["p2"], rt["p2"], rt["m1"], ALU.subtract)
            step(nc.vector.reduce_max(rt["emax"], rt["p2"], AX_X))
            first_of(rt["m2"], rt["p2"], rt["emax"], rt["run"])
            tt(rt["m1"], rt["m1"], rt["m2"], ALU.add)
            tt(rt["p"], rt["p"], rt["m1"], ALU.mult)
            step(nc.vector.reduce_sum(rt["emax"], rt["p"], AX_X))
            step(nc.vector.reciprocal(rt["emax"], rt["emax"]))
            tt(rt["emax"], rt["emax"], rt["pg"], ALU.mult)
            tt(rt["p"], rt["p"], last4(rt["emax"]), ALU.mult)
            tt(rt["comb"], rt["gsel"].unsqueeze(3).broadcast_to([P, TT, 4, 4]), rt["p"].unsqueeze(2).broadcast_to([P, TT, 4, 4]), ALU.mult)
            dve.sem_inc(sem("comb_ready"), 1)
            step(nc.vector.tensor_copy(iota2[:, 0:BLK], iota))
            step(nc.vector.tensor_scalar(iota2[:, BLK:2 * BLK], iota, float(BLK), None, ALU.add))
            step(nc.vector.tensor_scalar(thresh, iota[0:E2, 0:T // BLK], -1.0, float(BLK), ALU.add, ALU.mult))
            dve.wait_ge(*reached("combT_mm", 1))
            nc.vector.tensor_scalar(chosen, PS[6][0:E2, :], 0.0, None, ALU.is_gt).then_inc(sem("chosen"), 1)
            dve.wait_ge(sem("chosen"), 1)
            dve.wait_ge(sem("zeros_by_pool"), 5)
            step(nc.vector.tensor_tensor_scan(place, chosen, full(y_low[0][0:E2, :]), 0.0, ALU.add, ALU.add))
            step(nc.vector.tensor_tensor(over, thresh, place[:, T - 1:T].broadcast_to([E2, T // BLK]), ALU.is_lt))
            nc.vector.reduce_sum(nblk, over, AX_X).then_inc(sem("block_counts"), 1)
            dve.wait_ge(*reached("ends_mm", 1))
            nc.vector.tensor_copy(ends, PS[7][0:E2, 0:1]).then_inc(sem("ends_v"), 1)
            dve.wait_ge(sem("ends_v"), 1)
            nc.vector.tensor_scalar(ended, iota[0:E2, 0:32], ends, None, ALU.is_gt).then_inc(sem("ended"), 1)
            step(nc.vector.tensor_tensor(blk_base, ends, nblk, ALU.subtract))
            step(nc.vector.tensor_scalar(blk_base, blk_base, float(BLK), None, ALU.mult))
            nc.vector.scalar_tensor_tensor(out=place, in0=place, scalar=blk_base, in1=chosen, op0=ALU.add, op1=ALU.mult).then_inc(sem("places"), 1)
            dve.wait_ge(*reached("which_mm", 1))
            nc.vector.tensor_scalar(block_expert[:, :], PS[6][0:1, 0:32], float(E2 - 1), None, ALU.min).then_inc(sem("block_expert"), 1)
            dve.wait_ge(*reached("posT_mm", 1))
            nc.vector.tensor_copy(pos_t, PS[5][:, 0:TT * E2].rearrange("p (t e) -> p t e", t=TT)).then_inc(sem("pos_v"), 1)
            dve.wait_ge(sem("pos_v"), 1)
            comb = rt["comb"].rearrange("p t g j -> p t (g j)")
            step(nc.vector.reduce_max(pos2[:, 0, :], pos_t, AX_X))
            step(nc.vector.reduce_sum(pos2[:, 1, :], pos_t, AX_X))
            tt(pos2[:, 1, :], pos2[:, 1, :], pos2[:, 0, :], ALU.subtract)
            for a in range(2):
                tt(hit_t, pos_t, pos2[:, a, :].unsqueeze(2).broadcast_to([P, TT, E2]), ALU.is_equal)
                tt(hit_t, hit_t, comb, ALU.mult)
                step(nc.vector.reduce_sum(wt2[:, a, :], hit_t, AX_X))
            def by_slot(a):
                return a.unsqueeze(2).broadcast_to([P, TT, 2 * BLK])

            def pick_step(i, n):
                if i < 2:
                    nc.vector.tensor_tensor(hits[i], iota2.unsqueeze(1).broadcast_to([P, TT, 2 * BLK]), by_slot(pos2[:, i, :]), ALU.is_equal).then_inc(sem("b_v"), 1)
                else:
                    dve.wait_ge(sem("b_v"), n + 2)
                    nc.vector.tensor_tensor(selb, hits[0], hits[1], ALU.add).then_inc(sem("b_sel"), 1)

            def weigh_blocks(n, done):
                dve.wait_ge(sem("b_sel"), done)
                for a in range(2):
                    nc.vector.tensor_tensor(hits[a], hits[a], by_slot(wt2[:, a, :]), ALU.mult).then_inc(sem("b_v"), 1)
                dve.wait_ge(sem("b_v"), n + 2)
                nc.vector.tensor_tensor(gb, hits[0], hits[1], ALU.add).then_inc(sem("b_gates"), 1)

            dve.sem_inc(sem("b_v"), 1)
            for i in range(3):
                pick_step(i, 1)
            weigh_blocks(3, 1)
            for name, times in (("b_hid", 1), ("b_hidT", 1), ("b_GT", 1), ("x5", 8), ("b_y_low", 2)):
                for i in range(times):
                    dve.sem_inc(sem(name), 1)

            def add_out(j, mm):
                dve.wait_ge(sem("b_scatter"), mm)
                nc.vector.tensor_tensor(xT[:, j, :], xT[:, j, :], PS[3 + j % 2][:, :], ALU.add).then_inc(sem("x5"), 1)

            with dve.Fori(0, NPAIR2 // 2) as step2:
                for odd in range(2):
                    pair = step2 * 2 + odd
                    dve.wait_ge(sem("b_turn_g"), pair + 1)
                    dve.wait_ge(sem("b_w"), pair + 1)
                    nc.vector.tensor_scalar(GTb[odd], PS[5][:, :], 0.0, None, ALU.is_gt).then_inc(sem("b_GT"), 1)
                    dve.wait_ge(sem("b_gates"), pair + 1)
                    nc.vector.tensor_scalar(pos2, pos2, -2.0 * BLK, None, ALU.add).then_inc(sem("b_v"), 1)
                    for j in range(KD):
                        add_out(j, pair * 8 + (j + 1))
                        if j in (1, 3, 5):
                            if j == 1:
                                dve.wait_ge(sem("b_v"), step2 * 10 + (5 * odd + 6))
                            pick_step((j - 1) // 2, step2 * 10 + (5 * odd + 6))
                    dve.wait_ge(sem("b_silu"), pair + 1)
                    nc.vector.tensor_tensor(hb, sgb, PS[2][:, FF:2 * FF], ALU.mult).then_inc(sem("b_hid"), 1)
                    weigh_blocks(step2 * 10 + (5 * odd + 8), pair + 2)
                    for half in range(2):
                        dve.wait_ge(sem("b_y_high"), step2 * 4 + (2 * odd + half + 1))
                        nc.vector.scalar_tensor_tensor(out=y_low[half], in0=PS[6 + half][:, :], scalar=w_slot[odd], in1=full(y_high[:, 512 * half:512 * (half + 1)]),
                                                       op0=ALU.mult, op1=ALU.subtract).then_inc(sem("b_y_low"), 1)
            for j in range(KD):
                add_out(j, 8 * NPAIR2 + j + 1)
            dve.wait_ge(sem("x5"), 8 * (NPAIR2 + 2))
            rms_scale(dve, "n6", lambda k: xT[:, k, :], lambda k: H[:, k, 0:T], T, std[:, 0:T], rstd2[:, 0:T], lambda k: v("final2", k))

        @block.gpsimd
        def _(pool):
            nc.gpsimd.memset(wsmall[:, :, 60:72], 0.0).then_inc(sem("zeros_by_pool"), 1)
            pool.wait_ge(sem("rms_out"), norm_out("n5", KD - 1))
            for a in (y_high, GTb[1], y_low[0], y_low[1]):
                nc.gpsimd.memset(full(a), 0.0).then_inc(sem("zeros_by_pool"), 1)
            for j in range(8):
                pool.wait_ge(*reached("h2_ev", j + 1))
                pool.wait_ge(sem("h2_full"), j + 1)
                c = 512 * (j % 2)
                nc.gpsimd.tensor_tensor(h2_low[:, j // 2, c:c + 512], h2_all[:, j // 2, c:c + 512], full(h2_high[:, j // 2, c:c + 512]), ALU.subtract).then_inc(sem("h2_low"), 1)

        @block.tensor
        def _(pe):
            freed = {}

            def take(bank, s, value):
                if bank in freed:
                    pe.wait_ge(*freed[bank])
                freed[bank] = reached(s, value)
                return PS[bank]

            def product(dst, pairs):
                for i, (lhsT, rhs) in enumerate(pairs):
                    ins = nc.tensor.matmul(dst, lhsT, rhs, start=(i == 0), stop=(i == len(pairs) - 1))
                return ins

            pe.wait_ge(sem("const_in"), 16)
            pe.wait_ge(sem("ctx_in"), 16)
            for j in range(4):
                b = take(4 + j, "cT_ev", j + 1)
                for i in range(4):
                    k, t = 2 * j + i // 2, i % 2
                    ins = nc.tensor.transpose(b[:, 128 * i:128 * (i + 1)], c_tok[:, t, 128 * k:128 * (k + 1)], ident)
                ins.then_inc(sem("cT_mm"), 1)
            rms_sum(pe, "nc", take(1, "rms_std", NORMS["nc"] + 1), sqc, TC)
            pe.wait_ge(sem("x_in"), 16)
            for k in range(KD):
                b = take(k % 4, "xT_ev", k + 1)
                for t in range(TT):
                    ins = nc.tensor.transpose(b[:, 128 * t:128 * (t + 1)], x_tok[:, t, 128 * k:128 * (k + 1)], ident)
                ins.then_inc(sem("xT_mm"), 1)
            pe.wait_ge(sem("vecs_in"), 16 * 16)
            b = take(7, "vec_ready", 1)
            for i, (n, c) in enumerate(((128, 0), (84, 128), (124, 212))):
                ins = nc.tensor.transpose(b[:, c:c + n], vpack[0:n, i, :], ident[0:n, 0:n])
            ins.then_inc(sem("vec_mm"), 1)

            def ada(s):
                w = weights(f"ada{s}", KD)
                wait_weights(pe, f"ada{s}")
                b = take(4 + s % 2, "ada_ev", s + 1)
                for k in range(KD):
                    g = k % 4
                    ins = nc.tensor.matmul(b[32 * g:32 * g + 32, :], silu_c[:, k, :], w[:, k, :], start=(k < 4), stop=(k >= 4),
                                           tile_position=(0, 32 * g))
                ins.then_inc(sem("ada_mm"), 1)

            def ada_sum(s, part):
                pe.wait_ge(sem("ada_ev"), s + 1)
                b = take(6 + s % 2, "mods", 2 * (s + 1))
                for c in range(4):
                    ins = nc.tensor.matmul(b[:, 2 * c:2 * c + 2], part[:, s % 2, 128 * c:128 * (c + 1)], pick, start=True, stop=True)
                ins.then_inc(sem("ada_t"), 1)

            pe.wait_ge(sem("silu_c"), 2)
            ada(0)
            ada(1)
            ada_sum(0, ada_part0)
            ada(2)
            ada_sum(1, ada_part0)
            ada(3)
            ada_sum(2, ada_part0)
            ada_sum(3, ada_part0)
            wide_sum(pe, "n1", take(PART_BANK, "rms_part", WIDE["n1"]), take(0, "rms_std", NORMS["n1"] + 1))
            w = weights("k", KD)
            wait_weights(pe, "k")
            for j in range(8):
                b = take(j % 4, "conv_k", 3 * (j + 1) if j < 4 else 12 + 9 * (j - 3))
                c = 128 * (j % 4)
                toks = slice(T, T + TC) if j < 4 else slice(0, T)
                n = TC if j < 4 else T
                pe.wait_ge(sem("h_ready"), KD if j < 4 else 2 * KD)
                product(b[:, 0:n], [(w[:, k, c:c + 128], H[:, k, toks]) for k in range(KD)]).then_inc(sem("k_mm"), 1)
            w = weights("v", KD)
            wait_weights(pe, "v")
            for t in range(TA):
                b = take(4 + t % 4, "v_ev", t + 1)
                product(b[:, :], [(H[:, k, 128 * t:128 * (t + 1)], w[:, k, :]) for k in range(KD)]).then_inc(sem("v_mm"), 1)

            def thin_product(pieces, c0, ready=None):
                for bank, toks in pieces:
                    for k in range(KD):
                        g = k % 4
                        if ready:
                            pe.wait_ge(ready[0], ready[1](k))
                        ins = nc.tensor.matmul(bank[32 * g:32 * g + 32, 0:toks.stop - toks.start], wsmall[:, k, c0:c0 + 32], H[:, k, toks],
                                               start=(k < 4), stop=(k >= 4), tile_position=(0, 32 * g))
                ins.then_inc(sem("thin_mm"), 1)

            def thin_sum(dst, parts, tiles, n, copied, bias=None):
                pe.wait_ge(sem("thin_ev"), copied)
                for t in range(tiles):
                    first = [] if bias is None else [(ones[0:1, :], bias)]
                    ins = product(dst[:, n * t:n * (t + 1)], first + [(parts[:, 128 * t:128 * (t + 1)], fold[:, 0:n])])
                return ins

            pe.wait_ge(sem("zeros_by_pool"), 1)
            pe.wait_ge(sem("wsmall_in"), 80)
            pe.wait_ge(sem("rowb_in"), 64)
            thin_product([(take(6, "thin_ev", 1), slice(0, T)), (take(7, "thin_ev", 2), slice(T, T + TC))], 0)
            w = weights("u", KD)
            wait_weights(pe, "u")
            for j in range(4):
                b = take(4 + j, "u_ev", j + 1)
                product(b[:, :], [(w[:, k, 128 * j:128 * (j + 1)], H[:, k, 0:T]) for k in range(KD)]).then_inc(sem("u_mm"), 1)
            thin_sum(take(0, "gate_v", 1), thin_gates, TA, 16, 2, rowb[0:1, 0:16]).then_inc(sem("gate_mm"), 1)
            pe.wait_ge(sem("gate_v"), 4)
            b0, b1, b2 = take(0, "rows_v", 4), take(1, "rows_s", 1), take(2, "ig_ctx", 1)
            for t in range(TA):
                lf_dst = b0[0:36, 128 * t:128 * (t + 1)] if t < TT else b2[0:36, 128 * (t - TT):128 * (t - TT + 1)]
                ig_dst = b1[0:36, 128 * t:128 * (t + 1)] if t < TT else b2[0:36, 256 + 128 * (t - TT):256 + 128 * (t - TT + 1)]
                nc.tensor.transpose(lf_dst, tok_lf2[:, t, 0:36], ident)
                ins = nc.tensor.transpose(ig_dst, tok_ig2[:, t, 0:36], ident)
            ins.then_inc(sem("rows_mm"), 1)
            pe.wait_ge(sem("rows_v"), 4)
            w = weights("q", KD)
            wait_weights(pe, "q")
            for j in range(4):
                b = take(j, "conv_q", 9 * (j + 1))
                product(b[:, :], [(w[:, k, 128 * j:128 * (j + 1)], H[:, k, 0:T]) for k in range(KD)]).then_inc(sem("q_mm"), 1)
            ada(4)
            ada(5)
            w = weights("o", KD)
            wait_weights(pe, "o")
            for j in range(4):
                b = take(j, "o_ev", j + 1)
                product(b[:, :], [(w[:, k, 128 * j:128 * (j + 1)], H[:, k, 0:T]) for k in range(KD)]).then_inc(sem("o_mm"), 1)
            pe.wait_ge(sem("rows_s"), 3)
            pe.wait_ge(sem("rows_v"), 16)
            b = take(3, "tokg_ev", 1)
            for i, (src, tiles) in enumerate(((a_r, 4), (mm_r, 4), (wa_r, 2))):
                for t in range(tiles):
                    c = 144 * i + 36 * t
                    nc.tensor.transpose(b[:, c:c + 36], src[:, 128 * t:128 * (t + 1)], ident[0:36, 0:36])
            for r in range(8):
                row = 32 * (r // 4) + r % 4
                ins = nc.tensor.matmul(b[:, 360 + r:361 + r], ident[0:36, row:row + 1].broadcast_to([36, 128]), m0, start=True, stop=True)
            ins.then_inc(sem("tokg_mm"), 1)
            pe.wait_ge(*reached("k_silu", 8))
            for t in range(2):
                b = take(t, "kw_ev", 8 * (t + 1))
                for h in range(NH):
                    ins = nc.tensor.transpose(b[:, 128 * h:128 * (h + 1)], kcT[:, h, 128 * t:128 * (t + 1)], ident)
                ins.then_inc(sem("kc_mm"), 1)
            pe.wait_ge(sem("kw_ev"), 16)
            pe.wait_ge(sem("boot"), 5)
            for h in range(NH):
                b = take(2 + h % 2, "C0_ev", h + 1)
                for e in range(2):
                    ins = product(b[:, 129 * e:129 * (e + 1)], [(kw[:, t, e, h, :], Vc[:, t, h, :]) for t in range(2)])
                ins.then_inc(sem("C0_mm"), 1)
            ada_sum(4, ada_part)
            for s in range(6, 12):
                ada(s)
                ada_sum(s - 1, ada_part)
            ada_sum(11, ada_part)
            pe.wait_ge(*reached("u_ev", 4))
            for j in range(8):
                b = take(4 + j % 4, "Z_ev", j + 1)
                for i in range(2):
                    g = 2 * (j % 2) + i
                    ins = nc.tensor.matmul(b[:, 256 * i:256 * (i + 1)], uT[:, g, 128 * (j // 2):128 * (j // 2) + 128], dftF, start=True, stop=True)
                ins.then_inc(sem("Z_mm"), 1)
            w = weights("dft", TT)
            wait_weights(pe, "dft")
            pe.wait_ge(*reached("Z_ev", 8))
            for g in range(4):
                b = take(g, "fu_ev", g + 1)
                product(b[:, :], [(Z[:, t, g, 128 * s:128 * (s + 1)], w[:, t, 512 * s:512 * (s + 1)]) for t in range(TT) for s in range(2)]).then_inc(sem("fu_mm"), 1)
            w = weights("w_fourier", KH)
            wait_weights(pe, "w_fourier")
            pe.wait_ge(*reached("fu_ev", 4))
            for j in range(8):
                b = take(4 + j % 4, "yf_ev", j + 1)
                product(b[:, :], [(w[:, k, 128 * j:128 * (j + 1)], fuT[:, k, :]) for k in range(KH)]).then_inc(sem("yf_mm"), 1)

            def gate_a(j):
                name = f"brA{j // 4}"
                if j % 4 == 0:
                    wait_weights(pe, name)
                w = weights(name, KD)
                b = take(6 + j % 2, "bra_ev", j + 1)
                c = 128 * (j % 4)
                product(b[:, :], [(w[:, k, c:c + 128], H[:, k, 0:T]) for k in range(KD)]).then_inc(sem("bra_mm"), 1)

            pe.wait_ge(*reached("q_silu", 4))
            pe.wait_ge(*reached("C0_ev", 4))
            for h in range(NH):
                for e in range(2):
                    b = take(e, "mb_ev", 2 * h + e + 1)
                    r = 32 * e + h
                    nc.tensor.matmul(b[:, :], ident[0:36, r:r + 1].broadcast_to([36, 128]), Mrow[:, :], start=True, stop=True).then_inc(sem("mb_mm"), 1)
                for t in range(TT):
                    b = take(2 + t % 2, "attn_v", 23 * h + 2 + 5 * (t + 1))
                    nc.tensor.matmul(b[:, :], kT[:, h, 128 * t:128 * (t + 1)], qT[:, h, :], start=True, stop=True).then_inc(sem("S_mm"), 1)
                    if t == 1:
                        gate_a(2 * h)
                    if t == 3:
                        gate_a(2 * h + 1)
                pe.wait_ge(sem("attn_v"), 23 * h + 22)
                for j in range(TT):
                    b = take(PV_BANKS[j], "pv_v", 6 * (4 * h + j + 1))
                    jt = slice(128 * j, 128 * (j + 1))
                    for e in range(2):
                        keys = range(j + 1) if e == 0 else range(j, TT)
                        ins = product(b[:, 129 * e:129 * (e + 1)], [(qd[:, e, jt], C0[:, e, h, :])] +
                                      [(PT[:, t, e, jt], Vx[:, t, h, :]) for t in keys])
                    ins.then_inc(sem("pv_mm"), 1)
                b = take(5, "attn_v", 23 * h + 23)
                pe.wait_ge(sem("pv_v"), 24 * (h + 1))
                for t in range(TT):
                    ins = nc.tensor.transpose(b[:, 128 * t:128 * (t + 1)], hm[:, t, :], ident)
                ins.then_inc(sem("hmT_mm"), 1)
            pe.wait_ge(sem("mem_in"), 16)
            for j in range(4):
                b = take(j, "mT_ev", j + 1)
                for i in range(4):
                    k, t = 2 * j + i // 2, i % 2
                    ins = nc.tensor.transpose(b[:, 128 * i:128 * (i + 1)], m_tok[:, t, 128 * k:128 * (k + 1)], ident)
                ins.then_inc(sem("mT_mm"), 1)
            rms_sum(pe, "nm", take(5, "rms_std", NORMS["nm"] + 1), sqc, TC)
            w = weights("w_mlstm", KH)
            wait_weights(pe, "w_mlstm")
            pe.wait_ge(sem("attn_v"), 23 * 4)
            for j in range(8):
                b = take(j % 4, "ym_ev", j + 1)
                product(b[:, :], [(w[:, k, 128 * j:128 * (j + 1)], qT[:, k, :]) for k in range(KH)]).then_inc(sem("ym_mm"), 1)
            for j in range(8):
                name = f"brB{j // 4}"
                if j % 4 == 0:
                    wait_weights(pe, name)
                w = weights(name, KD)
                b = take(4 + j % 4, "brb_ev", j + 1)
                c = 128 * (j % 4)
                product(b[:, :], [(w[:, k, c:c + 128], H[:, k, 0:T]) for k in range(KD)]).then_inc(sem("brb_mm"), 1)
            pe.wait_ge(sem("brb_v"), 16)
            for j in range(8):
                name = f"wo{j // 4}"
                if j % 4 == 0:
                    wait_weights(pe, name)
                w = weights(name, KD)
                b = take(j % 4, "x1", j + 1)
                c = 128 * (j % 4)
                product(b[:, :], [(w[:, k, c:c + 128], merged[:, k, :]) for k in range(KD)]).then_inc(sem("wo_mm"), 1)

            wide_sum(pe, "n2", take(PART_BANK, "rms_part", WIDE["n2"]), take(4, "rms_std", NORMS["n2"] + 1))
            thin_product([(take(6, "thin_ev", 3), slice(0, T))], 16, (sem("h2_ready"), lambda k: k + 1))
            thin_sum(take(5, "aff_v", 2), thin, TT, 16, 3).then_inc(sem("logit_mm"), 1)
            for j in range(8):
                b = take(j % 4, "htok_ev", j + 1)
                for i in range(4):
                    k, t = 4 * (j % 2) + i, j // 2
                    ins = nc.tensor.transpose(b[:, 128 * i:128 * (i + 1)], H[:, k, 128 * t:128 * (t + 1)], ident)
                ins.then_inc(sem("htok_mm"), 1)
            pe.wait_ge(sem("aff_v"), 5)
            b = take(6, "top_v", 1)
            for t in range(TT):
                ins = nc.tensor.transpose(b[0:NE, 128 * t:128 * (t + 1)], aff[:, t, 0:NE], ident)
            ins.then_inc(sem("affT_mm"), 1)
            w = weights("xa_wk", KD)
            wait_weights(pe, "xa_wk")
            for j in range(4):
                b = take(j, "km_ev", j + 1)
                product(b[:, 0:TC], [(w[:, k, 128 * j:128 * (j + 1)], H[:, k, T:T + TC]) for k in range(KD)]).then_inc(sem("km_mm"), 1)
            w = weights("xa_wv", KD)
            wait_weights(pe, "xa_wv")
            for j in range(2):
                b = take(6 + j, "vm_ev", j + 1)
                product(b[:, :], [(H[:, k, T + 128 * j:T + 128 * (j + 1)], w[:, k, :]) for k in range(KD)]).then_inc(sem("vm_mm"), 1)
            pe.wait_ge(sem("top_v"), 2 * (CAP // 8) + 4)
            b = take(7, "slot_ready", 1)
            for t in range(TT):
                ins = nc.tensor.transpose(b[:, 16 * t:16 * (t + 1)], taken[:, 128 * t:128 * (t + 1)], ident[0:NE, 0:NE])
            ins.then_inc(sem("slotT_mm"), 1)
            for name, value in (("km_ev", 4), ("vm_ev", 2), ("slot_ready", 1), ("rms_std", NORMS["n2"] + 1), ("htok_ev", 8)):
                pe.wait_ge(*reached(name, value))

            def gather(sel):
                pe.wait_ge(sem("sel_v"), sel)
                for i in range(2):
                    for k in range(4 * i, 4 * i + 4):
                        c = 128 * (k - 4 * i)
                        ins = product(PS[i][:, c:c + 128], [(h_tok[:, t, 128 * k:128 * (k + 1)], selc[:, t, :, :]) for t in range(TT)])
                    ins.then_inc(sem("gather_mm"), 1)

            def scatter(done):
                for j in range(KD):
                    if j >= 2:
                        pe.wait_ge(sem("sc_v"), done(j))
                    nc.tensor.matmul(PS[2 + j % 2][:, :], ypair[:, 128 * j:128 * (j + 1)], GT, start=True, stop=True).then_inc(sem("sc_mm"), 1)

            n0 = len(W)

            def expert_weights(pair, i):
                s = (n0 + i) % NSLOT
                pe.wait_ge(arrived[s], pair * (16 * 12 // NSLOT) + 16 * ((n0 + i) // NSLOT + 1))
                return ring[:, s, :].rearrange("p (k n) -> p k n", k=KD)

            gather(1)
            with pe.Fori(0, NPAIR) as pair:
                pe.wait_ge(sem("xs_ev"), pair * 2 + 2)
                for e in range(2):
                    if e == 1:
                        pe.wait_ge(sem("gt_ev"), pair + 1)
                        pe.wait_ge(sem("y0_ev"), pair + 1)
                        pe.wait_ge(sem("y1_ev"), pair + 1)
                        scatter(lambda j: pair * 8 + (7 + j))
                        pe.wait_ge(sem("sc_v"), pair * 8 + 16)
                    for i in range(2):
                        b = PS[2 * e + i]
                        w2 = [expert_weights(pair, 4 * e + 2 * i + half) for half in range(2)]
                        for k in range(KD):
                            for half in range(2):
                                ins = nc.tensor.matmul(b[64 * half:64 * half + 64, :], xs[:, k, 64 * e:64 * e + 64], w2[half][:, k, :],
                                                       start=(k == 0), stop=(k == KD - 1), tile_position=(0, 64 * half))
                        ins.then_inc(sem("moe_mm"), 1)

                def turn(e):
                    pe.wait_ge(sem("hid_v"), pair * 2 + (3 + e))
                    for i in range(4):
                        ins = nc.tensor.transpose(PS[4 + e][:, 128 * i:128 * (i + 1)], hid[:, e, 128 * i:128 * (i + 1)], ident)
                    ins.then_inc(sem("tr_mm"), 1)

                turn(0)
                gather(pair + 2)
                turn(1)
                pe.wait_ge(sem("hidT_ev"), pair * 2 + 2)
                pe.wait_ge(sem("gc_v"), pair + 1)
                for t in range(TT):
                    ins = nc.tensor.transpose(PS[4][:, 128 * t:128 * (t + 1)], gc[:, t, :, :], ident)
                ins.then_inc(sem("gt_mm"), 1)
                for half in range(2):
                    w2 = [expert_weights(pair, 8 + 2 * half + e) for e in range(2)]
                    for k in range(KD):
                        for e in range(2):
                            ins = nc.tensor.matmul(PS[6 + half][64 * e:64 * e + 64, :], hidT[:, e, k % 4, 64 * (k // 4):64 * (k // 4) + 64],
                                                   w2[e][:, k, :], start=(k == 0), stop=(k == KD - 1), tile_position=(0, 64 * e))
                    ins.then_inc(sem("moe_mm"), 1)
            pe.wait_ge(sem("gt_ev"), NPAIR + 1)
            pe.wait_ge(sem("y0_ev"), NPAIR + 1)
            pe.wait_ge(sem("y1_ev"), NPAIR + 1)
            pe.wait_ge(sem("sc_v"), 8 * (NPAIR + 1))
            pe.wait_ge(sem("xs_ev"), 2 * (NPAIR + 1))
            scatter(lambda j: 8 * NPAIR + 7 + j)

            def project(name, dst_bank, evac, tiles=4, k=KD, act_in=None, j0=0, mm=None, norm=None):
                w = weights(name, k)
                wait_weights(pe, name)
                if norm:
                    banks = [take(dst_bank(j), *evac(j)) for j in range(tiles)]
                    for i in range(k):
                        pe.wait_ge(sem("rms_out"), norm_out(norm, i))
                        for j in range(tiles):
                            ins = nc.tensor.matmul(banks[j][:, :], w[:, i, 128 * j:128 * (j + 1)], act_in(i), start=(i == 0), stop=(i == k - 1))
                            if i == k - 1:
                                ins.then_inc(sem(mm), 1)
                    return
                for j in range(tiles):
                    b = take(dst_bank(j + j0), evac(j + j0)[0], evac(j + j0)[1])
                    product(b[:, :], [(w[:, i, 128 * j:128 * (j + 1)], act_in(i)) for i in range(k)]).then_inc(sem(mm), 1)

            hx = lambda i: H[:, i, 0:T]
            for i in (2, 3):
                freed[i] = (sem("sc_v"), 8 * (NPAIR + 2))
            for i in (0, 1, 4, 5, 6, 7):
                freed.pop(i, None)
            wide_sum(pe, "nf", take(PART_BANK, "rms_part", WIDE["nf"]), take(4, "rms_std", NORMS["nf"] + 1))
            wide_sum(pe, "n3", take(PART_BANK, "rms_part", WIDE["n3"]), take(4, "rms_std", NORMS["n3"] + 1))
            project("glu", lambda j: j, lambda j: ("glu_ev", j + 1), act_in=hx, mm="glu_mm", norm="n3")
            project("a", lambda j: 4 + j, lambda j: ("u_v", j + 2), act_in=hx, mm="a_mm")
            w = weights("v2", KD)
            wait_weights(pe, "v2")
            for t in range(TT):
                b = take(t, "v2_ev", t + 1)
                product(b[:, :], [(H[:, k, 128 * t:128 * (t + 1)], w[:, k, :]) for k in range(KD)]).then_inc(sem("v2_mm"), 1)
            thin_product([(take(6, "thin_ev", 4), slice(0, T))], 32)
            project("q2", lambda j: 4 + j, lambda j: ("q2_ev", j + 1), act_in=hx, mm="q2_mm")
            thin_sum(take(7, "f_v", 1), thin, TT, 8, 4, rowb[0:1, 16:24]).then_inc(sem("f_mm"), 1)
            project("k2", lambda j: j, lambda j: ("k2_ev", j + 1), act_in=hx, mm="k2_mm")
            pe.wait_ge(sem("dw_v"), KH * TAPS)
            product(take(4, "ln_v", KH)[:, :], [(ones, cT[:, k, :]) for k in range(KH)]).then_inc(sem("lnm_mm"), 1)
            pe.wait_ge(sem("f_v"), 4)
            b = take(6, "f_v", 5)
            for t in range(TT):
                ins = nc.tensor.transpose(b[0:FOX_H, 128 * t:128 * (t + 1)], f_tok[:, t, :], ident)
            ins.then_inc(sem("fT_mm"), 1)
            b = take(5, "ln_std", 1)
            for k in range(KH):
                pe.wait_ge(sem("ln_sq"), k + 1)
                nc.tensor.matmul(b[:, :], ones, sq[:, k % 2, :], start=(k == 0), stop=(k == KH - 1)).then_inc(sem("lnq_mm"), 1)

            def logits(hp):
                for e in range(2):
                    b = take(6 + e, "cb_ev", 2 * hp + e + 1)
                    h = 2 * hp + e
                    nc.tensor.matmul(b[:, :], ident[0:FOX_H, h:h + 1].broadcast_to([FOX_H, 128]), c_row[0:FOX_H, :], start=True, stop=True).then_inc(sem("cb_mm"), 1)
                for i in range(TT):
                    w = 128 * (i + 1)
                    bs = [take(2 * (i % 2) + e, "L_v", 3 * (8 * hp + 2 * i + e) + 1) for e in range(2)]
                    for e in range(2):
                        r = slice(64 * e, 64 * e + 64)
                        ins = nc.tensor.matmul(bs[e][:, 0:w], q2[r, hp, 128 * i:128 * (i + 1)], k2[r, hp, 0:w], start=True, stop=True)
                    ins.then_inc(sem("S2_mm"), 1)

            def gate_c(j):
                name = f"gc{j // 4}"
                if j % 4 == 0:
                    wait_weights(pe, name)
                w = weights(name, KD)
                b = take(4 + j % 2, "gc_ev", j + 1)
                product(b[:, :], [(w[:, k, 128 * (j % 4):128 * (j % 4) + 128], H[:, k, 0:T]) for k in range(KD)]).then_inc(sem("gcm"), 1)

            pe.wait_ge(*reached("q2_ev", 4))
            pe.wait_ge(*reached("k2_ev", 4))
            pe.wait_ge(sem("c_v"), 1)
            logits(0)
            for hp in range(FOX_H // 2):
                if hp + 1 < FOX_H // 2:
                    logits(hp + 1)
                gate_c(2 * hp)
                gate_c(2 * hp + 1)
                pe.wait_ge(sem("P_ready"), 8 * (hp + 1))
                out_b = take(5, "attn_ev", hp + 1)
                for e in range(2):
                    for t in range(TT):
                        b = take(6 + t % 2, "PT_ev", 8 * hp + 4 * e + t + 1)
                        for i in range(t, TT):
                            c = 1280 * e + 64 * i * (i + 1) + 128 * t
                            ins = nc.tensor.transpose(b[:, 128 * i:128 * (i + 1)], Pbuf[hp % 2][:, c:c + 128], ident)
                        ins.then_inc(sem("PT_mm"), 1)
                    for t in range(TT):
                        pe.wait_ge(sem("PT_ev"), 8 * hp + 4 * e + t + 1)
                        c = (0, 512, 896, 1152)[t]
                        ins = nc.tensor.matmul(out_b[64 * e:64 * e + 64, 128 * t:T], V2[:, t, 2 * hp + e, :], PT2[:, c:c + 512 - 128 * t],
                                               start=(t == 0), stop=(t == TT - 1), tile_position=(0, 64 * e))
                    ins.then_inc(sem("pv2_mm"), 1)
            pe.wait_ge(*reached("c_ready", KH))
            w = weights("pw", KH)
            wait_weights(pe, "pw")
            for j in range(8):
                b = take(j % 4, "pw_v", j + 1)
                product(b[:, :], [(w[:, k, 128 * j:128 * (j + 1)], cT[:, k, :]) for k in range(KH)]).then_inc(sem("pw_mm"), 1)
            for s in range(2):
                project(f"ga{s}", lambda j: 4 + j % 4, lambda j: ("ga_ev", j + 1), act_in=hx, j0=4 * s, mm="gam")
            pe.wait_ge(sem("attn_ev"), 4)
            project("ab", lambda j: j % 4, lambda j: ("ab_v", 2 * j + 1), tiles=8, k=KH, act_in=lambda i: q2[:, i, :], mm="ab_mm")
            pe.wait_ge(sem("ab_v"), 16)
            for s in range(2):
                project(f"w2o{s}", lambda j: j % 4, lambda j: ("x3", j + 1), act_in=lambda i: merged[:, i, :], j0=4 * s, mm="w2o_mm")

            def xpv(h):
                pe.wait_ge(sem("xT2_ev"), 2 * (h + 1))
                b = take(4 + h, "ox_ev", h + 1)
                product(b[:, :], [(Vm[:, m, 128 * h:128 * (h + 1)], PTx[:, h, m, :]) for m in range(2)]).then_inc(sem("xo_pv"), 1)

            wide_sum(pe, "n4", take(PART_BANK, "rms_part", WIDE["n4"]), take(4, "rms_std", NORMS["n4"] + 1))
            project("xa_wq", lambda j: j, lambda j: ("xq_ev", j + 1), act_in=hx, mm="xq_mm", norm="n4")
            pe.wait_ge(*reached("xq_ev", 4))
            for h in range(4):
                for i in range(2):
                    b = take((2 * h + i) % 8, "xexp_s", 4 * h + 2 * i + 2)
                    for j in range(2):
                        q = 128 * (2 * i + j)
                        ins = nc.tensor.matmul(b[:, 256 * j:256 * (j + 1)], q2[:, h, q:q + 128], kmT[:, h, :], start=True, stop=True)
                    ins.then_inc(sem("xS_mm"), 1)
            for h in range(4):
                pe.wait_ge(sem("xP_ready"), 4 * (h + 1))
                for m in range(2):
                    b = take(2 * (h % 2) + m, "xT2_ev", 2 * h + m + 1)
                    for i in range(TT):
                        ins = nc.tensor.transpose(b[:, 128 * i:128 * (i + 1)], Px[:, h, i, 128 * m:128 * (m + 1)], ident)
                    ins.then_inc(sem("xT2_mm"), 1)
                if h:
                    xpv(h - 1)
            xpv(3)
            pe.wait_ge(sem("ox_ev"), 4)
            project("xa_wo", lambda j: j % 4, lambda j: ("x4", j + 1), tiles=8, k=KH, act_in=lambda i: k2[:, i, :], mm="xo_mm")
            wide_sum(pe, "n5", take(PART_BANK, "rms_part", WIDE["n5"]), take(4, "rms_std", NORMS["n5"] + 1))
            thin_product([(take(6, "thin_ev", 5), slice(0, T))], 40, (sem("rms_out"), lambda k: norm_out("n5", k)))
            thin_sum(take(5, "g_v", 1), thin, TT, 20, 5, rowb[0:1, 24:44]).then_inc(sem("rl_mm"), 1)
            for j in range(8):
                b = take(j % 4, "h2_ev", j + 1)
                for i in range(4):
                    k, t = 4 * (j % 2) + i, j // 2
                    ins = nc.tensor.transpose(b[:, 128 * i:128 * (i + 1)], H[:, k, 128 * t:128 * (t + 1)], ident)
                ins.then_inc(sem("h2_mm"), 1)
            pe.wait_ge(sem("comb_ready"), 1)
            b = take(6, "chosen", 1)
            for t in range(TT):
                ins = nc.tensor.transpose(b[0:16, 128 * t:128 * (t + 1)], rt["comb"][:, t, :, :], ident)
            ins.then_inc(sem("combT_mm"), 1)
            pe.wait_ge(sem("block_counts"), 1)
            nc.tensor.matmul(take(7, "ends_v", 1)[0:E2, 0:1], const[0:E2, CONST["s_le_j"]:CONST["s_le_j"] + E2], nblk, start=True, stop=True).then_inc(sem("ends_mm"), 1)
            pe.wait_ge(sem("ended"), 1)
            nc.tensor.matmul(take(6, "block_expert", 1)[0:1, 0:32], ones[0:E2, 0:1], ended, start=True, stop=True).then_inc(sem("which_mm"), 1)
            pe.wait_ge(sem("places"), 1)
            b = take(5, "pos_v", 1)
            for t in range(TT):
                ins = nc.tensor.transpose(b[:, E2 * t:E2 * (t + 1)], place[:, 128 * t:128 * (t + 1)], ident[0:E2, 0:E2])
            ins.then_inc(sem("posT_mm"), 1)
            for name, value in (("h2_ev", 8), ("rms_std", NORMS["n5"] + 1), ("pos_v", 1), ("block_expert", 1), ("ends_v", 1)):
                pe.wait_ge(*reached(name, value))

            def gather_blocks():
                for i in range(2):
                    product(PS[i][:, :], [(selb[:, t, :], h[:, t, 512 * i:512 * (i + 1)])
                                          for t in range(TT) for h in (h2_high, h2_low)]).then_inc(sem("b_gather"), 1)

            def turn_blocks(rows):
                for i in range(2):
                    pe.wait_ge(sem("b_x_rows"), rows(i))
                    for k in range(4):
                        ins = nc.tensor.transpose(PS[i][:, 128 * k:128 * (k + 1)], x_rows[:, 512 * i + 128 * k:512 * i + 128 * (k + 1)], ident)
                    ins.then_inc(sem("b_turn_x"), 1)

            def scatter_tile(j, pair, GT_):
                if j == 0:
                    pe.wait_ge(sem("b_GT"), pair + 1)
                if j % 4 == 0:
                    pe.wait_ge(sem("b_y_low"), pair * 2 + (1 + j // 4))
                pe.wait_ge(sem("x5"), pair * 8 + (7 + j))
                parts = (y_high[:, 128 * j:128 * (j + 1)], y_low[j // 4][:, 128 * (j % 4):128 * (j % 4 + 1)])
                product(PS[3 + j % 2][:, :], [(y, GT_) for y in parts]).then_inc(sem("b_scatter"), 1)

            pe.wait_ge(sem("h2_low"), 8)
            pe.wait_ge(sem("b_sel"), 1)
            gather_blocks()
            turn_blocks(lambda i: i + 1)
            between = {1: [0], 2: [1], 3: [2], 4: [3], 5: [4], 6: [5], 7: [6, 7]}
            with pe.Fori(0, NPAIR2 // 2) as step2:
                for odd in range(2):
                    pair = step2 * 2 + odd
                    pe.wait_ge(sem("b_gates"), pair + 1)
                    pe.wait_ge(sem("b_hidT"), step2 * 2 + (odd + 1))
                    for t in range(TT):
                        ins = nc.tensor.transpose(PS[5][:, 128 * t:128 * (t + 1)], gb[:, t, :], ident)
                    ins.then_inc(sem("b_turn_g"), 1)
                    pe.wait_ge(sem("b_x"), step2 * 4 + (2 * odd + 2))
                    pe.wait_ge(sem("b_hid"), step2 * 2 + (odd + 1))
                    for i in range(2):
                        pe.wait_ge(sem(f"gate_up{2 * odd + i}_in"), step2 * 32 + 32)
                    for k in range(KD):
                        for i in range(2):
                            ins = nc.tensor.matmul(PS[2][BLK * i:BLK * (i + 1), :], xb[:, k, BLK * i:BLK * (i + 1)], ring[:, 2 * odd + i, 512 * k:512 * (k + 1)],
                                                   start=(k == 0), stop=(k == KD - 1), tile_position=(0, BLK * i))
                        if k == KD - 1:
                            ins.then_inc(sem("b_gate_up"), 1)
                        for j in between.get(k, []):
                            scatter_tile(j, pair, GTb[1 - odd])
                    pe.wait_ge(sem("b_sel"), pair + 2)
                    pe.wait_ge(sem("b_x"), step2 * 4 + (2 * odd + 2))
                    gather_blocks()
                    pe.wait_ge(sem("b_hid"), pair + 2)
                    pe.wait_ge(sem("b_GT"), pair + 2)
                    for i in range(2):
                        ins = nc.tensor.transpose(PS[5][:, 128 * i:128 * (i + 1)], hb[:, 128 * i:128 * (i + 1)], ident)
                    ins.then_inc(sem("b_turn"), 1)
                    turn_blocks(lambda i: step2 * 4 + (3 + 2 * odd + i))
                    pe.wait_ge(sem("b_hidT"), pair + 2)
                    pe.wait_ge(sem("b_y_low"), step2 * 4 + (2 * odd + 2))
                    pe.wait_ge(sem("down_in"), pair * 32 + 32)
                    for half in range(2):
                        for f in range(2):
                            for i in range(2):
                                c = 2048 * i + 1024 * f + 512 * half
                                ins = nc.tensor.matmul(PS[6 + half][BLK * i:BLK * (i + 1), :], hbT[:, f, BLK * i:BLK * (i + 1)], down2[:, c:c + 512],
                                                       start=(f == 0), stop=(f == 1), tile_position=(0, BLK * i))
                        ins.then_inc(sem("b_down"), 1)
            for j in range(KD):
                scatter_tile(j, NPAIR2, GTb[(NPAIR2 - 1) % 2])
            freed.clear()
            for i, (name, value) in enumerate((("b_x", 2 * NPAIR2 + 2), ("b_x", 2 * NPAIR2 + 2), ("b_hid", NPAIR2 + 1), ("x5", 8 * (NPAIR2 + 2)), ("x5", 8 * (NPAIR2 + 2)))):
                freed[i] = (sem(name), value)
            freed[5] = (sem("b_hidT"), NPAIR2 + 1)
            wide_sum(pe, "n6", take(PART_BANK, "rms_part", WIDE["n6"]), take(4, "rms_std", NORMS["n6"] + 1))
            for j in range(8):
                b = take(j % 4, "ot_ev", j + 1)
                t = j // 2
                for i in range(4):
                    k = 4 * (j % 2) + i
                    pe.wait_ge(sem("rms_out"), norm_out("n6", k))
                    ins = nc.tensor.transpose(b[:, 128 * i:128 * (i + 1)], H[:, k, 128 * t:128 * (t + 1)], ident)
                ins.then_inc(sem("ot_mm"), 1)


def kernel(**inputs):
    import concourse.bacc as bacc
    from concourse.bass_utils import run_bass_kernel_spmd

    nc = bacc.Bacc("TRN2", target_bir_lowering=False, num_devices=1)
    sent = {name: np.ascontiguousarray(a) for name, a in inputs.items()}
    sent["consts"], sent["dft"] = constant_tables()
    arrays, A = {}, {}
    for name, a in sent.items():
        arrays[f"in_{name}"] = a
        A[name] = nc.dram_tensor(f"in_{name}", a.shape, mybir.dt.from_np(a.dtype), kind="ExternalInput").ap()
    out = nc.dram_tensor("out", (1, T, D), F32, kind="ExternalOutput").ap()
    build(nc, A, out)
    result = run_bass_kernel_spmd(nc, [arrays], core_ids=[0])
    return result.results[0]["out"]
```
